# Optimizing a Trainium2 kernel written in Bass

```python
import jax
import jax.numpy as jnp
from jax import lax
import numpy as np

D_MODEL = 1024
BATCH = 1
SEQ = 512
DEPTH = 1
DEC_BATCH = 8
DEC_SEQ = 16
PAST_LEN = 512

CHUNK = 64
Q_BLOCK = 128
MIX_WIDTH = D_MODEL
SB_HEADS = 8
SB_HEAD_DIM = MIX_WIDTH // 2 // SB_HEADS
SB_WIDTH = SB_HEADS * SB_HEAD_DIM
MLA_HEADS = 8
MLA_NOPE_DIM = 64
MLA_ROPE_DIM = 32
MLA_V_DIM = (MIX_WIDTH - SB_WIDTH) // MLA_HEADS
MLA_WIDTH = MLA_HEADS * MLA_V_DIM
MLA_Q_RANK = 384
MLA_KV_RANK = 256
MLA_QK_DIM = MLA_NOPE_DIM + MLA_ROPE_DIM
MLA_SCALE = MLA_QK_DIM ** -0.5
ROPE_BASE = 10000.0
IN_SPLITS = (SB_WIDTH, 2 * SB_WIDTH, 3 * SB_WIDTH,
             3 * SB_WIDTH + MLA_Q_RANK, 3 * SB_WIDTH + MLA_Q_RANK + MLA_KV_RANK)
IN_WIDTH = 3 * SB_WIDTH + MLA_Q_RANK + MLA_KV_RANK + MLA_ROPE_DIM
PEER_HEADS = 8
PEER_N_KEYS = 128
PEER_N_EXPERTS = PEER_N_KEYS * PEER_N_KEYS
PEER_KEY_DIM = 256
PEER_HALF = PEER_KEY_DIM // 2
PEER_TOPK = 16
PEER_TOKEN_BLOCK = 256
ADA_SCALE = 0.5
NORM_EPS = 1e-6

kernel_name = 'sb_mla_peer_streaming_encoder_step'

def rmsnorm(x, g):
    xf = x.astype(jnp.float32)
    y = xf * lax.rsqrt(jnp.mean(xf * xf, axis=-1, keepdims=True) + NORM_EPS)
    return (y * g.astype(jnp.float32)).astype(x.dtype)

def rope(x, pos):
    half = x.shape[-1] // 2
    inv = ROPE_BASE ** (-jnp.arange(half, dtype=jnp.float32) / half)
    ang = pos.astype(jnp.float32)[:, None] * inv[None, :]
    shape = (1, pos.shape[0]) + (1,) * (x.ndim - 3) + (half,)
    cos = jnp.cos(ang).reshape(shape)
    sin = jnp.sin(ang).reshape(shape)
    x1 = x[..., :half].astype(jnp.float32)
    x2 = x[..., half:].astype(jnp.float32)
    return jnp.concatenate([x1 * cos - x2 * sin, x2 * cos + x1 * sin], axis=-1).astype(x.dtype)

def stick_breaking_block(q, k, v, q_pos, k_pos):
    z = jnp.einsum('bqhd,bkhd->bhqk', q, k).astype(jnp.float32) * (SB_HEAD_DIM ** -0.5)
    valid = k_pos[None, :] < q_pos[:, None]
    log_keep = jnp.where(valid, jax.nn.log_sigmoid(-z), 0.0)
    tail = lax.cumsum(log_keep, axis=3, reverse=True) - log_keep
    a = jnp.where(valid, jnp.exp(jax.nn.log_sigmoid(z) + tail), 0.0)
    return jnp.einsum('bhqk,bkhd->bqhd', a.astype(v.dtype), v)

def chunk_causal_softmax(s, q_pos, k_pos):
    visible = (k_pos[None, :] // CHUNK) <= (q_pos[:, None] // CHUNK)
    return jax.nn.softmax(jnp.where(visible, s.astype(jnp.float32) * MLA_SCALE, -jnp.inf), axis=-1)

def peer(h, w_peer_q, sub_keys_1, sub_keys_2, u_experts, v_experts):
    B, T, D = h.shape
    x = h.reshape(B * T, D)
    n = x.shape[0]
    q = (x @ w_peer_q).reshape(n, PEER_HEADS, 2, PEER_HALF)
    s1 = jnp.einsum('nhk,ek->nhe', q[:, :, 0], sub_keys_1).astype(jnp.float32)
    s2 = jnp.einsum('nhk,ek->nhe', q[:, :, 1], sub_keys_2).astype(jnp.float32)
    v1, i1 = lax.top_k(s1, PEER_TOPK)
    v2, i2 = lax.top_k(s2, PEER_TOPK)
    cand_s = (v1[..., :, None] + v2[..., None, :]).reshape(n, PEER_HEADS, PEER_TOPK * PEER_TOPK)
    cand_i = (i1[..., :, None] * PEER_N_KEYS + i2[..., None, :]).reshape(n, PEER_HEADS, PEER_TOPK * PEER_TOPK)
    top_s, top_j = lax.top_k(cand_s, PEER_TOPK)
    idx = jnp.take_along_axis(cand_i, top_j, axis=-1)
    gate = jax.nn.softmax(top_s, axis=-1)
    n_pad = (-n) % PEER_TOKEN_BLOCK
    nb = (n + n_pad) // PEER_TOKEN_BLOCK
    xb = jnp.pad(x, ((0, n_pad), (0, 0))).reshape(nb, PEER_TOKEN_BLOCK, D)
    ib = jnp.pad(idx, ((0, n_pad), (0, 0), (0, 0))).reshape(nb, PEER_TOKEN_BLOCK, PEER_HEADS, PEER_TOPK)
    gb = jnp.pad(gate, ((0, n_pad), (0, 0), (0, 0))).reshape(nb, PEER_TOKEN_BLOCK, PEER_HEADS, PEER_TOPK)

    def token_block(args):
        xt, it, gt = args
        u = u_experts[it]
        act = jax.nn.gelu(jnp.einsum('td,thkd->thk', xt, u).astype(jnp.float32), approximate=False) * gt
        return jnp.einsum('thk,thkd->td', act.astype(xt.dtype), v_experts[it])

    out = lax.map(token_block, (xb, ib, gb)).reshape(nb * PEER_TOKEN_BLOCK, D)[:n]
    return out.reshape(B, T, D)

def hybrid_layer(x, c, pos, past, w_ada, b_ada, g_mix_pre, g_mix_post, g_ffn_pre, g_ffn_post,
                 w_in, g_q_lat, g_kv_lat, w_uq, w_uk, w_uv, g_sb_out, g_mla_out, w_out,
                 w_peer_q, sub_keys_1, sub_keys_2, u_experts, v_experts):
    B, T, _ = x.shape
    ada = jax.nn.silu(c) @ w_ada + b_ada
    sh1, sc1, gt1, sh2, sc2, gt2 = jnp.split(ada[:, None, :], 6, axis=-1)

    h = rmsnorm(x, g_mix_pre) * (1 + sc1) + sh1
    sb_q, sb_k, sb_v, q_lat, ckv, krope = jnp.split(h @ w_in, IN_SPLITS, axis=-1)
    sb_q = sb_q.reshape(B, T, SB_HEADS, SB_HEAD_DIM)
    sb_k = sb_k.reshape(B, T, SB_HEADS, SB_HEAD_DIM)
    sb_v = sb_v.reshape(B, T, SB_HEADS, SB_HEAD_DIM)
    q = (rmsnorm(q_lat, g_q_lat) @ w_uq).reshape(B, T, MLA_HEADS, MLA_QK_DIM)
    q_nope = q[..., :MLA_NOPE_DIM]
    q_rope = rope(q[..., MLA_NOPE_DIM:], pos)
    ckv = rmsnorm(ckv, g_kv_lat)
    krope = rope(krope, pos)

    if past is None:
        k_nope = jnp.einsum('btc,chn->bthn', ckv, w_uk)
        v_mla = jnp.einsum('btc,chv->bthv', ckv, w_uv)
        sb_parts, mla_parts = [], []
        for i in range(T // Q_BLOCK):
            lo, hi = i * Q_BLOCK, (i + 1) * Q_BLOCK
            qp, kp = pos[lo:hi], pos[:hi]
            sb_parts.append(stick_breaking_block(sb_q[:, lo:hi], sb_k[:, :hi], sb_v[:, :hi], qp, kp))
            s = (jnp.einsum('bqhn,bkhn->bhqk', q_nope[:, lo:hi], k_nope[:, :hi])
                 + jnp.einsum('bqhr,bkr->bhqk', q_rope[:, lo:hi], krope[:, :hi]))
            p = chunk_causal_softmax(s, qp, kp)
            mla_parts.append(jnp.einsum('bhqk,bkhv->bqhv', p.astype(v_mla.dtype), v_mla[:, :hi]))
        sb_o = jnp.concatenate(sb_parts, axis=1)
        mla_o = jnp.concatenate(mla_parts, axis=1)
    else:
        c_sb_k, c_sb_v, c_ckv, c_krope = past
        kp = jnp.arange(c_sb_k.shape[1] + T)
        all_sb_k = jnp.concatenate([c_sb_k, sb_k], axis=1)
        all_sb_v = jnp.concatenate([c_sb_v, sb_v], axis=1)
        sb_o = stick_breaking_block(sb_q, all_sb_k, all_sb_v, pos, kp)
        all_ckv = jnp.concatenate([c_ckv, ckv], axis=1)
        all_kr = jnp.concatenate([c_krope, krope], axis=1)
        q_abs = jnp.einsum('bthn,chn->bthc', q_nope, w_uk)
        s = (jnp.einsum('bqhc,bkc->bhqk', q_abs, all_ckv)
             + jnp.einsum('bqhr,bkr->bhqk', q_rope, all_kr))
        p = chunk_causal_softmax(s, pos, kp)
        o_lat = jnp.einsum('bhqk,bkc->bqhc', p.astype(all_ckv.dtype), all_ckv)
        mla_o = jnp.einsum('bqhc,chv->bqhv', o_lat, w_uv)

    merged = jnp.concatenate([rmsnorm(sb_o.reshape(B, T, SB_WIDTH), g_sb_out),
                              rmsnorm(mla_o.reshape(B, T, MLA_WIDTH), g_mla_out)], axis=-1)
    x = x + gt1 * rmsnorm(merged @ w_out, g_mix_post)

    h2 = rmsnorm(x, g_ffn_pre) * (1 + sc2) + sh2
    f = peer(h2, w_peer_q, sub_keys_1, sub_keys_2, u_experts, v_experts)
    x = x + gt2 * rmsnorm(f, g_ffn_post)
    return x, (sb_k, sb_v, ckv, krope)

def setup_inputs(seed: int = 0) -> dict:
    key = jax.random.key(seed)
    ks = iter(jax.random.split(key, 40))
    f32 = jnp.float32

    def nrm(shape, scale):
        return jax.random.normal(next(ks), shape, f32) * scale

    def gain(shape):
        return 1.0 + 0.02 * jax.random.normal(next(ks), shape, f32)

    L, D = DEPTH, D_MODEL
    return {
        'x_prompt': nrm((BATCH, SEQ, D), 1.0),
        'x_sample': nrm((DEC_BATCH, DEC_SEQ, D), 1.0),
        'c_prompt': nrm((BATCH, D), 1.0),
        'c_sample': nrm((DEC_BATCH, D), 1.0),
        'cache_sb_k': nrm((L, DEC_BATCH, PAST_LEN, SB_HEADS, SB_HEAD_DIM), 1.0),
        'cache_sb_v': nrm((L, DEC_BATCH, PAST_LEN, SB_HEADS, SB_HEAD_DIM), 1.0),
        'cache_mla_ckv': nrm((L, DEC_BATCH, PAST_LEN, MLA_KV_RANK), 1.0),
        'cache_mla_krope': nrm((L, DEC_BATCH, PAST_LEN, MLA_ROPE_DIM), 1.0),
        'w_ada': nrm((L, D, 6 * D), ADA_SCALE * D ** -0.5),
        'b_ada': nrm((L, 6 * D), 0.01),
        'g_mix_pre': gain((L, D)),
        'g_mix_post': gain((L, D)),
        'g_ffn_pre': gain((L, D)),
        'g_ffn_post': gain((L, D)),
        'w_in': nrm((L, D, IN_WIDTH), D ** -0.5),
        'g_q_lat': gain((L, MLA_Q_RANK)),
        'g_kv_lat': gain((L, MLA_KV_RANK)),
        'w_uq': nrm((L, MLA_Q_RANK, MLA_HEADS * MLA_QK_DIM), MLA_Q_RANK ** -0.5),
        'w_uk': nrm((L, MLA_KV_RANK, MLA_HEADS, MLA_NOPE_DIM), MLA_KV_RANK ** -0.5),
        'w_uv': nrm((L, MLA_KV_RANK, MLA_HEADS, MLA_V_DIM), MLA_KV_RANK ** -0.5),
        'g_sb_out': gain((L, SB_WIDTH)),
        'g_mla_out': gain((L, MLA_WIDTH)),
        'w_out': nrm((L, MIX_WIDTH, D), MIX_WIDTH ** -0.5),
        'w_peer_q': nrm((L, D, PEER_HEADS * PEER_KEY_DIM), D ** -0.5),
        'sub_keys_1': nrm((L, PEER_N_KEYS, PEER_HALF), PEER_HALF ** -0.5),
        'sub_keys_2': nrm((L, PEER_N_KEYS, PEER_HALF), PEER_HALF ** -0.5),
        'u_experts': nrm((L, PEER_N_EXPERTS, D), D ** -0.5),
        'v_experts': nrm((L, PEER_N_EXPERTS, D), 1.0),
    }

def reference(x_prompt, x_sample, c_prompt, c_sample, cache_sb_k, cache_sb_v, cache_mla_ckv,
              cache_mla_krope, w_ada, b_ada, g_mix_pre, g_mix_post, g_ffn_pre, g_ffn_post,
              w_in, g_q_lat, g_kv_lat, w_uq, w_uk, w_uv, g_sb_out, g_mla_out, w_out,
              w_peer_q, sub_keys_1, sub_keys_2, u_experts, v_experts):
    pos_p = jnp.arange(x_prompt.shape[1])
    pos_s = cache_sb_k.shape[2] + jnp.arange(x_sample.shape[1])
    y_p, y_s = x_prompt, x_sample
    sbk_p, sbv_p, ckv_p, kr_p = [], [], [], []
    sbk_s, sbv_s, ckv_s, kr_s = [], [], [], []
    for l in range(DEPTH):
        lw = (w_ada[l], b_ada[l], g_mix_pre[l], g_mix_post[l], g_ffn_pre[l], g_ffn_post[l],
              w_in[l], g_q_lat[l], g_kv_lat[l], w_uq[l], w_uk[l], w_uv[l], g_sb_out[l],
              g_mla_out[l], w_out[l], w_peer_q[l], sub_keys_1[l], sub_keys_2[l],
              u_experts[l], v_experts[l])
        y_p, (a, b, cc, d) = hybrid_layer(y_p, c_prompt, pos_p, None, *lw)
        sbk_p.append(a); sbv_p.append(b); ckv_p.append(cc); kr_p.append(d)
        past = (cache_sb_k[l], cache_sb_v[l], cache_mla_ckv[l], cache_mla_krope[l])
        y_s, (a, b, cc, d) = hybrid_layer(y_s, c_sample, pos_s, past, *lw)
        sbk_s.append(a); sbv_s.append(b); ckv_s.append(cc); kr_s.append(d)
    return (y_p, y_s,
            jnp.stack(sbk_p), jnp.stack(sbv_p), jnp.stack(ckv_p), jnp.stack(kr_p),
            jnp.stack(sbk_s), jnp.stack(sbv_s), jnp.stack(ckv_s), jnp.stack(kr_s))


_drawn_inputs = setup_inputs


def setup_inputs(seed=0):
    import zlib

    import numpy as np

    out = dict(_drawn_inputs(seed))
    spreads = {}
    factors = {'g_ffn_post': 8.0, 'g_q_lat': 2.751}
    for name, (base, spread) in spreads.items():
        noise = np.random.default_rng([zlib.crc32(name.encode()), seed]).standard_normal(out[name].shape)
        drawn = base * np.exp(spread * noise) if base else spread * noise
        out[name] = jnp.asarray(drawn.astype(out[name].dtype))
    for name, factor in factors.items():
        out[name] = (out[name] * factor).astype(out[name].dtype)
    return out
```

```python
import math
from contextlib import ExitStack

import numpy as np

import concourse.bass as bass
from concourse import mybir

F32 = mybir.dt.float32
U32 = mybir.dt.uint32
F32R = mybir.dt.float32r
ALU = mybir.AluOpType
ACT = mybir.ActivationFunctionType
AX_X = mybir.AxisListType.X

P = 128
D = 1024
KD = D // P
SEQ = 512
NSEQ = 8
STEP = 16
PAST = 512
KEYS = PAST + STEP
N = SEQ + NSEQ * STEP
NT = N // P
PT = SEQ // P
HALF = N // 2
CHUNK = 64
H = 8
HD = 64
SBW = H * HD
QR = 384
KVR = 256
ROPE = 32
RH = ROPE // 2
QK = HD + ROPE
LAT = QR + KVR + ROPE
INW = 3 * SBW + LAT
NKEYS = 128
TOPK = 16
NEXP = NKEYS * NKEYS
NQ = 2 * H
EPS = 1e-6
NEG = -1e30
MLA_SCALE = float(QK) ** -0.5
SB_SCALE = float(HD) ** -0.5
NC_ = 1 + NSEQ
NM = 6 * KD
SH1, SC1, GT1, SH2, SC2, GT2 = (KD * i for i in range(6))

VECTORS = [("b_ada", NM), ("g_mix_pre", KD), ("g_mix_post", KD), ("g_ffn_pre", KD), ("g_ffn_post", KD),
           ("g_q_lat", QR // P), ("g_kv_lat", KVR // P), ("g_sb_out", SBW // P), ("g_mla_out", SBW // P)]
VROW, _at = {}, 0
for _name, _n in VECTORS:
    VROW[_name] = _at
    _at += _n
NV = _at

CONSTS = [("ident", P), ("iota", P), ("keep", P), ("drop", P), ("ones", 8), ("cos", NT * RH), ("sin", NT * RH),
          ("new_keep", STEP), ("new_drop", STEP), ("slot", TOPK), ("chunk_row", P), ("chunk_col", P)]
CCOL, _at = {}, 0
for _name, _n in CONSTS:
    CCOL[_name] = (_at, _n)
    _at += _n
NCONST = _at


def constant_table():
    t = np.zeros((P, NCONST), np.float32)

    def put(name, a):
        at, n = CCOL[name]
        t[:, at:at + n] = np.asarray(a, np.float32).reshape(-1, n)

    row, col = np.arange(P)[:, None], np.arange(P)[None, :]
    put("ident", row == col)
    put("iota", np.broadcast_to(col, (P, P)))
    put("keep", col < row)
    put("drop", np.where(col < row, 0.0, NEG))
    put("ones", np.ones((P, 8)))
    pos = np.concatenate([np.arange(SEQ), PAST + np.tile(np.arange(STEP), NSEQ)]).astype(np.float32)
    inv = (np.float32(10000.0) ** (-np.arange(RH, dtype=np.float32) / np.float32(RH))).astype(np.float32)
    angle = (pos[:, None] * inv[None, :]).astype(np.float32).astype(np.float64).reshape(NT, P, RH).transpose(1, 0, 2)
    put("cos", np.cos(angle).reshape(P, NT * RH))
    put("sin", np.sin(angle).reshape(P, NT * RH))
    query, key = (np.arange(P) % STEP)[:, None], np.arange(STEP)[None, :]
    put("new_keep", key < query)
    put("new_drop", np.where(key < query, 0.0, NEG))
    put("slot", np.broadcast_to(np.arange(TOPK), (P, TOPK)))
    put("chunk_row", (row == 0) & (col < CHUNK))
    put("chunk_col", np.where((row == 0) & (col >= CHUNK), NEG, 0.0))
    return t


class Step:

    def __init__(self, eng, sem, at=0):
        self.eng, self.sem, self.n = eng, sem, at

    def __call__(self, ins):
        ins.then_inc(self.sem, 1)
        self.n += 1
        return self.n

    def wait(self, n=None):
        self.eng.wait_ge(self.sem, self.n if n is None else n)


def build(nc, A, upto=99, dbg=None):
    ctx = ExitStack()
    KB = 1024
    BASE = 16512

    def sb(name, kb, shape, dt=F32):
        return nc.alloc_sbuf_tensor_at(name, shape, dt, offset=BASE + int(kb * KB))

    def run(phase):
        mine = {}

        def sem(name):
            if name not in mine:
                mine[name] = nc.alloc_semaphore(name)
            return mine[name]

        phase(nc, A, env | {"sem": sem, "env": env})
        nc.clear_and_free_semaphores(list(mine.values()))
        nc.all_engine_barrier()

    with ctx:
        PS = ctx.enter_context(nc.psum_tensor("PS", [P, 8, 512], F32))
        const = sb("const", 0, [P, NCONST])
        C = {k: const[:, a:a + n] for k, (a, n) in CCOL.items()}
        ident = C["ident"]
        KC = NCONST * 4 / KB
        assert KC <= 6
        vecT = sb("vecT", 6, [P, NV])
        adaT = sb("adaT", 6.375, [P, NM, NC_])
        coef = sb("coef", 8.0625, [P, 2, KD, NC_])
        stat = sb("stat", 8.65625, [P, 8, 16])
        cT = sb("cT", 9.1875, [P, NC_, KD])
        x = sb("x", 26, [P, NT, D])
        hT = sb("hT", 46, [P, KD, N])
        env = dict(locals())
        phases = (phase_condition_and_project, phase_latents, phase_prompt_attention, phase_sample_attention,
                  phase_merge, phase_keys, phase_gates, phase_experts)
        for phase in phases[:upto]:
            run(phase)
        if dbg:
            dbg(nc, env, nc.alloc_semaphore, sb)


def phase_condition_and_project(nc, A, env):
    sb, sem, PS, C, ident = (env[k] for k in ("sb", "sem", "PS", "C", "ident"))
    const, vecT, adaT, coef, stat, cT, x, hT = (env[k] for k in ("const", "vecT", "adaT", "coef", "stat", "cT", "x", "hT"))
    win = sb("win", 66, [P, KD, INW])
    WA = 2
    NWA = 2 * KD // WA
    wada = [sb(f"wada{i}", 135 + 8 * i, [P, KD, WA * P]) for i in range(NWA)]
    xn = [sb(f"xn{i}", 10 + 4 * i, [P, D]) for i in range(2)]
    ktok = [sb(f"ktok{i}", 18 + 2 * i, [P, SBW]) for i in range(2)]
    crow = sb("crow", 22, [NC_ * KD, P])
    cexp = sb("cexp", 22.5, [P, NC_ * KD])
    vrow = sb("vrow", 23, [NV, P])
    junk = sb("junk", 203, [P, D])
    qT = sb("qT", 159, [P, SBW // P, N])
    kT = sb("kT", 169, [P, SBW // P, N])
    vt = sb("vt", 179, [P, NT, SBW])
    lat = sb("lat", 189, [P, NT, LAT])
    env["env"].update(qT=qT, kT=kT, vt=vt, lat=lat, junk=junk)

    const_in, vec_in, c_in = sem("const_in"), sem("vec_in"), sem("c_in")
    x_in = [sem(f"x_in{t}") for t in range(NT)]
    wada_in = [sem(f"wada_in{i}") for i in range(NWA)]
    win_in = [sem(f"win_in{k}") for k in range(KD)]
    small_T, small_ready = sem("small_T"), sem("small_ready")
    c_exp = sem("c_exp")
    ada_psum, ada_ready = sem("ada_psum"), sem("ada_ready")
    x_sq, x_rstd, x_sqrt, xn_ready = sem("x_sq"), sem("x_rstd"), sem("x_sqrt"), sem("xn_ready")
    xT_psum, hT_ready, v_step = sem("xT_psum"), sem("hT_ready"), sem("v_step")
    q_psum, q_ready = sem("q_psum"), sem("q_ready")
    tok_psum = [sem(f"tok_psum{g}") for g in range(4)]
    tok_ready = [sem(f"tok_ready{g}") for g in range(4)]
    kT_psum, kT_ready, sbv_out = sem("kT_psum"), sem("kT_ready"), sem("sbv_out")
    sbk_out = [sem("sbk_out0"), sem("sbk_out1")]
    x_dram = [A["x_prompt"][0, t * P:(t + 1) * P, :] for t in range(PT)] + [A["x_sample"].rearrange("b q d -> (b q) d")]
    sbk_dram = ([A["sbk_p"][0, 0, t * P:(t + 1) * P].rearrange("t h d -> t (h d)") for t in range(PT)]
                + [A["sbk_s"][0].rearrange("b q h d -> (b q) (h d)")])
    sbv_dram = ([A["sbv_p"][0, 0, t * P:(t + 1) * P].rearrange("t h d -> t (h d)") for t in range(PT)]
                + [A["sbv_s"][0].rearrange("b q h d -> (b q) (h d)")])
    GROUPS = [(SBW, SBW), (2 * SBW, SBW), (3 * SBW, 512), (3 * SBW + 512, LAT - 512)]

    with nc.Block() as block:
        @block.sync
        def _(sp):
            sp.dma_start(crow[0:KD, :], A["c_prompt"].rearrange("b (k p) -> (b k) p", p=P)).then_inc(c_in, 16)
            sp.dma_start(crow[KD:, :], A["c_sample"].rearrange("b (k p) -> (b k) p", p=P)).then_inc(c_in, 16)
            for i in range(NWA):
                sp.dma_start(wada[i][:], A["w_ada"][0].rearrange("(k p) m -> p k m", p=P)[:, :, i * WA * P:(i + 1) * WA * P]
                             ).then_inc(wada_in[i], 16)
            for k in range(KD):
                sp.dma_start(win[:, k, :], A["w_in"][0, k * P:(k + 1) * P, :]).then_inc(win_in[k], 16)
            for t in range(NT):
                sp.wait_ge(tok_ready[0], t + 1)
                sp.dma_start(sbk_dram[t], ktok[t % 2][:]).then_inc(sbk_out[t % 2], 16)
                sp.wait_ge(tok_ready[1], t + 1)
                sp.dma_start(sbv_dram[t], vt[:, t, :]).then_inc(sbv_out, 16)
            sp.wait_ge(sbk_out[0], 16 * 3)
            sp.wait_ge(sbk_out[1], 16 * 2)
            sp.wait_ge(sbv_out, 16 * NT)

        @block.gpsimd
        def _(pool):
            pass

        @block.scalar
        def _(act):
            act.dma_start(const[:], A["table"]).then_inc(const_in, 16)
            for name, n in VECTORS:
                act.dma_start(vrow[VROW[name]:VROW[name] + n, :], A[name].rearrange("a (k p) -> (a k) p", p=P)).then_inc(vec_in, 16)
            for t in range(NT):
                act.dma_start(x[:, t, :], x_dram[t]).then_inc(x_in[t], 16)
            act.wait_ge(small_T, 2)
            act.activation(cexp[:], PS[:, 0, 0:NC_ * KD], ACT.Exp, scale=-1.0).then_inc(c_exp, 1)
            for t in range(NT):
                act.wait_ge(x_in[t], 16)
                if t >= 1:
                    act.wait_ge(x_sq, t)
                act.activation(junk[:], x[:, t, :], ACT.Square, accum_out=stat[:, 0, t:t + 1]).then_inc(x_sq, 1)
            act.wait_ge(x_rstd, 1)
            act.activation(stat[:, 1, 0:NT], stat[:, 1, 0:NT], ACT.Sqrt).then_inc(x_sqrt, 1)
            act.wait_ge(x_rstd, 2)
            for t in range(NT):
                if t >= 2:
                    act.wait_ge(xT_psum, 2 * (t - 1))
                act.activation(xn[t % 2][:], x[:, t, :], ACT.Copy, scale=stat[:, 2, t:t + 1]).then_inc(xn_ready, 1)
            for t in range(NT):
                act.wait_ge(tok_psum[0], t + 1)
                if t >= 2:
                    act.wait_ge(sbk_out[t % 2], 16 * (t // 2))
                    act.wait_ge(kT_psum, t - 1)
                act.activation(ktok[t % 2][:], PS[:, 0, :], ACT.Copy).then_inc(tok_ready[0], 1)
                act.wait_ge(tok_psum[2], t + 1)
                act.activation(lat[:, t, 0:512], PS[:, 2, :], ACT.Copy).then_inc(tok_ready[2], 1)
                act.wait_ge(kT_psum, t + 1)
                act.activation(kT[:, :, t * P:(t + 1) * P], PS[:, 4, :].rearrange("p (c n) -> p c n", c=4), ACT.Copy
                               ).then_inc(kT_ready, 1)

        @block.tensor
        def _(pe):
            pe.wait_ge(const_in, 16)
            pe.wait_ge(vec_in, 16 * len(VECTORS))
            pe.transpose(PS[:, 1, 0:NV], vrow[:], ident[0:NV, 0:NV]).then_inc(small_T, 1)
            pe.wait_ge(c_in, 32)
            pe.transpose(PS[:, 0, 0:NC_ * KD], crow[:], ident[0:NC_ * KD, 0:NC_ * KD]).then_inc(small_T, 1)
            pe.wait_ge(small_ready, 2)
            for i in range(NWA):
                pe.wait_ge(wada_in[i], 16)
                for j in range(WA):
                    m = i * WA + j
                    for k in range(KD):
                        mm = pe.matmul(PS[:, 2, m * NC_:(m + 1) * NC_], wada[i][:, k, j * P:(j + 1) * P], cT[:, :, k],
                                       start=k == 0, stop=k == KD - 1)
            mm.then_inc(ada_psum, 1)
            for t in range(NT):
                pe.wait_ge(xn_ready, t + 1)
                if t == 0:
                    pe.wait_ge(ada_ready, 3)
                for b in range(2):
                    if t >= 2:
                        pe.wait_ge(hT_ready, 2 * (t - 2) + b + 1)
                    for j in range(4):
                        k = 4 * b + j
                        mm = pe.transpose(PS[:, 4 + 2 * (t % 2) + b, j * P:(j + 1) * P], xn[t % 2][:, k * P:(k + 1) * P], ident)
                    mm.then_inc(xT_psum, 1)
            for t in range(NT):
                pe.wait_ge(hT_ready, 2 * (t + 1))
                for g, (c0, w) in enumerate(GROUPS):
                    if t >= 1:
                        pe.wait_ge(tok_ready[g], t)
                    elif g == 2:
                        pe.wait_ge(ada_ready, 3)
                    for k in range(KD):
                        if t == 0 and g == 0:
                            pe.wait_ge(win_in[k], 16)
                        mm = pe.matmul(PS[:, g, 0:w], hT[:, k, t * P:(t + 1) * P], win[:, k, c0:c0 + w],
                                       start=k == 0, stop=k == KD - 1)
                    mm.then_inc(tok_psum[g], 1)
                pe.wait_ge(tok_ready[0], t + 1)
                if t >= 1:
                    pe.wait_ge(kT_ready, t)
                else:
                    pe.wait_ge(hT_ready, 2 * NT)
                for c in range(4):
                    mm = pe.transpose(PS[:, 4, c * P:(c + 1) * P], ktok[t % 2][:, c * P:(c + 1) * P], ident)
                mm.then_inc(kT_psum, 1)
            for c in range(SBW // P):
                for b in range(2):
                    i = 2 * c + b
                    if i >= 2:
                        pe.wait_ge(q_ready, i - 1)
                    for k in range(KD):
                        mm = pe.matmul(PS[:, 6 + b, 0:HALF], win[:, k, c * P:(c + 1) * P], hT[:, k, b * HALF:(b + 1) * HALF],
                                       start=k == 0, stop=k == KD - 1)
                    mm.then_inc(q_psum, 1)

        @block.vector
        def _(dve):
            step = Step(dve, v_step)
            dve.wait_ge(small_T, 1)
            dve.tensor_copy(vecT[:], PS[:, 1, 0:NV]).then_inc(small_ready, 1)
            dve.wait_ge(c_exp, 1)
            step(dve.tensor_scalar(cexp[:], cexp[:], 1.0, None, ALU.add))
            step.wait()
            step(dve.reciprocal(cexp[:], cexp[:]))
            step.wait()
            dve.tensor_tensor(cT[:].rearrange("p a k -> p (a k)"), PS[:, 0, 0:NC_ * KD], cexp[:], ALU.mult).then_inc(small_ready, 1)
            dve.wait_ge(x_sq, NT)
            dve.tensor_scalar(stat[:, 1, 0:NT], stat[:, 0, 0:NT], 1.0 / D, EPS, ALU.mult, ALU.add).then_inc(x_rstd, 1)
            dve.wait_ge(x_sqrt, 1)
            dve.reciprocal(stat[:, 2, 0:NT], stat[:, 1, 0:NT]).then_inc(x_rstd, 1)
            dve.wait_ge(ada_psum, 1)
            dve.wait_ge(small_ready, 1)
            m = 2 * KD
            dve.tensor_tensor(adaT[:, 0:m, :], PS[:, 2, 0:m * NC_].rearrange("p (m c) -> p m c", c=NC_),
                              vecT[:, VROW["b_ada"]:VROW["b_ada"] + m].unsqueeze(2).broadcast_to((P, m, NC_)), ALU.add).then_inc(ada_ready, 1)
            dve.wait_ge(ada_ready, 1)
            dve.tensor_scalar(coef[:, 0], adaT[:, SC1:SC1 + KD, :], 1.0, None, ALU.add).then_inc(ada_ready, 1)
            dve.wait_ge(ada_ready, 2)
            g = VROW["g_mix_pre"]
            dve.tensor_tensor(coef[:, 0], coef[:, 0], vecT[:, g:g + KD].unsqueeze(2).broadcast_to((P, KD, NC_)), ALU.mult).then_inc(ada_ready, 1)
            dve.wait_ge(ada_ready, 3)
            for t in range(NT):
                for b in range(2):
                    dve.wait_ge(xT_psum, 2 * t + b + 1)
                    modulate(dve, step, hT, PS[:, 4 + 2 * (t % 2) + b, :], coef[:, 0], adaT[:, SH1:SH1 + KD, :], t, b, hT_ready)
            for t in range(NT):
                dve.wait_ge(tok_psum[1], t + 1)
                dve.tensor_copy(vt[:, t, :], PS[:, 1, :]).then_inc(tok_ready[1], 1)
                dve.wait_ge(tok_psum[3], t + 1)
                dve.tensor_copy(lat[:, t, 512:LAT], PS[:, 3, 0:LAT - 512]).then_inc(tok_ready[3], 1)
            for c in range(SBW // P):
                for b in range(2):
                    dve.wait_ge(q_psum, 2 * c + b + 1)
                    dve.tensor_scalar(qT[:, c, b * HALF:(b + 1) * HALF], PS[:, 6 + b, 0:HALF], SB_SCALE, None, ALU.mult).then_inc(q_ready, 1)


def modulate(dve, step, out, psum, scale, shift, t, b, done):
    cols = slice(4 * b, 4 * b + 4)
    if t < PT:
        dst = out[:, cols, t * P:(t + 1) * P]
        src = psum.rearrange("p (k n) -> p k n", k=4)
        s, h = (v[:, cols, 0:1].broadcast_to((P, 4, P)) for v in (scale, shift))
    else:
        dst = out[:, cols, t * P:(t + 1) * P].rearrange("p k (s q) -> p k s q", q=STEP)
        src = psum.rearrange("p (k s q) -> p k s q", k=4, q=STEP)
        s, h = (v[:, cols, 1:NC_].unsqueeze(3).broadcast_to((P, 4, NSEQ, STEP)) for v in (scale, shift))
    step(dve.tensor_tensor(dst, src, s, ALU.mult))
    step.wait()
    dve.tensor_tensor(dst, dst, h, ALU.add).then_inc(done, 1)


def phase_latents(nc, A, env):
    sb, sem, PS, C, ident = (env[k] for k in ("sb", "sem", "PS", "C", "ident"))
    vecT, stat, lat, junk = (env[k] for k in ("vecT", "stat", "lat", "junk"))
    CQ, CK = QR // P, KVR // P
    wuq = sb("wuq", 135, [P, CQ, H * QK])
    wuk = sb("wuk", 144, [P, CK, H * HD])
    wuv = sb("wuv", 148, [P, CK, H * HD])
    qtok = [sb(f"qtok{i}", 152 + 3 * i, [P, H * QK]) for i in range(2)]
    gkv = sb("gkv", 158, [P, KVR])
    qlatT = sb("qlatT", 66, [P, CQ, N])
    ckvT = sb("ckvT", 74, [P, CK, N])
    qmT = sb("qmT", 79, [QK, H, N])
    kmT = sb("kmT", 99, [QK, H, SEQ])
    vm = sb("vm", 115, [P, PT, SBW])
    krT = sb("krT", 123, [QK, P])
    wukT = sb("wukT", 123.5, [HD, H, CK, P])
    krpad = sb("krpad", 10, [P, NT, QK])
    rtmp = sb("rtmp", 12, [P, 2, H * RH])
    rtmp2 = sb("rtmp2", 13, [P, 4, H * RH])
    qabsT = sb("qabsT", 18, [P, CK, H, P])
    env["env"].update(ckvT=ckvT, qmT=qmT, kmT=kmT, vm=vm, krT=krT, qabsT=qabsT, qlatT=qlatT)
    cos = C["cos"].rearrange("p (t r) -> p t r", r=RH)
    sin = C["sin"].rearrange("p (t r) -> p t r", r=RH)
    nq, nkv, nrope = 0, QR, QR + KVR

    wuq_in, wuk_in, wuv_in, gkv_in = sem("wuq_in"), sem("wuk_in"), sem("wuv_in"), sem("gkv_in")
    l_sq, l_var, l_sqrt, l_rstd, l_step = sem("l_sq"), sem("l_var"), sem("l_sqrt"), sem("l_rstd"), sem("l_step")
    pad_zero, kr_ready, ckv_ready, qn_ready = sem("pad_zero"), sem("kr_ready"), sem("ckv_ready"), sem("qn_ready")
    lat_out = sem("lat_out")
    ql_psum, ql_ready, cl_psum, cl_ready, kr_evac = sem("ql_psum"), sem("ql_ready"), sem("cl_psum"), sem("cl_ready"), sem("kr_evac")
    up_psum, up_ready, rot_ready = sem("up_psum"), sem("up_ready"), sem("rot_ready")
    qm_psum, qm_ready = sem("qm_psum"), [sem("qm_ready0"), sem("qm_ready1")]
    item_psum, item_ready = [sem("item_psum0"), sem("item_psum1")], [sem("item_ready0"), sem("item_ready1")]
    ckv_dram = ([A["ckv_p"][0, 0, t * P:(t + 1) * P, :] for t in range(PT)] + [A["ckv_s"][0].rearrange("b q c -> (b q) c")])
    kr_dram = ([A["kr_p"][0, 0, t * P:(t + 1) * P, :] for t in range(PT)] + [A["kr_s"][0].rearrange("b q c -> (b q) c")])
    NITEM = H + PT + 2 * H * CK // 4

    def item_target(i):
        if i < H:
            return kmT[0:HD, i, :], PS[0:HD, 6 + i % 2, :]
        if i < H + PT:
            return vm[:, i - H, :], PS[:, 6 + i % 2, :]
        j = i - H - PT
        if j < 4:
            return wukT[:].rearrange("p h c n -> p (h c n)")[:, 512 * j:512 * (j + 1)], PS[0:HD, 6 + i % 2, :]
        j -= 4
        return qabsT[:].rearrange("p c h n -> p (c h n)")[:, 512 * j:512 * (j + 1)], PS[:, 6 + i % 2, :]

    with nc.Block() as block:
        @block.sync
        def _(sp):
            sp.dma_start(wuq[:], A["w_uq"][0].rearrange("(c p) m -> p c m", p=P)).then_inc(wuq_in, 16)
            sp.dma_start(gkv[:], A["g_kv_lat"].broadcast_to((P, KVR))).then_inc(gkv_in, 16)
            sp.dma_start(wuk[:], A["w_uk"][0].rearrange("(c p) h m -> p c (h m)", p=P)).then_inc(wuk_in, 16)
            sp.dma_start(wuv[:], A["w_uv"][0].rearrange("(c p) h m -> p c (h m)", p=P)).then_inc(wuv_in, 16)
            sp.wait_ge(kr_ready, 1)
            for t in range(NT):
                sp.dma_start(kr_dram[t], krpad[:, t, HD:QK]).then_inc(lat_out, 16)
            for t in range(NT):
                sp.wait_ge(ckv_ready, t + 1)
                sp.dma_start(ckv_dram[t], lat[:, t, nkv:nrope]).then_inc(lat_out, 16)
            sp.wait_ge(lat_out, 16 * 2 * NT)

        @block.gpsimd
        def _(pool):
            pool.memset(krpad[:, :, 0:HD], 0.0).then_inc(pad_zero, 1)

        @block.scalar
        def _(act):
            for t in range(NT):
                for j, (a, b) in enumerate(((nq, nkv), (nkv, nrope))):
                    if t + j:
                        act.wait_ge(l_sq, 2 * t + j)
                    act.activation(junk[:, 0:b - a], lat[:, t, a:b], ACT.Square, accum_out=stat[:, 3 + j, t:t + 1]).then_inc(l_sq, 1)
            act.wait_ge(l_var, 2)
            act.activation(stat[:, 3:5, 0:NT], stat[:, 3:5, 0:NT], ACT.Sqrt).then_inc(l_sqrt, 1)
            act.wait_ge(l_rstd, 1)
            for t in range(NT):
                act.activation(lat[:, t, nq:nkv], lat[:, t, nq:nkv], ACT.Copy, scale=stat[:, 5, t:t + 1]).then_inc(qn_ready, 1)
            for t in range(NT):
                act.wait_ge(cl_psum, t + 1)
                act.activation(ckvT[:, :, t * P:(t + 1) * P], PS[:, 1, 0:KVR].rearrange("p (c n) -> p c n", c=CK), ACT.Copy
                               ).then_inc(cl_ready, 1)
                src = PS[HD:QK, 1, KVR:KVR + P]
                if t < PT:
                    act.activation(kmT[HD:QK, :, t * P:(t + 1) * P], src.unsqueeze(1).broadcast_to((ROPE, H, P)), ACT.Copy).then_inc(kr_evac, 1)
                else:
                    act.activation(krT[:], PS[0:QK, 1, KVR:KVR + P], ACT.Copy).then_inc(kr_evac, 1)
                act.wait_ge(up_psum, t + 1)
                if t >= 2:
                    act.wait_ge(qm_psum, 2 * (t - 1))
                act.activation(qtok[t % 2][:].rearrange("p (a b) -> p a b", a=2), PS[:, 2:4, 0:H * QK // 2], ACT.Copy).then_inc(up_ready, 1)
                act.wait_ge(qm_psum, 2 * t + 1)
                act.activation(qmT[:, 0:4, t * P:(t + 1) * P], PS[0:QK, 4, :].rearrange("p (h n) -> p h n", h=4), ACT.Copy).then_inc(qm_ready[0], 1)
            for i in range(0, NITEM, 2):
                act.wait_ge(item_psum[0], i // 2 + 1)
                act.activation(*item_target(i), ACT.Copy).then_inc(item_ready[0], 1)

        @block.tensor
        def _(pe):
            for t in range(NT):
                cols = slice(t * P, (t + 1) * P)
                pe.wait_ge(qn_ready, t + 1)
                if t:
                    pe.wait_ge(ql_ready, t)
                for c in range(CQ):
                    mm = pe.transpose(PS[:, 0, c * P:(c + 1) * P], lat[:, t, c * P:(c + 1) * P], ident)
                mm.then_inc(ql_psum, 1)
                pe.wait_ge(ckv_ready, t + 1)
                pe.wait_ge(kr_ready, 1)
                if t:
                    pe.wait_ge(kr_evac, t)
                for c in range(CK):
                    pe.transpose(PS[:, 1, c * P:(c + 1) * P], lat[:, t, nkv + c * P:nkv + (c + 1) * P], ident)
                pe.transpose(PS[0:QK, 1, KVR:KVR + P], krpad[:, t, :], ident).then_inc(cl_psum, 1)
                pe.wait_ge(ql_ready, t + 1)
                if t:
                    pe.wait_ge(up_ready, t)
                else:
                    pe.wait_ge(wuq_in, 16)
                for b in range(2):
                    for c in range(CQ):
                        mm = pe.matmul(PS[:, 2 + b, 0:H * QK // 2], qlatT[:, c, cols], wuq[:, c, b * H * QK // 2:(b + 1) * H * QK // 2],
                                       start=c == 0, stop=c == CQ - 1)
                mm.then_inc(up_psum, 1)
                pe.wait_ge(rot_ready, t + 1)
                for b in range(2):
                    if t:
                        pe.wait_ge(qm_ready[b], t)
                    for j in range(4):
                        h = 4 * b + j
                        mm = pe.transpose(PS[0:QK, 4 + b, j * P:(j + 1) * P], qtok[t % 2][:, h * QK:(h + 1) * QK], ident)
                    mm.then_inc(qm_psum, 1)
            pe.wait_ge(cl_ready, NT)
            pe.wait_ge(wuk_in, 16)
            pe.wait_ge(wuv_in, 16)
            for i in range(NITEM):
                out = item_target(i)[1]
                if i >= 2:
                    pe.wait_ge(item_ready[i % 2], i // 2)
                if i < H:
                    for c in range(CK):
                        mm = pe.matmul(out, wuk[:, c, i * HD:(i + 1) * HD], ckvT[:, c, 0:SEQ], start=c == 0, stop=c == CK - 1)
                elif i < H + PT:
                    t = i - H
                    for c in range(CK):
                        mm = pe.matmul(out, ckvT[:, c, t * P:(t + 1) * P], wuv[:, c, :], start=c == 0, stop=c == CK - 1)
                elif i < H + PT + 4:
                    for n in range(4):
                        h, c = divmod(4 * (i - H - PT) + n, CK)
                        mm = pe.transpose(out[:, n * P:(n + 1) * P], wuk[:, c, h * HD:(h + 1) * HD], ident)
                else:
                    if i == H + PT + 4:
                        pe.wait_ge(item_ready[0], (i + 1) // 2)
                        pe.wait_ge(item_ready[1], i // 2)
                        pe.wait_ge(qm_ready[0], NT)
                        pe.wait_ge(qm_ready[1], NT)
                    for n in range(4):
                        c, h = divmod(4 * (i - H - PT - 4) + n, H)
                        mm = pe.matmul(out[:, n * P:(n + 1) * P], wukT[:, h, c, :], qmT[0:HD, h, SEQ:N], start=True, stop=True)
                mm.then_inc(item_psum[i % 2], 1)

        @block.vector
        def _(dve):
            step = Step(dve, l_step)
            dve.wait_ge(l_sq, 2 * NT)
            dve.tensor_scalar(stat[:, 3, 0:NT], stat[:, 3, 0:NT], 1.0 / QR, EPS, ALU.mult, ALU.add).then_inc(l_var, 1)
            dve.tensor_scalar(stat[:, 4, 0:NT], stat[:, 4, 0:NT], 1.0 / KVR, EPS, ALU.mult, ALU.add).then_inc(l_var, 1)
            a, b = lat[:, :, nrope:nrope + RH], lat[:, :, nrope + RH:LAT]
            u, v = (rtmp[:, i, 0:NT * RH].rearrange("p (t r) -> p t r", r=RH) for i in range(2))
            for x1, x2, op, dst in ((a, b, ALU.subtract, krpad[:, :, HD:HD + RH]), (b, a, ALU.add, krpad[:, :, HD + RH:QK])):
                step(dve.tensor_tensor(u, x1, cos, ALU.mult))
                step(dve.tensor_tensor(v, x2, sin, ALU.mult))
                step.wait()
                step(last := dve.tensor_tensor(dst, u, v, op))
                step.wait()
            dve.wait_ge(l_sqrt, 1)
            dve.reciprocal(stat[:, 5:7, 0:NT], stat[:, 3:5, 0:NT]).then_inc(l_rstd, 1)
            dve.wait_ge(l_rstd, 1)
            dve.wait_ge(pad_zero, 1)
            dve.sem_inc(kr_ready, 1)
            dve.wait_ge(gkv_in, 16)
            for t in range(NT):
                dve.scalar_tensor_tensor(out=lat[:, t, nkv:nrope], in0=lat[:, t, nkv:nrope], scalar=stat[:, 6, t:t + 1], in1=gkv[:],
                                         op0=ALU.mult, op1=ALU.mult).then_inc(ckv_ready, 1)
            g = VROW["g_q_lat"]
            for t in range(NT):
                cols = slice(t * P, (t + 1) * P)
                dve.wait_ge(ql_psum, t + 1)
                dve.tensor_tensor(qlatT[:, :, cols], PS[:, 0, 0:QR].rearrange("p (c n) -> p c n", c=CQ),
                                  vecT[:, g:g + CQ].unsqueeze(2).broadcast_to((P, CQ, P)), ALU.mult).then_inc(ql_ready, 1)
                dve.wait_ge(up_ready, t + 1)
                q = qtok[t % 2][:].rearrange("p (h m) -> p h m", h=H)
                a, b = q[:, :, HD:HD + RH], q[:, :, HD + RH:QK]
                c, s = (w[:, t, :].unsqueeze(1).broadcast_to((P, H, RH)) for w in (cos, sin))
                u, v = (rtmp2[:, i, :].rearrange("p (h r) -> p h r", h=H) for i in range(2))
                w, z = (rtmp2[:, i, :].rearrange("p (h r) -> p h r", h=H) for i in range(2, 4))
                step(dve.tensor_tensor(u, a, c, ALU.mult))
                step(dve.tensor_tensor(v, b, s, ALU.mult))
                step(dve.tensor_tensor(w, b, c, ALU.mult))
                step(dve.tensor_tensor(z, a, s, ALU.mult))
                step.wait()
                step(dve.tensor_tensor(a, u, v, ALU.subtract))
                step.wait()
                step(dve.tensor_tensor(b, w, z, ALU.add))
                step.wait()
                dve.sem_inc(rot_ready, 1)
                dve.wait_ge(qm_psum, 2 * t + 2)
                dve.tensor_copy(qmT[:, 4:8, cols], PS[0:QK, 5, :].rearrange("p (h n) -> p h n", h=4)).then_inc(qm_ready[1], 1)
            for i in range(1, NITEM, 2):
                dve.wait_ge(item_psum[1], i // 2 + 1)
                dve.tensor_copy(*item_target(i)).then_inc(item_ready[1], 1)


def phase_prompt_attention(nc, A, env):
    sb, sem, PS, C, ident = (env[k] for k in ("sb", "sem", "PS", "C", "ident"))
    stat, qT, kT, vt, qmT, kmT, vm = (env[k] for k in ("stat", "qT", "kT", "vt", "qmT", "kmT", "vm"))
    osT = sb("osT", 135, [P, SBW // P, N])
    omT = sb("omT", 145, [P, SBW // P, N])
    env["env"].update(osT=osT, omT=omT)
    t1 = sb("t1", 189, [P, 2, SEQ])
    t2 = sb("t2", 193, [P, 2, SEQ])
    pr = sb("pr", 197, [P, 2, SEQ])
    aT = sb("aT", 10, [P, 2, PT, P])
    pT = sb("pT", 14, [P, 2, PT, P])
    peak, total, inverse = stat[:, 3, 0:2], stat[:, 4, 0:2], stat[:, 5, 0:2]
    names = ("z_psum s_psum z_abs s_peak s_bias soft1 soft2 soft soft_kept tail logit logit_kept a_ready p_exp p_inv p_ready "
             "mT_psum aT_psum mT0 mT1 aT0 aT1 om_psum os_psum om_out os_out").split()
    S = {n: sem("pa_" + n) for n in names}
    ROUNDS = [(i, hp) for i in range(PT) for hp in range(H // 2)]
    R = len(ROUNDS)

    def W(r):
        return (ROUNDS[r][0] + 1) * P

    with nc.Block() as block:
        @block.gpsimd
        def _(pool):
            for r, (i, hp) in enumerate(ROUNDS):
                d = slice(i * P, i * P + P)
                for buf, mask, op, need, done in ((t1, "keep", ALU.mult, "soft", "soft_kept"), (t2, "drop", ALU.add, "logit", "logit_kept")):
                    pool.wait_ge(S[need], r + 1)
                    pool.tensor_tensor(buf[:, :, d], buf[:, :, d], C[mask].unsqueeze(1).broadcast_to((P, 2, P)), op).then_inc(S[done], 1)

        @block.scalar
        def _(act):
            def softplus(r):
                w = W(r)
                act.wait_ge(S["z_psum"], r + 1)
                if r:
                    act.wait_ge(S["tail"], 2 * r)
                act.activation(t1[:, :, 0:w], PS[:, 0:2, 0:w], ACT.Abs).then_inc(S["z_abs"], 1)
                act.wait_ge(S["z_abs"], r + 1)
                act.activation(t1[:, :, 0:w], t1[:, :, 0:w], ACT.Exp, scale=-1.0).then_inc(S["soft1"], 1)
                act.wait_ge(S["soft1"], r + 1)
                act.activation(t1[:, :, 0:w], t1[:, :, 0:w], ACT.Ln, bias=1.0).then_inc(S["soft2"], 1)

            def softmax(r):
                w = W(r)
                act.wait_ge(S["s_bias"], r + 1)
                if r:
                    act.wait_ge(S["mT_psum"], r)
                for j in range(2):
                    act.activation(pr[:, j, 0:w], PS[:, 2 + j, 0:w], ACT.Exp, bias=peak[:, j:j + 1], scale=MLA_SCALE,
                                   accum_out=total[:, j:j + 1]).then_inc(S["p_exp"], 1)

            def transposed(r, dst, psum, done, used):
                i = ROUNDS[r][0]
                act.wait_ge(S[psum], r + 1)
                if r:
                    act.wait_ge(S[used], r)
                act.activation(dst[:, 0, 0:i + 1, :], PS[:, 4, 0:W(r)].rearrange("p (k n) -> p k n", n=P), ACT.Copy).then_inc(S[done], 1)

            softplus(0)
            softmax(0)
            transposed(0, pT, "mT_psum", "mT0", "om_psum")
            for r, (i, hp) in enumerate(ROUNDS):
                act.wait_ge(S["logit_kept"], r + 1)
                act.activation(t2[:, :, 0:W(r)], t2[:, :, 0:W(r)], ACT.Exp).then_inc(S["a_ready"], 1)
                if r + 1 < R:
                    softplus(r + 1)
                act.wait_ge(S["om_psum"], r + 1)
                act.activation(omT[:, hp, i * P:(i + 1) * P], PS[:, 7, 0:P], ACT.Copy).then_inc(S["om_out"], 1)
                transposed(r, aT, "aT_psum", "aT0", "os_psum")
                if r + 1 < R:
                    softmax(r + 1)
                    transposed(r + 1, pT, "mT_psum", "mT0", "om_psum")

        @block.tensor
        def _(pe):
            def sb_scores(r):
                i, hp = ROUNDS[r]
                if r:
                    pe.wait_ge(S["logit"], r)
                for j in range(2):
                    rows = slice(j * HD, (j + 1) * HD)
                    mm = pe.matmul(PS[:, j, 0:W(r)], qT[rows, hp, i * P:(i + 1) * P], kT[rows, hp, 0:W(r)], start=True, stop=True)
                mm.then_inc(S["z_psum"], 1)

            def mla_scores(r):
                i, hp = ROUNDS[r]
                if r:
                    pe.wait_ge(S["p_exp"], 2 * r)
                for j in range(2):
                    h = 2 * hp + j
                    pe.matmul(PS[:, 2 + j, 0:W(r)], qmT[:, h, i * P:(i + 1) * P], kmT[:, h, 0:W(r)], start=True, stop=False)
                    mm = pe.matmul(PS[:, 2 + j, i * P:(i + 1) * P], C["chunk_row"][0:QK, :], C["chunk_col"][0:QK, :], start=False, stop=True)
                mm.then_inc(S["s_psum"], 1)

            def transposes(r, src, need, count, free, done):
                for j in range(2):
                    pe.wait_ge(S[need], count)
                    for f, n in free:
                        if n:
                            pe.wait_ge(S[f], n)
                    for k in range(ROUNDS[r][0] + 1):
                        mm = pe.transpose(PS[:, 4 + j, k * P:(k + 1) * P], src[:, j, k * P:(k + 1) * P], ident)
                mm.then_inc(S[done], 1)

            def values(r, v, wT, need, free, bank, done):
                i, hp = ROUNDS[r]
                for n in need:
                    pe.wait_ge(S[n], r + 1)
                if r:
                    pe.wait_ge(S[free], r)
                for j in range(2):
                    h = 2 * hp + j
                    for k in range(i + 1):
                        mm = pe.matmul(PS[j * HD:(j + 1) * HD, bank, 0:P], v[:, k, h * HD:(h + 1) * HD], wT[:, j, k, :],
                                       start=k == 0, stop=k == i)
                mm.then_inc(S[done], 1)

            sb_scores(0)
            mla_scores(0)
            for r in range(R):
                transposes(r, pr, "p_ready", 2 * (r + 1), (("aT0", r), ("aT1", r)), "mT_psum")
                if r + 1 < R:
                    mla_scores(r + 1)
                values(r, vm, pT, ("mT0", "mT1"), "om_out", 7, "om_psum")
                if r + 1 < R:
                    sb_scores(r + 1)
                transposes(r, t2, "a_ready", r + 1, (("mT0", r + 1), ("mT1", r + 1)), "aT_psum")
                values(r, vt, aT, ("aT0", "aT1"), "os_out", 6, "os_psum")

        @block.vector
        def _(dve):
            def start(r):
                w = W(r)
                dve.wait_ge(S["s_psum"], r + 1)
                if r:
                    dve.wait_ge(S["p_ready"], 2 * r)
                dve.tensor_reduce(peak, PS[:, 2:4, 0:w], AX_X, ALU.max).then_inc(S["s_peak"], 1)
                dve.wait_ge(S["s_peak"], r + 1)
                dve.tensor_scalar(peak, peak, -MLA_SCALE, None, ALU.mult).then_inc(S["s_bias"], 1)

            def transposed(r, dst, psum, done, used):
                i = ROUNDS[r][0]
                dve.wait_ge(S[psum], r + 1)
                if r:
                    dve.wait_ge(S[used], r)
                dve.tensor_copy(dst[:, 1, 0:i + 1, :], PS[:, 5, 0:W(r)].rearrange("p (k n) -> p k n", n=P)).then_inc(S[done], 1)

            start(0)
            for r, (i, hp) in enumerate(ROUNDS):
                w = W(r)
                dve.wait_ge(S["soft2"], r + 1)
                dve.scalar_tensor_tensor(out=t1[:, :, 0:w], in0=PS[:, 0:2, 0:w], scalar=0.0, in1=t1[:, :, 0:w],
                                         op0=ALU.max, op1=ALU.add).then_inc(S["soft"], 1)
                dve.wait_ge(S["p_exp"], 2 * (r + 1))
                dve.reciprocal(inverse, total).then_inc(S["p_inv"], 1)
                dve.wait_ge(S["p_inv"], r + 1)
                for j in range(2):
                    dve.tensor_scalar(pr[:, j, 0:w], pr[:, j, 0:w], inverse[:, j:j + 1], None, ALU.mult).then_inc(S["p_ready"], 1)
                dve.wait_ge(S["soft_kept"], r + 1)
                if r:
                    dve.wait_ge(S["aT_psum"], r)
                last = w - 1
                for j in range(2):
                    rev = (lambda b: b[:, j, last::-1])
                    dve.tensor_tensor_scan(rev(t2), C["ones"][:, 0:1].broadcast_to((P, w)), rev(t1), 0.0, ALU.mult, ALU.add).then_inc(S["tail"], 1)
                dve.wait_ge(S["tail"], 2 * (r + 1))
                dve.tensor_tensor(t2[:, :, 0:w], PS[:, 0:2, 0:w], t2[:, :, 0:w], ALU.subtract).then_inc(S["logit"], 1)
                transposed(r, pT, "mT_psum", "mT1", "om_psum")
                if r + 1 < R:
                    start(r + 1)
                transposed(r, aT, "aT_psum", "aT1", "os_psum")
                dve.wait_ge(S["os_psum"], r + 1)
                dve.tensor_copy(osT[:, hp, i * P:(i + 1) * P], PS[:, 6, 0:P]).then_inc(S["os_out"], 1)


def phase_sample_attention(nc, A, env):
    sb, sem, PS, C, ident = (env[k] for k in ("sb", "sem", "PS", "C", "ident"))
    stat, qT, kT, qmT, ckvT, krT, qabsT, osT, omT = (env[k] for k in ("stat", "qT", "kT", "qmT", "ckvT", "krT", "qabsT", "osT", "omT"))
    KBLK, CQ, CK = PAST // P, SBW // P, KVR // P
    flat = PS[:].rearrange("p b n -> p (b n)")
    z, s = flat[:, 0:KEYS], flat[:, 1024:1024 + KEYS]
    kc = [sb("kc0", 46, [P, KBLK, SBW]), sb("kc1", 99, [P, KBLK, SBW])]
    vc = [sb("vc0", 54, [P, KBLK, SBW]), sb("vc1", 107, [P, KBLK, SBW])]
    cc = [sb("cc0", 62, [P, KBLK, KVR]), sb("cc1", 115, [P, KBLK, KVR])]
    kr = [sb("kr0", 201, [P, KBLK, QK]), sb("kr1", 119, [P, KBLK, QK])]
    vnew = [sb("vnew0", 155, [P, SBW]), sb("vnew1", 131.5, [P, SBW])]
    cnew = [sb("cnew0", 157, [P, KVR]), sb("cnew1", 133.5, [P, KVR])]
    keyT = sb("keyT", 10, [P, CQ, PAST])
    latT = sb("latT", 66, [P, CK, PAST])
    rotT = sb("rotT", 70, [QK, PAST])
    qblk = sb("qblk", 72, [P, CQ, P])
    qabs = sb("qabs", 120.5, [P, CK, P])
    qrot = sb("qrot", 121.5, [QK, P])
    olatT = sb("olatT", 123.5, [P, CK, H, P])
    t1, t2, pr = sb("st1", 189, [P, KEYS]), sb("st2", 191.25, [P, KEYS]), sb("spr", 193.5, [P, KEYS])
    aT, pT = sb("saT", 196, [P, KBLK + 1, P]), sb("spT", 198.5, [P, KBLK + 1, P])
    wuv = sb("wuv_again", 203, [P, CK, SBW])
    peak, total, inverse = stat[:, 3, 0:1], stat[:, 4, 0:1], stat[:, 5, 0:1]
    names = ("zeroed qblk_ready q_ready z_psum s_psum z_abs soft1 soft2 soft soft_kept tail logit logit_kept a_ready s_peak s_bias "
             "p_exp p_inv p_ready turned turn0 turn1 ol_psum ol_out os_psum os_out om_psum om_out wuv_in").split()
    S = {n: sem("sa_" + n) for n in names}
    IN = {n: [sem(f"sa_{n}{i}") for i in range(2)] for n in ("kc_in", "vc_in", "cc_in", "kr_in", "new_in")}
    turn = [S["turn0"], S["turn1"]]
    KV, PER = CQ + CK + 1, CQ + CK + 1 + 4

    def new_cols(b, step=STEP):
        return bass.ds(SEQ + b * step, step)

    def loop(eng, body):
        with eng.Fori(0, NSEQ // 2 - 1) as pair:
            body(pair, 0, True)
            body(pair, 1, True)
        body(NSEQ // 2 - 1, 0, True)
        body(NSEQ // 2 - 1, 1, False)

    def place(e, n, more):
        return KV + PER * e + (n if more else n - KV)

    def piece(pair, e, n, more):
        return pair * (2 * PER) + place(e, n, more)

    def parity(e, n, more):
        return place(e, n, more) % 2

    def before(pair, e, n, more):
        return pair * PER + (place(e, n, more) // 2 + 1)

    def piece_target(n, e):
        bank = 4 + e
        if n < CQ:
            return keyT[:, n, :], PS[:, bank, :]
        if n < CQ + CK:
            return latT[:, n - CQ, :], PS[:, bank, :]
        if n < KV:
            return rotT[:], PS[0:QK, bank, :]
        dst = (pT, aT)[(n - KV) // 2]
        if (n - KV) % 2 == 0:
            return dst[:, 0:KBLK, :], PS[:, bank, :].rearrange("p (k n) -> p k n", n=P)
        return dst[0:STEP, KBLK, :], PS[0:STEP, bank, 0:P]

    def evacuate_first(eng, copy, mine):
        for n in range(mine, KV, 2):
            eng.wait_ge(S["turned"], n + 1)
            copy(*piece_target(n, mine)).then_inc(turn[mine], 1)

    def evacuate(eng, copy, mine, pair, e, ns, more):
        for n in ns:
            if parity(e, n, more) == mine:
                eng.wait_ge(S["turned"], piece(pair, e, n, more) + 1)
                copy(*piece_target(n, mine)).then_inc(turn[mine], 1)

    with nc.Block() as block:
        @block.sync
        def _(sp):
            def load(b, e):
                sp.dma_start(kc[e][:], A["cache_sb_k"][0, b].rearrange("(k p) h d -> p k (h d)", p=P)).then_inc(IN["kc_in"][e], 16)
                sp.dma_start(cc[e][:], A["cache_mla_ckv"][0, b].rearrange("(k p) c -> p k c", p=P)).then_inc(IN["cc_in"][e], 16)
                sp.dma_start(kr[e][:, :, HD:QK], A["cache_mla_krope"][0, b].rearrange("(k p) c -> p k c", p=P)).then_inc(IN["kr_in"][e], 16)
                sp.dma_start(vc[e][:], A["cache_sb_v"][0, b].rearrange("(k p) h d -> p k (h d)", p=P)).then_inc(IN["vc_in"][e], 16)
                sp.dma_start(vnew[e][0:STEP, :], A["sbv_s"][0, b].rearrange("q h d -> q (h d)")).then_inc(IN["new_in"][e], 16)
                sp.dma_start(cnew[e][0:STEP, :], A["ckv_s"][0, b]).then_inc(IN["new_in"][e], 16)

            sp.wait_ge(S["zeroed"], 6)
            load(0, 0)
            load(1, 1)
            sp.dma_start(wuv[:], A["w_uv"][0].rearrange("(c p) h m -> p c (h m)", p=P)).then_inc(S["wuv_in"], 16)
            with sp.Fori(1, NSEQ // 2) as it:
                for e in range(2):
                    sp.wait_ge(S["os_psum"], it * 2 + (e - 1))
                    load(it * 2 + e, e)

        @block.gpsimd
        def _(pool):
            for i in range(2):
                pool.memset(vnew[i][:], 0.0).then_inc(S["zeroed"], 1)
                pool.memset(cnew[i][:], 0.0).then_inc(S["zeroed"], 1)
                pool.memset(kr[i][:, :, 0:HD], 0.0).then_inc(S["zeroed"], 1)
            pool.memset(qblk[:], 0.0).then_inc(S["zeroed"], 1)
            pool.memset(aT[:, KBLK, :], 0.0).then_inc(S["zeroed"], 1)
            pool.memset(pT[:, KBLK, :], 0.0).then_inc(S["zeroed"], 1)

            def body(pair, e, more):
                b = pair * 2 + e
                new = slice(PAST, KEYS)
                pool.wait_ge(S["soft"], b + 1)
                pool.tensor_tensor(t1[:, new], t1[:, new], C["new_keep"], ALU.mult).then_inc(S["soft_kept"], 1)
                pool.wait_ge(S["logit"], b + 1)
                pool.tensor_tensor(t2[:, new], t2[:, new], C["new_drop"], ALU.add).then_inc(S["logit_kept"], 1)

            loop(pool, body)

        @block.scalar
        def _(act):
            def copy(dst, src):
                return act.activation(dst, src, ACT.Copy)

            act.sem_inc(turn[0], 1)
            act.sem_inc(S["ol_out"], 1)
            act.wait_ge(S["zeroed"], 9)
            evacuate_first(act, copy, 0)

            def body(pair, e, more):
                b = pair * 2 + e
                act.wait_ge(S["z_psum"], b + 1)
                act.activation(t1[:], z, ACT.Abs).then_inc(S["z_abs"], 1)
                act.wait_ge(S["z_abs"], b + 1)
                act.activation(t1[:], t1[:], ACT.Exp, scale=-1.0).then_inc(S["soft1"], 1)
                act.wait_ge(S["soft1"], b + 1)
                act.activation(t1[:], t1[:], ACT.Ln, bias=1.0).then_inc(S["soft2"], 1)
                act.wait_ge(S["s_bias"], b + 1)
                act.activation(pr[:], s, ACT.Exp, bias=peak, scale=MLA_SCALE, accum_out=total).then_inc(S["p_exp"], 1)
                if more:
                    evacuate(act, copy, 0, pair, e, range(KV), more)
                evacuate(act, copy, 0, pair, e, (KV, KV + 1), more)
                act.wait_ge(S["logit_kept"], b + 1)
                act.activation(t2[:], t2[:], ACT.Exp).then_inc(S["a_ready"], 1)
                act.wait_ge(S["ol_psum"], b + 1)
                act.activation(olatT[:, :, :, bass.ds(b * STEP, STEP)],
                               PS[:, 7, 0:CK * P].rearrange("p (c h q) -> p c h q", c=CK, h=H), ACT.Copy).then_inc(S["ol_out"], 1)
                evacuate(act, copy, 0, pair, e, (KV + 2, KV + 3), more)

            loop(act, body)

        @block.tensor
        def _(pe):
            def turn_piece(out, ins, bank, before):
                pe.wait_ge(turn[bank], before)
                for k, (o, i, idn) in enumerate(zip(out, ins, [ident] * len(ins))):
                    mm = pe.transpose(o, i, idn)
                mm.then_inc(S["turned"], 1)

            def caches(e, count, bank_of, before):
                for n in range(KV):
                    bank = bank_of(n)
                    if n < CQ:
                        src, arrived, rows, width = kc[e], "kc_in", P, slice(n * P, (n + 1) * P)
                    elif n < CQ + CK:
                        src, arrived, rows, width = cc[e], "cc_in", P, slice((n - CQ) * P, (n - CQ + 1) * P)
                    else:
                        src, arrived, rows, width = kr[e], "kr_in", QK, slice(0, QK)
                    pe.wait_ge(IN[arrived][e], count)
                    turn_piece([PS[0:rows, 4 + bank, k * P:(k + 1) * P] for k in range(KBLK)],
                               [src[:, k, width] for k in range(KBLK)], bank, before(n))

            caches(0, 16, lambda n: n % 2, lambda n: n // 2 + 1)
            pe.wait_ge(turn[0], (KV + 1) // 2 + 1)
            pe.wait_ge(turn[1], KV // 2 + 1)

            def body(pair, e, more):
                b = pair * 2 + e
                pe.wait_ge(S["qblk_ready"], b + 1)
                for c in range(CQ):
                    pe.matmul(flat[:, 0:PAST], qblk[:, c, :], keyT[:, c, :], start=c == 0, stop=c == CQ - 1)
                for c in range(CQ):
                    mm = pe.matmul(flat[:, PAST:KEYS], qblk[:, c, :], kT[:, c, new_cols(b)], start=c == 0, stop=c == CQ - 1)
                mm.then_inc(S["z_psum"], 1)
                pe.wait_ge(S["q_ready"], 2 * (b + 1))
                for c in range(CK):
                    pe.matmul(s[:, 0:PAST], qabs[:, c, :], latT[:, c, :], start=c == 0, stop=False)
                pe.matmul(s[:, 0:PAST], qrot[:], rotT[:], start=False, stop=True)
                for c in range(CK):
                    pe.matmul(s[:, PAST:KEYS], qabs[:, c, :], ckvT[:, c, new_cols(b)], start=c == 0, stop=False)
                pe.matmul(s[:, PAST:KEYS], qrot[:], krT[:, bass.ds(b * STEP, STEP)], start=False, stop=True).then_inc(S["s_psum"], 1)
                if more:
                    caches(1 - e, pair * 16 + 16 * (e + 1), lambda n: parity(e, n, more), lambda n: before(pair, e, n, more))
                for w, (src, need) in enumerate(((pr, "p_ready"), (t2, "a_ready"))):
                    pe.wait_ge(S[need], b + 1)
                    n = KV + 2 * w
                    bank = parity(e, n, more)
                    turn_piece([PS[:, 4 + bank, k * P:(k + 1) * P] for k in range(KBLK)],
                               [src[:, k * P:(k + 1) * P] for k in range(KBLK)], bank, before(pair, e, n, more))
                    turn_piece([PS[0:STEP, 5 - bank, 0:P]], [src[:, PAST:KEYS]], 1 - bank, before(pair, e, n + 1, more))
                    pe.wait_ge(turn[bank], before(pair, e, n, more) + 1)
                    pe.wait_ge(turn[1 - bank], before(pair, e, n + 1, more) + 1)
                    if w == 0:
                        pe.wait_ge(IN["new_in"][e], pair * 32 + 32)
                        pe.wait_ge(S["ol_out"], b + 1)
                        for c in range(CK):
                            for k in range(KBLK + 1):
                                v = cc[e][:, k, c * P:(c + 1) * P] if k < KBLK else cnew[e][:, c * P:(c + 1) * P]
                                mm = pe.matmul(PS[:, 7, c * P:(c + 1) * P], v, pT[:, k, :], start=k == 0, stop=k == KBLK)
                        mm.then_inc(S["ol_psum"], 1)
                    else:
                        pe.wait_ge(IN["vc_in"][e], pair * 16 + 16)
                        pe.wait_ge(S["os_out"], b + 1)
                        for h in range(H):
                            rows = slice((h % 2) * HD, (h % 2 + 1) * HD)
                            cols = slice(h // 2 * STEP, (h // 2 + 1) * STEP)
                            for k in range(KBLK + 1):
                                v = vc[e][:, k, h * HD:(h + 1) * HD] if k < KBLK else vnew[e][:, h * HD:(h + 1) * HD]
                                mm = pe.matmul(PS[rows, 6, cols], v, aT[:, k, h * STEP:(h + 1) * STEP], start=k == 0, stop=k == KBLK)
                        mm.then_inc(S["os_psum"], 1)

            loop(pe, body)
            pe.wait_ge(S["ol_out"], NSEQ + 1)
            pe.wait_ge(S["wuv_in"], 16)
            for h in range(H):
                rows = slice((h % 2) * HD, (h % 2 + 1) * HD)
                for c in range(CK):
                    mm = pe.matmul(PS[rows, 4, h // 2 * P:(h // 2 + 1) * P], wuv[:, c, h * HD:(h + 1) * HD], olatT[:, c, h, :],
                                   start=c == 0, stop=c == CK - 1)
            mm.then_inc(S["om_psum"], 1)

        @block.vector
        def _(dve):
            def copy(dst, src):
                return dve.tensor_copy(dst, src)

            def queries(b):
                for j in range(2):
                    rows = slice(j * HD, (j + 1) * HD)
                    diag = qblk[rows].rearrange("p c (h q) -> p (c h) q", q=STEP)[:, j::H + 2, :]
                    ins = dve.tensor_copy(diag, qT[rows, :, new_cols(b)])
                    if j:
                        ins.then_inc(S["qblk_ready"], 1)
                dve.tensor_copy(qabs[:].rearrange("p c (h q) -> p c h q", q=STEP), qabsT[:, :, :, bass.ds(b * STEP, STEP)]).then_inc(S["q_ready"], 1)
                dve.tensor_copy(qrot[:].rearrange("p (h q) -> p h q", q=STEP), qmT[:, :, new_cols(b)]).then_inc(S["q_ready"], 1)

            dve.sem_inc(turn[1], 1)
            dve.sem_inc(S["os_out"], 1)
            dve.wait_ge(S["zeroed"], 9)
            queries(0)
            evacuate_first(dve, copy, 1)

            def body(pair, e, more):
                b = pair * 2 + e
                dve.wait_ge(S["s_psum"], b + 1)
                dve.tensor_reduce(peak, s, AX_X, ALU.max).then_inc(S["s_peak"], 1)
                dve.wait_ge(S["s_peak"], b + 1)
                dve.tensor_scalar(peak, peak, -MLA_SCALE, None, ALU.mult).then_inc(S["s_bias"], 1)
                if more:
                    queries(b + 1)
                    evacuate(dve, copy, 1, pair, e, range(KV), more)
                dve.wait_ge(S["soft2"], b + 1)
                dve.scalar_tensor_tensor(out=t1[:], in0=z, scalar=0.0, in1=t1[:], op0=ALU.max, op1=ALU.add).then_inc(S["soft"], 1)
                dve.wait_ge(S["p_exp"], b + 1)
                dve.reciprocal(inverse, total).then_inc(S["p_inv"], 1)
                dve.wait_ge(S["p_inv"], b + 1)
                dve.tensor_scalar(pr[:], pr[:], inverse, None, ALU.mult).then_inc(S["p_ready"], 1)
                dve.wait_ge(S["soft_kept"], b + 1)
                dve.tensor_tensor_scan(t2[:, ::-1], C["ones"][:, 0:1].broadcast_to((P, KEYS)), t1[:, ::-1], 0.0, ALU.mult, ALU.add).then_inc(S["tail"], 1)
                dve.wait_ge(S["tail"], b + 1)
                dve.tensor_tensor(t2[:], z, t2[:], ALU.subtract).then_inc(S["logit"], 1)
                evacuate(dve, copy, 1, pair, e, range(KV, PER), more)
                dve.wait_ge(S["os_psum"], b + 1)
                dve.tensor_copy(osT[:, :, new_cols(b)], PS[:, 6, 0:CQ * STEP].rearrange("p (c q) -> p c q", q=STEP)).then_inc(S["os_out"], 1)

            loop(dve, body)
            dve.wait_ge(S["om_psum"], 1)
            dve.tensor_copy(omT[:, :, SEQ:N], PS[:, 4, :].rearrange("p (c n) -> p c n", c=CQ)).then_inc(S["om_out"], 1)


def phase_merge(nc, A, env):
    sb, sem, PS, C, ident = (env[k] for k in ("sb", "sem", "PS", "C", "ident"))
    vecT, adaT, coef, stat, cT, x, hT, osT, omT = (env[k] for k in ("vecT", "adaT", "coef", "stat", "cT", "x", "hT", "osT", "omT"))
    CW = SBW // P
    wout = sb("wout", 66, [P, KD, D])
    WA, RING = 2, 4
    wada = [sb(f"wada_b{i}", 98 + 8 * i, [P, KD, WA * P]) for i in range(RING)]
    NLOAD = (NM - 2 * KD) // WA
    y = sb("y", 159, [P, NT, D])
    xn = [sb(f"xm{i}", 179 + 4 * i, [P, D]) for i in range(2)]
    sq = sb("sq", 187, [P, 2 * CW, N])
    junk = sq[:].rearrange("p c n -> p (c n)")[:, 0:D]
    gmix, gffn = sb("gmix", 10, [P, 2, D]), sb("gffn", 18, [P, 2, D])
    env["env"].update(gffn=gffn)
    gated = sq[:].rearrange("p c n -> p (c n)")[:, D:D + 2 * KD * NC_].rearrange("p (g k c) -> p g k c", g=2, c=NC_)
    at = D + 2 * KD * NC_
    per_query = sq[:].rearrange("p c n -> p (c n)")[:, at:at + 2 * KD * P].rearrange("p (g k n) -> p g k n", g=2, n=P)
    names = ("squared scaled ss_psum g_var g_sqrt g_rstd oa_psum ob_psum ya_ready y_ready y_sq y_var y_sqrt y_rstd ada_psum ada_ready "
             "gated row_psum row_ready mixed x1_ready x_sq x_var x_sqrt x_rstd xn_ready xT_psum h_ready step").split()
    S = {n: sem("mg_" + n) for n in names}
    wada_in = [sem(f"mg_wada_in{i}") for i in range(RING)]
    wout_in = [sem(f"mg_wout_in{k}") for k in range(2)]
    groups = ((osT, "g_sb_out"), (omT, "g_mla_out"))

    with nc.Block() as block:
        @block.sync
        def _(sp):
            for k in range(2):
                sp.dma_start(wout[:, 4 * k:4 * k + 4, :], A["w_out"][0, 4 * k * P:4 * (k + 1) * P].rearrange("(k p) m -> p k m", p=P)
                             ).then_inc(wout_in[k], 16)
            for i in range(NLOAD):
                if i >= RING:
                    sp.wait_ge(S["ada_psum"], i - RING + 1)
                c0 = (2 * KD + i * WA) * P
                sp.dma_start(wada[i % RING][:], A["w_ada"][0].rearrange("(k p) m -> p k m", p=P)[:, :, c0:c0 + WA * P]
                             ).then_inc(wada_in[i % RING], 16)

        @block.gpsimd
        def _(pool):
            pass

        @block.scalar
        def _(act):
            for g, (o, _) in enumerate(groups):
                act.activation(sq[:, g * CW:(g + 1) * CW, :], o[:], ACT.Square).then_inc(S["squared"], 1)
            act.wait_ge(S["g_var"], 1)
            act.activation(stat[:, 0, 0:2 * NT], stat[:, 0, 0:2 * NT], ACT.Sqrt).then_inc(S["g_sqrt"], 1)
            act.wait_ge(S["g_rstd"], 1)
            for t in range(NT):
                act.wait_ge(S["oa_psum"], t + 1)
                act.activation(y[:, t, :].rearrange("p (b n) -> p b n", b=2), PS[:, 0:2, :], ACT.Copy,
                               scale=stat[:, 1, 2 * t:2 * t + 1]).then_inc(S["ya_ready"], 1)
            for t in range(NT):
                act.wait_ge(S["y_ready"], t + 1)
                if t:
                    act.wait_ge(S["y_sq"], t)
                act.activation(junk, y[:, t, :], ACT.Square, accum_out=stat[:, 2, t:t + 1]).then_inc(S["y_sq"], 1)
            act.wait_ge(S["y_var"], 1)
            act.activation(stat[:, 2, 0:NT], stat[:, 2, 0:NT], ACT.Sqrt).then_inc(S["y_sqrt"], 1)
            for i in range(4):
                act.wait_ge(S["row_psum"], i + 1)
                act.activation((gmix, gffn)[i // 2][:, i % 2, :].rearrange("p (b n) -> p b n", b=2),
                               PS[:, 4:6, :] if i % 2 else PS[:, 6:8, :], ACT.Copy).then_inc(S["row_ready"], 1)
            for t in range(NT):
                act.wait_ge(S["x1_ready"], t + 1)
                if t:
                    act.wait_ge(S["x_sq"], t)
                act.activation(junk, x[:, t, :], ACT.Square, accum_out=stat[:, 4, t:t + 1]).then_inc(S["x_sq"], 1)
            act.wait_ge(S["x_var"], 1)
            act.activation(stat[:, 4, 0:NT], stat[:, 4, 0:NT], ACT.Sqrt).then_inc(S["x_sqrt"], 1)
            act.wait_ge(S["x_rstd"], 1)
            for t in range(NT):
                if t >= 2:
                    act.wait_ge(S["xT_psum"], 2 * (t - 1))
                act.activation(xn[t % 2][:], x[:, t, :], ACT.Copy, scale=stat[:, 5, t:t + 1]).then_inc(S["xn_ready"], 1)

        @block.tensor
        def _(pe):
            pe.wait_ge(S["squared"], 2)
            for t in range(NT):
                for g in range(2):
                    for c in range(CW):
                        mm = pe.matmul(PS[:, 4, 2 * t + g:2 * t + g + 1], sq[:, g * CW + c, t * P:(t + 1) * P], C["ones"][:, 0:1],
                                       start=c == 0, stop=c == CW - 1)
            mm.then_inc(S["ss_psum"], 1)
            for t in range(NT):
                for g, (o, _) in enumerate(groups):
                    if t == 0:
                        pe.wait_ge(wout_in[g], 16)
                        pe.wait_ge(S["scaled"], CW * (g + 1))
                    else:
                        pe.wait_ge(S[("ya_ready", "y_ready")[g]], t)
                    for b in range(2):
                        for c in range(CW):
                            mm = pe.matmul(PS[:, 2 * g + b, :], o[:, c, t * P:(t + 1) * P], wout[:, g * CW + c, b * 512:(b + 1) * 512],
                                           start=c == 0, stop=c == CW - 1)
                    mm.then_inc(S[("oa_psum", "ob_psum")[g]], 1)
            pe.wait_ge(S["g_var"], 1)
            for i in range(NLOAD):
                pe.wait_ge(wada_in[i % RING], 16 * (i // RING + 1))
                for j in range(WA):
                    m = i * WA + j
                    for k in range(KD):
                        mm = pe.matmul(PS[:, 4, m * NC_:(m + 1) * NC_], wada[i % RING][:, k, j * P:(j + 1) * P], cT[:, :, k],
                                       start=k == 0, stop=k == KD - 1)
                mm.then_inc(S["ada_psum"], 1)
            pe.wait_ge(S["gated"], 4)
            for i in range(4):
                if i >= 2:
                    pe.wait_ge(S["row_ready"], i - 1)
                for k in range(KD):
                    per_token = gated[:, i // 2, k, 0:1].broadcast_to((P, P)) if i % 2 == 0 else per_query[:, i // 2, k, :]
                    bank = (6 if i % 2 == 0 else 4) + k // 4
                    mm = pe.matmul(PS[:, bank, (k % 4) * P:(k % 4 + 1) * P], per_token, ident, start=True, stop=True)
                mm.then_inc(S["row_psum"], 1)
            for t in range(NT):
                pe.wait_ge(S["xn_ready"], t + 1)
                if t == 0:
                    pe.wait_ge(S["row_ready"], 4)
                for b in range(2):
                    if t >= 2:
                        pe.wait_ge(S["h_ready"], 2 * (t - 2) + b + 1)
                    for j in range(4):
                        k = 4 * b + j
                        mm = pe.transpose(PS[:, 4 + 2 * (t % 2) + b, j * P:(j + 1) * P], xn[t % 2][:, k * P:(k + 1) * P], ident)
                    mm.then_inc(S["xT_psum"], 1)

        @block.vector
        def _(dve):
            step = Step(dve, S["step"])
            dve.wait_ge(S["squared"], 2)
            for o, name in groups:
                for c in range(CW):
                    g = vecT[:, VROW[name] + c:VROW[name] + c + 1]
                    dve.tensor_scalar(o[:, c, :], o[:, c, :], g, None, ALU.mult).then_inc(S["scaled"], 1)
            dve.wait_ge(S["ss_psum"], 1)
            dve.tensor_scalar(stat[:, 0, 0:2 * NT], PS[:, 4, 0:2 * NT], 1.0 / SBW, EPS, ALU.mult, ALU.add).then_inc(S["g_var"], 1)
            dve.wait_ge(S["g_sqrt"], 1)
            dve.reciprocal(stat[:, 1, 0:2 * NT], stat[:, 0, 0:2 * NT]).then_inc(S["g_rstd"], 1)
            dve.wait_ge(S["g_rstd"], 1)
            for t in range(NT):
                dve.wait_ge(S["ob_psum"], t + 1)
                dve.wait_ge(S["ya_ready"], t + 1)
                v = y[:, t, :].rearrange("p (b n) -> p b n", b=2)
                dve.scalar_tensor_tensor(out=v, in0=PS[:, 2:4, :], scalar=stat[:, 1, 2 * t + 1:2 * t + 2], in1=v,
                                         op0=ALU.mult, op1=ALU.add).then_inc(S["y_ready"], 1)
            dve.wait_ge(S["y_sq"], NT)
            dve.tensor_scalar(stat[:, 2, 0:NT], stat[:, 2, 0:NT], 1.0 / D, EPS, ALU.mult, ALU.add).then_inc(S["y_var"], 1)
            dve.wait_ge(S["y_sqrt"], 1)
            dve.reciprocal(stat[:, 3, 0:NT], stat[:, 2, 0:NT]).then_inc(S["y_rstd"], 1)
            m = NM - 2 * KD
            dve.wait_ge(S["ada_psum"], NLOAD)
            dve.tensor_tensor(adaT[:, 2 * KD:NM, :], PS[:, 4, 0:m * NC_].rearrange("p (m c) -> p m c", c=NC_),
                              vecT[:, 2 * KD:NM].unsqueeze(2).broadcast_to((P, m, NC_)), ALU.add).then_inc(S["ada_ready"], 1)
            dve.wait_ge(S["ada_ready"], 1)
            for i, (row, name) in enumerate(((GT1, "g_mix_post"), (GT2, "g_ffn_post"))):
                gain = vecT[:, VROW[name]:VROW[name] + KD].unsqueeze(2).broadcast_to((P, KD, NC_))
                dve.tensor_tensor(gated[:, i], adaT[:, row:row + KD, :], gain, ALU.mult).then_inc(S["gated"], 1)
            dve.wait_ge(S["gated"], 2)
            for i in range(2):
                dve.tensor_copy(per_query[:, i].rearrange("p k (s q) -> p k s q", q=STEP),
                                gated[:, i, :, 1:NC_].unsqueeze(3).broadcast_to((P, KD, NSEQ, STEP))).then_inc(S["gated"], 1)
            step(dve.tensor_scalar(coef[:, 1], adaT[:, SC2:SC2 + KD, :], 1.0, None, ALU.add))
            step.wait()
            g = VROW["g_ffn_pre"]
            step(dve.tensor_tensor(coef[:, 1], coef[:, 1], vecT[:, g:g + KD].unsqueeze(2).broadcast_to((P, KD, NC_)), ALU.mult))
            dve.wait_ge(S["y_rstd"], 1)
            for t in range(NT):
                dve.wait_ge(S["row_ready"], 1 if t < PT else 2)
                dve.scalar_tensor_tensor(out=y[:, t, :], in0=y[:, t, :], scalar=stat[:, 3, t:t + 1], in1=gmix[:, int(t >= PT), :],
                                         op0=ALU.mult, op1=ALU.mult).then_inc(S["mixed"], 1)
                dve.wait_ge(S["mixed"], t + 1)
                dve.tensor_tensor(x[:, t, :], x[:, t, :], y[:, t, :], ALU.add).then_inc(S["x1_ready"], 1)
            dve.wait_ge(S["x_sq"], NT)
            dve.tensor_scalar(stat[:, 4, 0:NT], stat[:, 4, 0:NT], 1.0 / D, EPS, ALU.mult, ALU.add).then_inc(S["x_var"], 1)
            dve.wait_ge(S["x_sqrt"], 1)
            dve.reciprocal(stat[:, 5, 0:NT], stat[:, 4, 0:NT]).then_inc(S["x_rstd"], 1)
            for t in range(NT):
                for b in range(2):
                    dve.wait_ge(S["xT_psum"], 2 * t + b + 1)
                    modulate(dve, step, hT, PS[:, 4 + 2 * (t % 2) + b, :], coef[:, 1], adaT[:, SH2:SH2 + KD, :], t, b, S["h_ready"])


def phase_keys(nc, A, env):
    sb, sem, PS, C, ident = (env[k] for k in ("sb", "sem", "PS", "C", "ident"))
    hT = env["hT"]
    wq = sb("wq", 66, [P, KD, NQ * P])
    PAIR = 2 * P
    qp = [sb(f"qp{i}", 130 + 16 * i, [P, NQ, PAIR]) for i in range(2)]
    sc = [sb(f"sc{i}", 162 + 8 * i, [P, NQ, NKEYS]) for i in range(2)]
    cand = sb("cand", 178, [P, H, TOPK, TOPK])
    skey = sb("skey", 186, [P, 2, P])
    rest = sb("rest", 187, [P, NQ * NKEYS])
    hot = sb("hot", 187, [P, H, TOPK, TOPK])
    pick = sb("pick", 195, [P, NT, 3, H * TOPK])
    top = sb("top", 203, [P, NQ, TOPK])
    topi = sb("topi", 204, [P, NQ, TOPK], U32)
    topf = sb("topf", 205, [P, NQ, TOPK])
    best = sb("best", 206, [P, H, TOPK])
    besti = sb("besti", 206.5, [P, 2, H, TOPK], U32)
    sel = sb("sel", 10, [P, 3, N])
    bestf = sb("bestf", 17.5, [P, H, TOPK])
    flat_stat = env["stat"][:].rearrange("p a b -> p (a b)")
    total, peak = flat_stat[:, 0:NT * H], flat_stat[:, 64:64 + H]
    env["env"].update(sel=sel)
    names = "sk_psum sk_ready q_psum q_ready s_psum s_ready topped ranked gate_exp gates sel_psum sel_ready0 sel_ready1 step".split()
    S = {n: sem("pk_" + n) for n in names}
    sk_in, wq_in = sem("pk_sk_in"), [sem(f"pk_wq_in{k}") for k in range(KD)]
    PAIRS = [(0, PAIR), (PAIR, PAIR), (2 * PAIR, N - 2 * PAIR)]

    with nc.Block() as block:
        @block.sync
        def _(sp):
            for k in range(KD):
                sp.dma_start(wq[:, k, :], A["w_peer_q"][0, k * P:(k + 1) * P, :]).then_inc(wq_in[k], 16)

        @block.scalar
        def _(act):
            act.dma_start(skey[:, 0, :], A["sub_keys_1"][0]).then_inc(sk_in, 16)
            act.dma_start(skey[:, 1, :], A["sub_keys_2"][0]).then_inc(sk_in, 16)
            act.wait_ge(S["sk_psum"], 1)
            act.activation(skey[:].rearrange("p i n -> p (i n)"), PS[:, 7, 0:2 * P], ACT.Copy).then_inc(S["sk_ready"], 1)
            for n, (t0, w) in enumerate(PAIRS):
                for m in range(NQ):
                    act.wait_ge(S["q_psum"], n * NQ + m + 1)
                    if n >= 2:
                        act.wait_ge(S["s_psum"], 4 * 2 * (n - 1))
                    act.activation(qp[n % 2][:, m, 0:w], PS[:, m % 2, 0:w], ACT.Copy).then_inc(S["q_ready"], 1)
                for t in range(t0 // P, (t0 + w) // P):
                    if t >= 2:
                        act.wait_ge(S["topped"], t - 1)
                    for g in range(4):
                        act.wait_ge(S["s_psum"], 4 * t + g + 1)
                        act.activation(sc[t % 2][:, 4 * g:4 * g + 4, :], PS[:, 2 + g, :].rearrange("p (m e) -> p m e", e=NKEYS),
                                       ACT.Copy).then_inc(S["s_ready"], 1)
            act.wait_ge(S["ranked"], NT)
            act.activation(pick[:, :, 2, :], pick[:, :, 2, :], ACT.Exp).then_inc(S["gate_exp"], 1)
            for t in range(1, NT, 2):
                act.wait_ge(S["sel_psum"], t + 1)
                act.activation(sel[:, :, t * P:(t + 1) * P], PS[:, 7, 0:3 * P].rearrange("p (i n) -> p i n", i=3), ACT.Copy
                               ).then_inc(S["sel_ready1"], 1)

        @block.tensor
        def _(pe):
            pe.wait_ge(sk_in, 32)
            for i in range(2):
                mm = pe.transpose(PS[:, 7, i * P:(i + 1) * P], skey[:, i, :], ident)
            mm.then_inc(S["sk_psum"], 1)
            for k in range(KD):
                pe.wait_ge(wq_in[k], 16)
            for n, (t0, w) in enumerate(PAIRS):
                for m in range(NQ):
                    i = n * NQ + m
                    if i >= 2:
                        pe.wait_ge(S["q_ready"], i - 1)
                    for k in range(KD):
                        mm = pe.matmul(PS[:, m % 2, 0:w], wq[:, k, m * P:(m + 1) * P], hT[:, k, t0:t0 + w], start=k == 0, stop=k == KD - 1)
                    mm.then_inc(S["q_psum"], 1)
                pe.wait_ge(S["q_ready"], (n + 1) * NQ)
                for t in range(t0 // P, (t0 + w) // P):
                    for g in range(4):
                        if t:
                            pe.wait_ge(S["s_ready"], 4 * (t - 1) + g + 1)
                        elif g == 0:
                            pe.wait_ge(S["sk_ready"], 1)
                        for j in range(4):
                            m = 4 * g + j
                            mm = pe.matmul(PS[:, 2 + g, j * P:(j + 1) * P], qp[n % 2][:, m, t * P - t0:(t + 1) * P - t0], skey[:, m % 2, :],
                                           start=True, stop=True)
                        mm.then_inc(S["s_psum"], 1)
            pe.wait_ge(S["gates"], 1)
            for t in range(NT):
                if t >= 2:
                    pe.wait_ge(S[f"sel_ready{t % 2}"], t // 2)
                for i in range(3):
                    mm = pe.transpose(PS[:, 6 + t % 2, i * P:(i + 1) * P], pick[:, t, i, :], ident)
                mm.then_inc(S["sel_psum"], 1)

        @block.vector
        def _(dve):
            step = Step(dve, S["step"])

            def sync(ins):
                step(ins)
                step.wait()

            def top16(values, width, out, index, count):
                spare = rest[:, 0:count * width].rearrange("p (m e) -> p m e", m=count)
                for m in range(count):
                    step(dve.max(out[:, m, 0:8], values[:, m, :]))
                step.wait()
                for m in range(count):
                    step(dve.max_index(index[:, m, 0:8], out[:, m, 0:8], values[:, m, :]))
                    step(dve.match_replace(spare[:, m, :], out[:, m, 0:8], values[:, m, :], NEG))
                step.wait()
                for m in range(count):
                    step(dve.max(out[:, m, 8:16], spare[:, m, :]))
                step.wait()
                for m in range(count):
                    ins = dve.max_index(index[:, m, 8:16], out[:, m, 8:16], spare[:, m, :])
                return ins

            for t in range(NT):
                dve.wait_ge(S["s_ready"], 4 * (t + 1))
                top16(sc[t % 2], NKEYS, top, topi, NQ).then_inc(S["topped"], 1)
                dve.wait_ge(S["topped"], t + 1)
                step(dve.tensor_copy(topf[:], topi[:]))
                pairs = top[:].rearrange("p (h i) k -> p h i k", i=2)
                sync(dve.tensor_tensor(cand[:], pairs[:, :, 0, :].unsqueeze(3).broadcast_to((P, H, TOPK, TOPK)),
                                       pairs[:, :, 1, :].unsqueeze(2).broadcast_to((P, H, TOPK, TOPK)), ALU.add))
                sync(top16(cand[:].rearrange("p h a b -> p h (a b)"), TOPK * TOPK, best, besti[:, 0], H))
                step(dve.tensor_copy(peak, best[:, :, 0]))
                sync(dve.tensor_scalar(besti[:, 1], besti[:, 0], TOPK - 1, None, ALU.bitwise_and))
                dve.tensor_tensor(pick[:, t, 2, :].rearrange("p (h k) -> p h k", h=H), best[:], peak.unsqueeze(2).broadcast_to((P, H, TOPK)),
                                  ALU.subtract).then_inc(S["ranked"], 1)
                sync(dve.tensor_scalar(besti[:, 0], besti[:, 0], 4, None, ALU.logical_shift_right))
                keys = topf[:].rearrange("p (h i) k -> p h i k", i=2)
                for i in range(2):
                    sync(dve.tensor_copy(bestf[:], besti[:, i]))
                    sync(dve.tensor_tensor(hot[:].rearrange("p h k m -> p (h k) m"),
                                           bestf[:].rearrange("p h k -> p (h k)").unsqueeze(2).broadcast_to((P, H * TOPK, TOPK)),
                                           C["slot"].unsqueeze(1).broadcast_to((P, H * TOPK, TOPK)), ALU.is_equal))
                    sync(dve.tensor_tensor(hot[:], hot[:], keys[:, :, i, :].unsqueeze(2).broadcast_to((P, H, TOPK, TOPK)), ALU.mult))
                    sync(dve.tensor_reduce(pick[:, t, i, :].rearrange("p (h k) -> p h k", h=H), hot[:], AX_X, ALU.add))
            dve.wait_ge(S["gate_exp"], 1)
            gate = pick[:, :, 2, :].rearrange("p t (h k) -> p t h k", h=H)
            totals = total.rearrange("p (t h) -> p t h", h=H)
            sync(dve.tensor_reduce(totals, gate, AX_X, ALU.add))
            sync(dve.reciprocal(total, total))
            dve.tensor_tensor(gate, gate, totals.unsqueeze(3).broadcast_to((P, NT, H, TOPK)), ALU.mult).then_inc(S["gates"], 1)
            for t in range(0, NT, 2):
                dve.wait_ge(S["sel_psum"], t + 1)
                dve.tensor_copy(sel[:, :, t * P:(t + 1) * P], PS[:, 6, 0:3 * P].rearrange("p (i n) -> p i n", i=3)).then_inc(S["sel_ready0"], 1)


TB = 64


def phase_gates(nc, A, env):
    sb, sem, PS, C, sel = (env[k] for k in ("sb", "sem", "PS", "C", "sel"))
    stage = [sb(f"stage{i}", 74 + 32 * i, [P, NKEYS, TB]) for i in range(2)]
    G = 4
    first = [sb(f"first{i}", 138 + 2 * i, [P, G, NKEYS]) for i in range(G)]
    second = [sb(f"second{i}", 146 + 2 * i, [P, G, NKEYS]) for i in range(G)]
    hot_ready, hot_used, table_psum, table_ready = (sem("gt_" + n) for n in ("hot_ready", "hot_used", "table_psum", "table_ready"))
    stored = [sem(f"gt_stored{i}") for i in range(2)]
    BLOCKS, INNER = N // TB, TB // (G * G)
    PB = INNER * G

    def loop(eng, body, edge=None):
        with eng.Fori(0, BLOCKS // 2) as pair:
            for e in range(2):
                if edge:
                    edge(pair, e)
                with eng.Fori(0, INNER) as i:
                    for g in range(G):
                        body(pair * (2 * PB) + i * G + (e * PB + g), g, e, i * (G * G) + g * G, pair * (2 * TB) + i * (G * G) + (e * TB + g * G))

    with nc.Block() as block:
        @block.sync
        def _(sp):
            with sp.Fori(0, BLOCKS // 2) as pair:
                for e in range(2):
                    sp.wait_ge(table_ready, pair * (2 * PB) + (e + 1) * PB + G)
                    sp.dma_start(A["gates"][pair * 2 + e], stage[e][:]).then_inc(stored[e], 16)
            for e in range(2):
                sp.wait_ge(stored[e], 16 * (BLOCKS // 2 + 1))

        @block.vector
        def _(dve):
            def body(n, g, e, at, token):
                dve.wait_ge(hot_used, n + 1)
                for j in range(G):
                    col = bass.ds(token + j, 1)
                    dve.tensor_scalar(first[g][:, j, :], C["iota"], sel[:, 0, col], sel[:, 2, col], ALU.is_equal, ALU.mult)
                    ins = dve.tensor_scalar(second[g][:, j, :], C["iota"], sel[:, 1, col], None, ALU.is_equal)
                ins.then_inc(hot_ready, 1)

            loop(dve, body)

        @block.tensor
        def _(pe):
            pe.sem_inc(hot_used, G)

            def body(n, g, e, at, token):
                pe.wait_ge(hot_ready, n + 1)
                pe.wait_ge(table_ready, n + 1)
                for j in range(G):
                    mm = pe.matmul(PS[:, g, j * NKEYS:(j + 1) * NKEYS], second[g][:, j, :], first[g][:, j, :], start=True, stop=True)
                mm.then_inc(hot_used, 1)

            loop(pe, body)

        @block.scalar
        def _(act):
            act.sem_inc(table_ready, G)
            for e in range(2):
                act.sem_inc(stored[e], 16)

            def edge(pair, e):
                act.wait_ge(stored[e], pair * 16 + 16)

            def body(n, g, e, at, token):
                act.wait_ge(hot_used, n + G + 1)
                act.activation(stage[e][:, :, bass.ds(at, G)].rearrange("p i n -> p n i"), PS[:, g, :].rearrange("p (n i) -> p n i", n=G),
                               ACT.Copy).then_inc(table_ready, 1)

            loop(act, body, edge)


def phase_experts(nc, A, env):
    sb, sem, PS, C, ident = (env[k] for k in ("sb", "sem", "PS", "C", "ident"))
    x, hT, gffn, stat = (env[k] for k in ("x", "hT", "gffn", "stat"))
    GC = 2
    NCH = NEXP // P
    NG = NCH // GC
    PAIR = 2 * GC
    NPAIR = NCH // PAIR
    BLK = N // TB
    UR = PAIR
    HI, LO = 0, 1
    uT = [[sb(f"uT_{'hl'[s]}{i}", (10, 122)[s] + 4 * i, [P, KD, P], F32R) for s in (HI, LO)] for i in range(2)]
    acc = sb("acc", 66, [P, NT, D])
    h = [sb("h_hi", 86, [P, KD, N], F32R), sb("h_lo", 46, [P, KD, N], F32R)]
    u = [sb(f"u{i}", 106 + 4 * i, [P, D]) for i in range(UR)]
    v = [[sb(f"v_{'hl'[s]}{i}", 130 + 16 * s + 8 * i, [P, GC, D], F32R) for s in (HI, LO)] for i in range(2)]
    a = [[sb(f"a_{'hl'[s]}{i}", 162 + 10 * s + 5 * i, [P, GC, N], F32R) for s in (HI, LO)] for i in range(2)]
    gt = [sb(f"gt{i}", 182 + 5 * i, [P, BLK, GC, TB]) for i in range(2)]
    gl = [sb(f"gl{i}", 192 + 2.5 * i, [P, 2, HALF]) for i in range(2)]
    vraw = [sb(f"vraw{i}", 197 + 4 * i, [P, D]) for i in range(2)]
    y = [sb(f"yo{i}", 106 + 4 * i, [P, D]) for i in range(2)]
    junk = sb("ej", 114, [P, D])
    names = ("zeroed h_hi h_lo uT_psum uT_hi uT_lo s_psum gelu weighed a_hi a_lo v_hi v_lo f_psum added f_sq f_var f_sqrt f_rstd scaled "
             "y_ready").split()
    S = {n: sem("ex_" + n) for n in names}
    u_in = [sem(f"ex_u_in{i}") for i in range(UR)]
    v_in, g_in = ([sem(f"ex_{n}_in{i}") for i in range(2)] for n in "vg")
    y_out = [sem(f"ex_y_out{i}") for i in range(2)]
    ADDS = 2 * NT
    y_dram = [A["y_p"][0, t * P:(t + 1) * P, :] for t in range(PT)] + [A["y_s"].rearrange("b q d -> (b q) d")]

    def pairs(eng, body):
        body(0, True, False)
        with eng.Fori(1, NPAIR - 1) as i:
            body(i, False, False)
        body(NPAIR - 1, False, True)

    with nc.Block() as block:
        @block.sync
        def _(sp):
            def body(i, first, last):
                for q in range(PAIR):
                    e, c = divmod(q, GC)
                    if not first:
                        sp.wait_ge(S["uT_psum"], i * (2 * PAIR) + 2 * (q + 1 - UR))
                    sp.dma_start(u[q][:], A["u_experts"][0, bass.ds(i * (PAIR * P) + q * P, P), :]).then_inc(u_in[q], 16)
                    if c == 0:
                        if not first:
                            sp.wait_ge(S["weighed"], i * PAIR + (e - 1) * GC)
                        sp.dma_start(gt[e][:], A["gates"][:, :, bass.ds(i * PAIR + e * GC, GC), :].rearrange("b p c n -> p b c n")
                                     ).then_inc(g_in[e], 16)
                    if not (first and q < 2):
                        sp.wait_ge(S["v_lo"], i * PAIR + q - 1)
                    sp.dma_start(vraw[q % 2][:], A["v_experts"][0, bass.ds(i * (PAIR * P) + q * P, P), :]).then_inc(v_in[q % 2], 16)

            pairs(sp, body)
            for t in range(NT):
                sp.wait_ge(S["y_ready"], t + 1)
                sp.dma_start(y_dram[t], y[t % 2][:]).then_inc(y_out[t % 2], 16)
            sp.wait_ge(y_out[0], 16 * 3)
            sp.wait_ge(y_out[1], 16 * 2)

        @block.gpsimd
        def _(pool):
            def body(i, first, last):
                for q in range(PAIR):
                    e, c = divmod(q, GC)
                    pool.wait_ge(S["gelu"], i * PAIR + q + 1)
                    if c == 0:
                        pool.wait_ge(g_in[e], i * 16 + 16)
                    act_by_block = gl[q % 2][:].rearrange("p s n -> p (s n)").rearrange("p (b n) -> p b n", n=TB)
                    pool.tensor_tensor(act_by_block, act_by_block, gt[e][:, :, c, :], ALU.mult).then_inc(S["weighed"], 1)

            pairs(pool, body)

        @block.scalar
        def _(act):
            def turned(i, q):
                for b in range(2):
                    act.wait_ge(S["uT_psum"], i * (2 * PAIR) + 2 * q + b + 1)
                    act.activation(uT[q % 2][HI][:, 4 * b:4 * b + 4, :], PS[:, b, :].rearrange("p (k n) -> p k n", k=4), ACT.Copy
                                   ).then_inc(S["uT_hi"], 1)

            def body(i, first, last):
                if first:
                    turned(0, 0)
                for q in range(PAIR):
                    e, c = divmod(q, GC)
                    if not (last and q == PAIR - 1):
                        turned(i, q + 1)
                    act.wait_ge(v_in[q % 2], i * (16 * PAIR // 2) + 16 * (q // 2 + 1))
                    if c == 0 and not first:
                        act.wait_ge(S["f_psum"], i * (2 * ADDS) + (e - 1) * ADDS)
                    act.activation(v[e][HI][:, c, :], vraw[q % 2][:], ACT.Copy).then_inc(S["v_hi"], 1)
                    act.wait_ge(S["s_psum"], i * PAIR + q + 1)
                    if not (first and q < 2):
                        act.wait_ge(S["a_lo"], i * PAIR + q - 1)
                    act.activation(gl[q % 2][:], PS[:, 2 + 2 * (q % 2):4 + 2 * (q % 2), 0:HALF], ACT.Gelu).then_inc(S["gelu"], 1)
                    act.wait_ge(S["weighed"], i * PAIR + q + 1)
                    act.activation(a[e][HI][:, c, :], gl[q % 2][:].rearrange("p s n -> p (s n)"), ACT.Copy).then_inc(S["a_hi"], 1)

            act.activation(h[HI][:, KD // 2:KD, :], hT[:, KD // 2:KD, :], ACT.Copy).then_inc(S["h_hi"], 1)
            pairs(act, body)
            act.wait_ge(S["added"], NG * ADDS)
            for t in range(NT):
                if t:
                    act.wait_ge(S["f_sq"], t)
                act.activation(junk[:], acc[:, t, :], ACT.Square, accum_out=stat[:, 0, t:t + 1]).then_inc(S["f_sq"], 1)
            act.wait_ge(S["f_var"], 1)
            act.activation(stat[:, 0, 0:NT], stat[:, 0, 0:NT], ACT.Sqrt).then_inc(S["f_sqrt"], 1)

        @block.tensor
        def _(pe):
            PASSES = ((HI, HI), (HI, LO), (LO, HI))

            def turn(i, q, first_of_all=False):
                pe.wait_ge(u_in[q % UR], i * 16 + 16 * (q // UR + 1))
                for b in range(2):
                    if not first_of_all:
                        pe.wait_ge(S["uT_lo"], i * (2 * PAIR) + 2 * q - 1 + b)
                    for j in range(4):
                        k = 4 * b + j
                        mm = pe.transpose(PS[:, b, j * P:(j + 1) * P], u[q % UR][:, k * P:(k + 1) * P], ident)
                    mm.then_inc(S["uT_psum"], 1)

            def hidden(i, q, fresh):
                if not fresh:
                    pe.wait_ge(S["gelu"], i * PAIR + q - 1)
                for b in range(2):
                    for k in range(KD):
                        if b == 0 and k % (KD // 2) == 0:
                            pe.wait_ge(S["uT_lo"], i * (2 * PAIR) + 2 * q + 1 + k // (KD // 2))
                        for w, m in PASSES:
                            mm = pe.matmul(PS[:, 2 + 2 * (q % 2) + b, 0:HALF], uT[q % 2][w][:, k, :], h[m][:, k, b * HALF:(b + 1) * HALF],
                                           start=k == 0 and (w, m) == PASSES[0], stop=k == KD - 1 and (w, m) == PASSES[-1])
                mm.then_inc(S["s_psum"], 1)

            def outputs(i, e, before, fresh):
                pe.wait_ge(S["v_lo"], i * PAIR + (e + 1) * GC)
                pe.wait_ge(S["a_lo"], i * PAIR + (e + 1) * GC)
                for n in range(ADDS):
                    t, b = divmod(n, 2)
                    if not (fresh and n < 2):
                        pe.wait_ge(S["added"], before + (n - 1))
                    for c in range(GC):
                        for w, m in PASSES:
                            mm = pe.matmul(PS[:, 6 + b, :], a[e][w][:, c, t * P:(t + 1) * P], v[e][m][:, c, b * 512:(b + 1) * 512],
                                           start=c == 0 and (w, m) == PASSES[0], stop=c == GC - 1 and (w, m) == PASSES[-1])
                    mm.then_inc(S["f_psum"], 1)

            def body(i, first, last):
                if first:
                    turn(0, 0, True)
                for q in range(PAIR):
                    if not (last and q == PAIR - 1):
                        turn(i, q + 1)
                    hidden(i, q, first and q < 2)
                    if q == GC - 1 and not first:
                        outputs(i - 1, 1, i * (2 * ADDS) - ADDS, False)
                    if q == PAIR - 1:
                        outputs(i, 0, i * (2 * ADDS), first)
                if last:
                    outputs(i, 1, i * (2 * ADDS) + ADDS, False)

            pe.wait_ge(S["h_lo"], 2)
            pairs(pe, body)

        @block.vector
        def _(dve):
            def turned(i, q):
                for b in range(2):
                    dve.wait_ge(S["uT_hi"], i * (2 * PAIR) + 2 * q + b + 1)
                    dve.tensor_tensor(uT[q % 2][LO][:, 4 * b:4 * b + 4, :], PS[:, b, :].rearrange("p (k n) -> p k n", k=4),
                                      uT[q % 2][HI][:, 4 * b:4 * b + 4, :], ALU.subtract).then_inc(S["uT_lo"], 1)

            def add(before):
                for n in range(ADDS):
                    t, b = divmod(n, 2)
                    dve.wait_ge(S["f_psum"], before + (n + 1))
                    dst = acc[:, t, b * 512:(b + 1) * 512]
                    dve.tensor_tensor(dst, PS[:, 6 + b, :], dst, ALU.add).then_inc(S["added"], 1)

            def body(i, first, last):
                if first:
                    turned(0, 0)
                for q in range(PAIR):
                    e, c = divmod(q, GC)
                    if not (last and q == PAIR - 1):
                        turned(i, q + 1)
                    dve.wait_ge(S["v_hi"], i * PAIR + q + 1)
                    dve.tensor_tensor(v[e][LO][:, c, :], vraw[q % 2][:], v[e][HI][:, c, :], ALU.subtract).then_inc(S["v_lo"], 1)
                    if q == GC - 1 and not first:
                        add(i * (2 * ADDS) - ADDS)
                    if q == PAIR - 1:
                        add(i * (2 * ADDS))
                    dve.wait_ge(S["a_hi"], i * PAIR + q + 1)
                    dve.tensor_tensor(a[e][LO][:, c, :], gl[q % 2][:].rearrange("p s n -> p (s n)"), a[e][HI][:, c, :], ALU.subtract
                                      ).then_inc(S["a_lo"], 1)
                if last:
                    add(i * (2 * ADDS) + ADDS)

            dve.tensor_copy(h[HI][:, 0:KD // 2, :], hT[:, 0:KD // 2, :]).then_inc(S["h_hi"], 1)
            dve.wait_ge(S["h_hi"], 2)
            for b in range(2):
                rows = slice(b * KD // 2, (b + 1) * KD // 2)
                dve.tensor_tensor(h[LO][:, rows, :], hT[:, rows, :], h[HI][:, rows, :], ALU.subtract).then_inc(S["h_lo"], 1)
            dve.memset(acc[:], 0.0).then_inc(S["zeroed"], 1)
            dve.wait_ge(S["zeroed"], 1)
            pairs(dve, body)
            dve.wait_ge(S["f_sq"], NT)
            dve.tensor_scalar(stat[:, 0, 0:NT], stat[:, 0, 0:NT], 1.0 / D, EPS, ALU.mult, ALU.add).then_inc(S["f_var"], 1)
            dve.wait_ge(S["f_sqrt"], 1)
            dve.reciprocal(stat[:, 1, 0:NT], stat[:, 0, 0:NT]).then_inc(S["f_rstd"], 1)
            dve.wait_ge(S["f_rstd"], 1)
            for t in range(NT):
                if t >= 2:
                    dve.wait_ge(y_out[t % 2], 16 * (t // 2))
                dve.scalar_tensor_tensor(out=y[t % 2][:], in0=acc[:, t, :], scalar=stat[:, 1, t:t + 1], in1=gffn[:, int(t >= PT), :],
                                         op0=ALU.mult, op1=ALU.mult).then_inc(S["scaled"], 1)
                dve.wait_ge(S["scaled"], t + 1)
                dve.tensor_tensor(y[t % 2][:], y[t % 2][:], x[:, t, :], ALU.add).then_inc(S["y_ready"], 1)


_INS = ["x_prompt", "x_sample", "c_prompt", "c_sample", "cache_sb_k", "cache_sb_v", "cache_mla_ckv", "cache_mla_krope",
        "w_ada", "b_ada", "g_mix_pre", "g_mix_post", "g_ffn_pre", "g_ffn_post", "w_in", "g_q_lat", "g_kv_lat", "w_uq",
        "w_uk", "w_uv", "g_sb_out", "g_mla_out", "w_out", "w_peer_q", "sub_keys_1", "sub_keys_2", "u_experts", "v_experts"]
_OUTS = [("y_p", (1, SEQ, D)), ("y_s", (NSEQ, STEP, D)),
         ("sbk_p", (1, 1, SEQ, H, HD)), ("sbv_p", (1, 1, SEQ, H, HD)), ("ckv_p", (1, 1, SEQ, KVR)), ("kr_p", (1, 1, SEQ, ROPE)),
         ("sbk_s", (1, NSEQ, STEP, H, HD)), ("sbv_s", (1, NSEQ, STEP, H, HD)), ("ckv_s", (1, NSEQ, STEP, KVR)),
         ("kr_s", (1, NSEQ, STEP, ROPE))]


def declare(nc, arrays):
    dram = {}
    for name in _INS + ["table"]:
        a = arrays[name]
        dram[name] = nc.dram_tensor(f"in_{name}", a.shape, mybir.dt.from_np(a.dtype), kind="ExternalInput").ap()
    for name, shape in _OUTS:
        dram[name] = nc.dram_tensor(f"out_{name}", shape, F32, kind="ExternalOutput").ap()
    dram["gates"] = nc.dram_tensor("gates", (N // 64, NKEYS, NKEYS, 64), F32).ap()
    return dram


def kernel(**inputs):
    import numpy as _np
    import concourse.bacc as _bacc
    from concourse.bass_utils import run_bass_kernel_spmd as _run

    nc = _bacc.Bacc("TRN2", target_bir_lowering=False, num_devices=1)
    arrays = {name: _np.ascontiguousarray(inputs[name]) for name in _INS}
    arrays["table"] = constant_table()
    build(nc, declare(nc, arrays))
    r = _run(nc, [{f"in_{k}": v for k, v in arrays.items()}], core_ids=[0])
    return tuple(r.results[0][f"out_{name}"] for name, _ in _OUTS)
```

```python
import math
from contextlib import ExitStack

import numpy as np

import concourse.bass as bass
from concourse import mybir

F32 = mybir.dt.float32
U32 = mybir.dt.uint32
F32R = mybir.dt.float32r
ALU = mybir.AluOpType
ACT = mybir.ActivationFunctionType
AX_X = mybir.AxisListType.X

P = 128
D = 1024
KD = D // P
SEQ = 512
NSEQ = 8
STEP = 16
PAST = 512
KEYS = PAST + STEP
N = SEQ + NSEQ * STEP
NT = N // P
PT = SEQ // P
HALF = N // 2
CHUNK = 64
H = 8
HD = 64
SBW = H * HD
QR = 384
KVR = 256
ROPE = 32
RH = ROPE // 2
QK = HD + ROPE
LAT = QR + KVR + ROPE
INW = 3 * SBW + LAT
NKEYS = 128
TOPK = 16
NEXP = NKEYS * NKEYS
NQ = 2 * H
EPS = 1e-6
NEG = -1e30
MLA_SCALE = float(QK) ** -0.5
SB_SCALE = float(HD) ** -0.5
NC_ = 1 + NSEQ
WIDE = 96
COPIES = WIDE // NC_ + 1
NM = 6 * KD
SH1, SC1, GT1, SH2, SC2, GT2 = (KD * i for i in range(6))

VECTORS = [("b_ada", NM), ("g_mix_pre", KD), ("g_mix_post", KD), ("g_ffn_pre", KD), ("g_ffn_post", KD),
           ("g_q_lat", QR // P), ("g_kv_lat", KVR // P), ("g_sb_out", SBW // P), ("g_mla_out", SBW // P)]
VROW, _at = {}, 0
for _name, _n in VECTORS:
    VROW[_name] = _at
    _at += _n
NV = _at

CONSTS = [("ident", P), ("iota", P), ("keep", P), ("drop", P), ("ones", 8), ("cos", NT * RH), ("sin", NT * RH),
          ("new_keep", STEP), ("new_drop", STEP), ("slot", TOPK), ("chunk_row", P), ("chunk_col", P)]
CCOL, _at = {}, 0
for _name, _n in CONSTS:
    CCOL[_name] = (_at, _n)
    _at += _n
NCONST = _at


def constant_table():
    t = np.zeros((P, NCONST), np.float32)

    def put(name, a):
        at, n = CCOL[name]
        t[:, at:at + n] = np.asarray(a, np.float32).reshape(-1, n)

    row, col = np.arange(P)[:, None], np.arange(P)[None, :]
    put("ident", row == col)
    put("iota", np.broadcast_to(col, (P, P)))
    put("keep", col < row)
    put("drop", np.where(col < row, 0.0, NEG))
    put("ones", np.ones((P, 8)))
    pos = np.concatenate([np.arange(SEQ), PAST + np.tile(np.arange(STEP), NSEQ)]).astype(np.float32)
    inv = (np.float32(10000.0) ** (-np.arange(RH, dtype=np.float32) / np.float32(RH))).astype(np.float32)
    angle = (pos[:, None] * inv[None, :]).astype(np.float32).astype(np.float64).reshape(NT, P, RH).transpose(1, 0, 2)
    put("cos", np.cos(angle).reshape(P, NT * RH))
    put("sin", np.sin(angle).reshape(P, NT * RH))
    query, key = (np.arange(P) % STEP)[:, None], np.arange(STEP)[None, :]
    put("new_keep", key < query)
    put("new_drop", np.where(key < query, 0.0, NEG))
    put("slot", np.broadcast_to(np.arange(TOPK), (P, TOPK)))
    put("chunk_row", (row == 0) & (col < CHUNK))
    put("chunk_col", np.where((row == 0) & (col >= CHUNK), NEG, 0.0))
    return t


class Step:

    def __init__(self, eng, sem, at=0):
        self.eng, self.sem, self.n = eng, sem, at

    def __call__(self, ins):
        ins.then_inc(self.sem, 1)
        self.n += 1
        return self.n

    def wait(self, n=None):
        self.eng.wait_ge(self.sem, self.n if n is None else n)


def build(nc, A, upto=99, dbg=None):
    ctx = ExitStack()
    KB = 1024
    BASE = 16512

    def sb(name, kb, shape, dt=F32):
        return nc.alloc_sbuf_tensor_at(name, shape, dt, offset=BASE + int(kb * KB))

    def run(phase):
        mine = {}

        def sem(name):
            if name not in mine:
                mine[name] = nc.alloc_semaphore(name)
            return mine[name]

        phase(nc, A, env | {"sem": sem, "env": env})
        nc.clear_and_free_semaphores(list(mine.values()))
        nc.all_engine_barrier()

    with ctx:
        PS = ctx.enter_context(nc.psum_tensor("PS", [P, 8, 512], F32))
        const = sb("const", 0, [P, NCONST])
        C = {k: const[:, a:a + n] for k, (a, n) in CCOL.items()}
        ident = C["ident"]
        KC = NCONST * 4 / KB
        assert KC <= 6
        vecT = sb("vecT", 6, [P, NV])
        adaT = sb("adaT", 6.375, [P, NM, NC_])
        coef = sb("coef", 8.0625, [P, 2, KD, NC_])
        stat = sb("stat", 8.65625, [P, 8, 16])
        cT = sb("cT", 9.1875, [P, NC_, KD])
        x = sb("x", 26, [P, NT, D])
        hT = sb("hT", 46, [P, KD, N])
        env = dict(locals())
        phases = (phase_condition_and_project, phase_latents, phase_prompt_attention, phase_sample_attention,
                  phase_merge, phase_keys, phase_gates, phase_experts)
        for phase in phases[:upto]:
            run(phase)
        if dbg:
            dbg(nc, env, nc.alloc_semaphore, sb)


def phase_condition_and_project(nc, A, env):
    sb, sem, PS, C, ident = (env[k] for k in ("sb", "sem", "PS", "C", "ident"))
    const, vecT, adaT, coef, stat, cT, x, hT = (env[k] for k in ("const", "vecT", "adaT", "coef", "stat", "cT", "x", "hT"))
    win = sb("win", 66, [P, KD, INW])
    WA = 2
    NWA = 2 * KD // WA
    wada = [sb(f"wada{i}", 135 + 8 * i, [P, KD, WA * P]) for i in range(NWA)]
    xn = [sb(f"xn{i}", 10 + 4 * i, [P, D]) for i in range(2)]
    ktok = [sb(f"ktok{i}", 18 + 2 * i, [P, SBW]) for i in range(2)]
    crow = sb("crow", 22, [NC_ * KD, P])
    cexp = sb("cexp", 22.5, [P, NC_ * KD])
    vrow = sb("vrow", 23, [NV, P])
    junk = sb("junk", 203, [P, D])
    qT = sb("qT", 159, [P, SBW // P, N])
    kT = sb("kT", 169, [P, SBW // P, N])
    vt = sb("vt", 179, [P, NT, SBW])
    lat = sb("lat", 189, [P, NT, LAT])
    env["env"].update(qT=qT, kT=kT, vt=vt, lat=lat, junk=junk)

    const_in, vec_in, c_in = sem("const_in"), sem("vec_in"), sem("c_in")
    x_in = [sem(f"x_in{t}") for t in range(NT)]
    wada_in = [sem(f"wada_in{i}") for i in range(NWA)]
    win_in = [sem(f"win_in{g}") for g in range(5)]
    small_T, small_ready = sem("small_T"), sem("small_ready")
    c_exp = sem("c_exp")
    ada_psum, ada_ready = sem("ada_psum"), sem("ada_ready")
    x_sq, x_rstd, x_sqrt, xn_ready = sem("x_sq"), sem("x_rstd"), sem("x_sqrt"), sem("xn_ready")
    xT_psum, hT_ready, v_step = sem("xT_psum"), sem("hT_ready"), sem("v_step")
    q_psum, q_ready = sem("q_psum"), sem("q_ready")
    tok_psum = [sem(f"tok_psum{g}") for g in range(4)]
    tok_ready = [sem(f"tok_ready{g}") for g in range(4)]
    kT_psum, kT_ready, sbv_out = sem("kT_psum"), sem("kT_ready"), sem("sbv_out")
    sbk_out = [sem("sbk_out0"), sem("sbk_out1")]
    x_dram = [A["x_prompt"][0, t * P:(t + 1) * P, :] for t in range(PT)] + [A["x_sample"].rearrange("b q d -> (b q) d")]
    sbk_dram = ([A["sbk_p"][0, 0, t * P:(t + 1) * P].rearrange("t h d -> t (h d)") for t in range(PT)]
                + [A["sbk_s"][0].rearrange("b q h d -> (b q) (h d)")])
    sbv_dram = ([A["sbv_p"][0, 0, t * P:(t + 1) * P].rearrange("t h d -> t (h d)") for t in range(PT)]
                + [A["sbv_s"][0].rearrange("b q h d -> (b q) (h d)")])
    GROUPS = [(SBW, SBW), (2 * SBW, SBW), (3 * SBW, 512), (3 * SBW + 512, LAT - 512)]

    with nc.Block() as block:
        @block.sync
        def _(sp):
            sp.dma_start(crow[0:KD, :], A["c_prompt"].rearrange("b (k p) -> (b k) p", p=P)).then_inc(c_in, 16)
            sp.dma_start(crow[KD:, :], A["c_sample"].rearrange("b (k p) -> (b k) p", p=P)).then_inc(c_in, 16)
            sp.wait_ge(const_in, 16)
            sp.wait_ge(vec_in, 16 * len(VECTORS))
            for i in range(NWA):
                sp.dma_start(wada[i][:], A["w_ada"][0].rearrange("(k p) m -> p k m", p=P)[:, :, i * WA * P:(i + 1) * WA * P]
                             ).then_inc(wada_in[i], 16)
                if i == NWA // 2:
                    for t in range(NT):
                        sp.dma_start(x[:, t, :], x_dram[t]).then_inc(x_in[t], 16)
            for g, (c0, w) in enumerate(GROUPS + [(0, SBW)]):
                sp.dma_start(win[:, :, c0:c0 + w], A["w_in"][0].rearrange("(k p) m -> p k m", p=P)[:, :, c0:c0 + w]).then_inc(win_in[g], 16)
            for t in range(NT):
                sp.wait_ge(tok_ready[0], t + 1)
                sp.dma_start(sbk_dram[t], ktok[t % 2][:]).then_inc(sbk_out[t % 2], 16)
                sp.wait_ge(tok_ready[1], t + 1)
                sp.dma_start(sbv_dram[t], vt[:, t, :]).then_inc(sbv_out, 16)
            sp.wait_ge(sbk_out[0], 16 * 3)
            sp.wait_ge(sbk_out[1], 16 * 2)
            sp.wait_ge(sbv_out, 16 * NT)

        @block.gpsimd
        def _(pool):
            pass

        @block.scalar
        def _(act):
            act.dma_start(const[:], A["table"]).then_inc(const_in, 16)
            for name, n in VECTORS:
                act.dma_start(vrow[VROW[name]:VROW[name] + n, :], A[name].rearrange("a (k p) -> (a k) p", p=P)).then_inc(vec_in, 16)
            act.wait_ge(small_T, 2)
            act.activation(cexp[:], PS[:, 0, 0:NC_ * KD], ACT.Exp, scale=-1.0).then_inc(c_exp, 1)
            for t in range(NT):
                act.wait_ge(x_in[t], 16)
                if t >= 1:
                    act.wait_ge(x_sq, t)
                act.activation(junk[:], x[:, t, :], ACT.Square, accum_out=stat[:, 0, t:t + 1]).then_inc(x_sq, 1)
            act.wait_ge(x_rstd, 1)
            act.activation(stat[:, 1, 0:NT], stat[:, 1, 0:NT], ACT.Sqrt).then_inc(x_sqrt, 1)
            act.wait_ge(x_rstd, 2)
            for t in range(NT):
                if t >= 2:
                    act.wait_ge(xT_psum, 2 * (t - 1))
                act.activation(xn[t % 2][:], x[:, t, :], ACT.Copy, scale=stat[:, 2, t:t + 1]).then_inc(xn_ready, 1)
            for t in range(NT):
                act.wait_ge(tok_psum[0], t + 1)
                if t >= 2:
                    act.wait_ge(sbk_out[t % 2], 16 * (t // 2))
                    act.wait_ge(kT_psum, t - 1)
                act.activation(ktok[t % 2][:], PS[:, 0, :], ACT.Copy).then_inc(tok_ready[0], 1)
                act.wait_ge(tok_psum[2], t + 1)
                act.activation(lat[:, t, 0:512], PS[:, 2, :], ACT.Copy).then_inc(tok_ready[2], 1)
                act.wait_ge(kT_psum, t + 1)
                act.activation(kT[:, :, t * P:(t + 1) * P], PS[:, 4, :].rearrange("p (c n) -> p c n", c=4), ACT.Copy
                               ).then_inc(kT_ready, 1)

        @block.tensor
        def _(pe):
            pe.wait_ge(const_in, 16)
            pe.wait_ge(vec_in, 16 * len(VECTORS))
            pe.transpose(PS[:, 1, 0:NV], vrow[:], ident[0:NV, 0:NV]).then_inc(small_T, 1)
            pe.wait_ge(c_in, 32)
            pe.transpose(PS[:, 0, 0:NC_ * KD], crow[:], ident[0:NC_ * KD, 0:NC_ * KD]).then_inc(small_T, 1)
            pe.wait_ge(small_ready, 2)
            for i in range(NWA):
                pe.wait_ge(wada_in[i], 16)
                for j in range(WA):
                    m = i * WA + j
                    for k in range(KD):
                        mm = pe.matmul(PS[:, 2, m * NC_:(m + COPIES) * NC_], wada[i][:, k, j * P:(j + 1) * P],
                                       cT[:, :, k].unsqueeze(1).broadcast_to((P, COPIES, NC_)), start=k == 0, stop=k == KD - 1)
            mm.then_inc(ada_psum, 1)
            for t in range(NT):
                pe.wait_ge(xn_ready, t + 1)
                if t == 0:
                    pe.wait_ge(ada_ready, 3)
                for b in range(2):
                    if t >= 2:
                        pe.wait_ge(hT_ready, 2 * (t - 2) + b + 1)
                    for j in range(4):
                        k = 4 * b + j
                        mm = pe.transpose(PS[:, 4 + 2 * (t % 2) + b, j * P:(j + 1) * P], xn[t % 2][:, k * P:(k + 1) * P], ident)
                    mm.then_inc(xT_psum, 1)
            for t in range(NT):
                pe.wait_ge(hT_ready, 2 * (t + 1))
                for g, (c0, w) in enumerate(GROUPS):
                    if t >= 1:
                        pe.wait_ge(tok_ready[g], t)
                    elif g == 2:
                        pe.wait_ge(ada_ready, 3)
                    if t == 0:
                        pe.wait_ge(win_in[g], 16)
                    for k in range(KD):
                        mm = pe.matmul(PS[:, g, 0:w], hT[:, k, t * P:(t + 1) * P], win[:, k, c0:c0 + w],
                                       start=k == 0, stop=k == KD - 1)
                    mm.then_inc(tok_psum[g], 1)
                pe.wait_ge(tok_ready[0], t + 1)
                if t >= 1:
                    pe.wait_ge(kT_ready, t)
                else:
                    pe.wait_ge(hT_ready, 2 * NT)
                for c in range(4):
                    mm = pe.transpose(PS[:, 4, c * P:(c + 1) * P], ktok[t % 2][:, c * P:(c + 1) * P], ident)
                mm.then_inc(kT_psum, 1)
            pe.wait_ge(win_in[4], 16)
            for c in range(SBW // P):
                for b in range(2):
                    i = 2 * c + b
                    if i >= 2:
                        pe.wait_ge(q_ready, i - 1)
                    for k in range(KD):
                        mm = pe.matmul(PS[:, 6 + b, 0:HALF], win[:, k, c * P:(c + 1) * P], hT[:, k, b * HALF:(b + 1) * HALF],
                                       start=k == 0, stop=k == KD - 1)
                    mm.then_inc(q_psum, 1)

        @block.vector
        def _(dve):
            step = Step(dve, v_step)
            dve.wait_ge(small_T, 1)
            dve.tensor_copy(vecT[:], PS[:, 1, 0:NV]).then_inc(small_ready, 1)
            dve.wait_ge(c_exp, 1)
            step(dve.tensor_scalar(cexp[:], cexp[:], 1.0, None, ALU.add))
            step.wait()
            step(dve.reciprocal(cexp[:], cexp[:]))
            step.wait()
            dve.tensor_tensor(cT[:].rearrange("p a k -> p (a k)"), PS[:, 0, 0:NC_ * KD], cexp[:], ALU.mult).then_inc(small_ready, 1)
            dve.wait_ge(x_sq, NT)
            dve.tensor_scalar(stat[:, 1, 0:NT], stat[:, 0, 0:NT], 1.0 / D, EPS, ALU.mult, ALU.add).then_inc(x_rstd, 1)
            dve.wait_ge(x_sqrt, 1)
            dve.reciprocal(stat[:, 2, 0:NT], stat[:, 1, 0:NT]).then_inc(x_rstd, 1)
            dve.wait_ge(ada_psum, 1)
            dve.wait_ge(small_ready, 1)
            m = 2 * KD
            dve.tensor_tensor(adaT[:, 0:m, :], PS[:, 2, 0:m * NC_].rearrange("p (m c) -> p m c", c=NC_),
                              vecT[:, VROW["b_ada"]:VROW["b_ada"] + m].unsqueeze(2).broadcast_to((P, m, NC_)), ALU.add).then_inc(ada_ready, 1)
            dve.wait_ge(ada_ready, 1)
            dve.tensor_scalar(coef[:, 0], adaT[:, SC1:SC1 + KD, :], 1.0, None, ALU.add).then_inc(ada_ready, 1)
            dve.wait_ge(ada_ready, 2)
            g = VROW["g_mix_pre"]
            dve.tensor_tensor(coef[:, 0], coef[:, 0], vecT[:, g:g + KD].unsqueeze(2).broadcast_to((P, KD, NC_)), ALU.mult).then_inc(ada_ready, 1)
            dve.wait_ge(ada_ready, 3)
            for t in range(NT):
                for b in range(2):
                    dve.wait_ge(xT_psum, 2 * t + b + 1)
                    modulate(dve, step, hT, PS[:, 4 + 2 * (t % 2) + b, :], coef[:, 0], adaT[:, SH1:SH1 + KD, :], t, b, hT_ready)
            for t in range(NT):
                dve.wait_ge(tok_psum[1], t + 1)
                dve.tensor_copy(vt[:, t, :], PS[:, 1, :]).then_inc(tok_ready[1], 1)
                dve.wait_ge(tok_psum[3], t + 1)
                dve.tensor_copy(lat[:, t, 512:LAT], PS[:, 3, 0:LAT - 512]).then_inc(tok_ready[3], 1)
            for c in range(SBW // P):
                for b in range(2):
                    dve.wait_ge(q_psum, 2 * c + b + 1)
                    dve.tensor_scalar(qT[:, c, b * HALF:(b + 1) * HALF], PS[:, 6 + b, 0:HALF], SB_SCALE, None, ALU.mult).then_inc(q_ready, 1)


def modulate(dve, step, out, psum, scale, shift, t, b, done):
    cols = slice(4 * b, 4 * b + 4)
    if t < PT:
        dst = out[:, cols, t * P:(t + 1) * P]
        src = psum.rearrange("p (k n) -> p k n", k=4)
        s, h = (v[:, cols, 0:1].broadcast_to((P, 4, P)) for v in (scale, shift))
    else:
        dst = out[:, cols, t * P:(t + 1) * P].rearrange("p k (s q) -> p k s q", q=STEP)
        src = psum.rearrange("p (k s q) -> p k s q", k=4, q=STEP)
        s, h = (v[:, cols, 1:NC_].unsqueeze(3).broadcast_to((P, 4, NSEQ, STEP)) for v in (scale, shift))
    step(dve.tensor_tensor(dst, src, s, ALU.mult))
    step.wait()
    dve.tensor_tensor(dst, dst, h, ALU.add).then_inc(done, 1)


def phase_latents(nc, A, env):
    sb, sem, PS, C, ident = (env[k] for k in ("sb", "sem", "PS", "C", "ident"))
    vecT, stat, lat, junk, qT = (env[k] for k in ("vecT", "stat", "lat", "junk", "qT"))
    CQ, CK = QR // P, KVR // P
    wuq = sb("wuq", 135, [P, CQ, H * QK])
    wuk = sb("wuk", 144, [P, CK, H * HD])
    wuv = sb("wuv", 148, [P, CK, H * HD])
    qtok = [sb(f"qtok{i}", 152 + 3 * i, [P, H * QK]) for i in range(2)]
    gkv = sb("gkv", 158, [P, KVR])
    qlatT = sb("qlatT", 66, [P, CQ, N])
    ckvT = sb("ckvT", 74, [P, CK, N])
    qmT = sb("qmT", 79, [QK, H, N])
    kmT = sb("kmT", 99, [QK, H, SEQ])
    vm = sb("vm", 115, [P, PT, SBW])
    krT = sb("krT", 123, [QK, P])
    wukT = sb("wukT", 123.5, [HD, H, CK, P])
    qz = [sb(f"qz{j}", 46 + 8 * j, [P, SBW // P, SEQ]) for j in range(2)]
    krpad = sb("krpad", 10, [P, NT, QK])
    rtmp = sb("rtmp", 12, [P, 2, H * RH])
    rtmp2 = sb("rtmp2", 13, [P, 4, H * RH])
    qabsT = sb("qabsT", 18, [P, CK, H, P])
    env["env"].update(ckvT=ckvT, qmT=qmT, kmT=kmT, vm=vm, krT=krT, qabsT=qabsT, qz=qz)
    cos = C["cos"].rearrange("p (t r) -> p t r", r=RH)
    sin = C["sin"].rearrange("p (t r) -> p t r", r=RH)
    nq, nkv, nrope = 0, QR, QR + KVR

    qz_ready = sem("qz_ready")
    wuq_in, wuk_in, wuv_in, gkv_in = sem("wuq_in"), sem("wuk_in"), sem("wuv_in"), sem("gkv_in")
    l_sq, l_var, l_sqrt, l_rstd, l_step = sem("l_sq"), sem("l_var"), sem("l_sqrt"), sem("l_rstd"), sem("l_step")
    pad_zero, kr_ready, ckv_ready, qn_ready = sem("pad_zero"), sem("kr_ready"), sem("ckv_ready"), sem("qn_ready")
    lat_out = sem("lat_out")
    ql_psum, ql_ready, cl_psum, cl_ready, kr_evac = sem("ql_psum"), sem("ql_ready"), sem("cl_psum"), sem("cl_ready"), sem("kr_evac")
    up_psum, up_ready, rot_ready = sem("up_psum"), sem("up_ready"), sem("rot_ready")
    qm_psum, qm_ready = sem("qm_psum"), [sem("qm_ready0"), sem("qm_ready1")]
    item_psum, item_ready = [sem("item_psum0"), sem("item_psum1")], [sem("item_ready0"), sem("item_ready1")]
    ckv_dram = ([A["ckv_p"][0, 0, t * P:(t + 1) * P, :] for t in range(PT)] + [A["ckv_s"][0].rearrange("b q c -> (b q) c")])
    kr_dram = ([A["kr_p"][0, 0, t * P:(t + 1) * P, :] for t in range(PT)] + [A["kr_s"][0].rearrange("b q c -> (b q) c")])
    NITEM = H + PT + 2 * H * CK // 4

    def item_target(i):
        if i < H:
            return kmT[0:HD, i, :], PS[0:HD, 6 + i % 2, :]
        if i < H + PT:
            return vm[:, i - H, :], PS[:, 6 + i % 2, :]
        j = i - H - PT
        if j < 4:
            return wukT[:].rearrange("p h c n -> p (h c n)")[:, 512 * j:512 * (j + 1)], PS[0:HD, 6 + i % 2, :]
        j -= 4
        return qabsT[:].rearrange("p c h n -> p (c h n)")[:, 512 * j:512 * (j + 1)], PS[:, 6 + i % 2, :]

    with nc.Block() as block:
        @block.sync
        def _(sp):
            sp.dma_start(wuq[:], A["w_uq"][0].rearrange("(c p) m -> p c m", p=P)).then_inc(wuq_in, 16)
            sp.dma_start(gkv[:], A["g_kv_lat"].broadcast_to((P, KVR))).then_inc(gkv_in, 16)
            sp.dma_start(wuk[:], A["w_uk"][0].rearrange("(c p) h m -> p c (h m)", p=P)).then_inc(wuk_in, 16)
            sp.dma_start(wuv[:], A["w_uv"][0].rearrange("(c p) h m -> p c (h m)", p=P)).then_inc(wuv_in, 16)
            sp.wait_ge(kr_ready, 1)
            for t in range(NT):
                sp.dma_start(kr_dram[t], krpad[:, t, HD:QK]).then_inc(lat_out, 16)
            for t in range(NT):
                sp.wait_ge(ckv_ready, t + 1)
                sp.dma_start(ckv_dram[t], lat[:, t, nkv:nrope]).then_inc(lat_out, 16)
            sp.wait_ge(lat_out, 16 * 2 * NT)

        @block.gpsimd
        def _(pool):
            pool.memset(krpad[:, :, 0:HD], 0.0).then_inc(pad_zero, 1)
            for j in range(2):
                pool.memset(qz[j][:], 0.0).then_inc(qz_ready, 1)
            pool.wait_ge(qz_ready, 2)
            for j in range(2):
                own = slice(j * HD, (j + 1) * HD)
                if j:
                    pool.wait_ge(qz_ready, 3)
                pool.tensor_copy(qz[j][own], qT[own, :, 0:SEQ]).then_inc(qz_ready, 1)

        @block.scalar
        def _(act):
            for t in range(NT):
                for j, (a, b) in enumerate(((nq, nkv), (nkv, nrope))):
                    if t + j:
                        act.wait_ge(l_sq, 2 * t + j)
                    act.activation(junk[:, 0:b - a], lat[:, t, a:b], ACT.Square, accum_out=stat[:, 3 + j, t:t + 1]).then_inc(l_sq, 1)
            act.wait_ge(l_var, 2)
            act.activation(stat[:, 3:5, 0:NT], stat[:, 3:5, 0:NT], ACT.Sqrt).then_inc(l_sqrt, 1)
            act.wait_ge(l_rstd, 1)
            for t in range(NT):
                act.activation(lat[:, t, nq:nkv], lat[:, t, nq:nkv], ACT.Copy, scale=stat[:, 5, t:t + 1]).then_inc(qn_ready, 1)

            def latent_columns(t):
                act.wait_ge(cl_psum, t + 1)
                act.activation(ckvT[:, :, t * P:(t + 1) * P], PS[:, 1, 0:KVR].rearrange("p (c n) -> p c n", c=CK), ACT.Copy
                               ).then_inc(cl_ready, 1)
                src = PS[HD:QK, 1, KVR:KVR + P]
                if t < PT:
                    act.activation(kmT[HD:QK, :, t * P:(t + 1) * P], src.unsqueeze(1).broadcast_to((ROPE, H, P)), ACT.Copy).then_inc(kr_evac, 1)
                else:
                    act.activation(krT[:], PS[0:QK, 1, KVR:KVR + P], ACT.Copy).then_inc(kr_evac, 1)

            latent_columns(0)
            for t in range(NT):
                act.wait_ge(up_psum, t + 1)
                if t >= 2:
                    act.wait_ge(qm_psum, 2 * (t - 1))
                act.activation(qtok[t % 2][:].rearrange("p (a b) -> p a b", a=2), PS[:, 2:4, 0:H * QK // 2], ACT.Copy).then_inc(up_ready, 1)
                if t + 1 < NT:
                    latent_columns(t + 1)
                act.wait_ge(qm_psum, 2 * t + 1)
                act.activation(qmT[:, 0:4, t * P:(t + 1) * P], PS[0:QK, 4, :].rearrange("p (h n) -> p h n", h=4), ACT.Copy).then_inc(qm_ready[0], 1)
            for i in range(0, NITEM, 2):
                act.wait_ge(item_psum[0], i // 2 + 1)
                act.activation(*item_target(i), ACT.Copy).then_inc(item_ready[0], 1)

        @block.tensor
        def _(pe):
            def latents(t):
                cols = slice(t * P, (t + 1) * P)
                pe.wait_ge(qn_ready, t + 1)
                if t:
                    pe.wait_ge(ql_ready, t)
                for c in range(CQ):
                    mm = pe.transpose(PS[:, 0, c * P:(c + 1) * P], lat[:, t, c * P:(c + 1) * P], ident)
                mm.then_inc(ql_psum, 1)
                pe.wait_ge(ckv_ready, t + 1)
                pe.wait_ge(kr_ready, 1)
                if t:
                    pe.wait_ge(kr_evac, t)
                for c in range(CK):
                    pe.transpose(PS[:, 1, c * P:(c + 1) * P], lat[:, t, nkv + c * P:nkv + (c + 1) * P], ident)
                pe.transpose(PS[0:QK, 1, KVR:KVR + P], krpad[:, t, :], ident).then_inc(cl_psum, 1)
                pe.wait_ge(ql_ready, t + 1)
                if t:
                    pe.wait_ge(up_ready, t)
                else:
                    pe.wait_ge(wuq_in, 16)
                for b in range(2):
                    for c in range(CQ):
                        mm = pe.matmul(PS[:, 2 + b, 0:H * QK // 2], qlatT[:, c, cols], wuq[:, c, b * H * QK // 2:(b + 1) * H * QK // 2],
                                       start=c == 0, stop=c == CQ - 1)
                mm.then_inc(up_psum, 1)

            def queries(t):
                pe.wait_ge(rot_ready, t + 1)
                for b in range(2):
                    if t:
                        pe.wait_ge(qm_ready[b], t)
                    for j in range(4):
                        h = 4 * b + j
                        mm = pe.transpose(PS[0:QK, 4 + b, j * P:(j + 1) * P], qtok[t % 2][:, h * QK:(h + 1) * QK], ident)
                    mm.then_inc(qm_psum, 1)

            latents(0)
            for t in range(NT):
                if t + 1 < NT:
                    latents(t + 1)
                queries(t)
            pe.wait_ge(cl_ready, NT)
            pe.wait_ge(wuk_in, 16)
            pe.wait_ge(wuv_in, 16)
            for i in range(NITEM):
                out = item_target(i)[1]
                if i >= 2:
                    pe.wait_ge(item_ready[i % 2], i // 2)
                if i < H:
                    for c in range(CK):
                        mm = pe.matmul(out, wuk[:, c, i * HD:(i + 1) * HD], ckvT[:, c, 0:SEQ], start=c == 0, stop=c == CK - 1)
                elif i < H + PT:
                    t = i - H
                    for c in range(CK):
                        mm = pe.matmul(out, ckvT[:, c, t * P:(t + 1) * P], wuv[:, c, :], start=c == 0, stop=c == CK - 1)
                elif i < H + PT + 4:
                    for n in range(4):
                        h, c = divmod(4 * (i - H - PT) + n, CK)
                        mm = pe.transpose(out[:, n * P:(n + 1) * P], wuk[:, c, h * HD:(h + 1) * HD], ident)
                else:
                    if i == H + PT + 4:
                        pe.wait_ge(item_ready[0], (i + 1) // 2)
                        pe.wait_ge(item_ready[1], i // 2)
                        pe.wait_ge(qm_ready[0], NT)
                        pe.wait_ge(qm_ready[1], NT)
                    for n in range(4):
                        c, h = divmod(4 * (i - H - PT - 4) + n, H)
                        mm = pe.matmul(out[:, n * P:(n + 1) * P], wukT[:, h, c, :], qmT[0:HD, h, SEQ:N], start=True, stop=True)
                mm.then_inc(item_psum[i % 2], 1)

        @block.vector
        def _(dve):
            step = Step(dve, l_step)
            dve.wait_ge(l_sq, 2 * NT)
            dve.tensor_scalar(stat[:, 3, 0:NT], stat[:, 3, 0:NT], 1.0 / QR, EPS, ALU.mult, ALU.add).then_inc(l_var, 1)
            dve.tensor_scalar(stat[:, 4, 0:NT], stat[:, 4, 0:NT], 1.0 / KVR, EPS, ALU.mult, ALU.add).then_inc(l_var, 1)
            a, b = lat[:, :, nrope:nrope + RH], lat[:, :, nrope + RH:LAT]
            u, v = (rtmp[:, i, 0:NT * RH].rearrange("p (t r) -> p t r", r=RH) for i in range(2))
            for x1, x2, op, dst in ((a, b, ALU.subtract, krpad[:, :, HD:HD + RH]), (b, a, ALU.add, krpad[:, :, HD + RH:QK])):
                step(dve.tensor_tensor(u, x1, cos, ALU.mult))
                step(dve.tensor_tensor(v, x2, sin, ALU.mult))
                step.wait()
                step(last := dve.tensor_tensor(dst, u, v, op))
                step.wait()
            dve.wait_ge(l_sqrt, 1)
            dve.reciprocal(stat[:, 5:7, 0:NT], stat[:, 3:5, 0:NT]).then_inc(l_rstd, 1)
            dve.wait_ge(l_rstd, 1)
            dve.wait_ge(pad_zero, 1)
            dve.sem_inc(kr_ready, 1)
            dve.wait_ge(gkv_in, 16)
            for t in range(NT):
                dve.scalar_tensor_tensor(out=lat[:, t, nkv:nrope], in0=lat[:, t, nkv:nrope], scalar=stat[:, 6, t:t + 1], in1=gkv[:],
                                         op0=ALU.mult, op1=ALU.mult).then_inc(ckv_ready, 1)
            g = VROW["g_q_lat"]

            def latent_columns(t):
                dve.wait_ge(ql_psum, t + 1)
                dve.tensor_tensor(qlatT[:, :, t * P:(t + 1) * P], PS[:, 0, 0:QR].rearrange("p (c n) -> p c n", c=CQ),
                                  vecT[:, g:g + CQ].unsqueeze(2).broadcast_to((P, CQ, P)), ALU.mult).then_inc(ql_ready, 1)

            latent_columns(0)
            for t in range(NT):
                cols = slice(t * P, (t + 1) * P)
                if t + 1 < NT:
                    latent_columns(t + 1)
                dve.wait_ge(up_ready, t + 1)
                q = qtok[t % 2][:].rearrange("p (h m) -> p h m", h=H)
                a, b = q[:, :, HD:HD + RH], q[:, :, HD + RH:QK]
                c, s = (w[:, t, :].unsqueeze(1).broadcast_to((P, H, RH)) for w in (cos, sin))
                u, v = (rtmp2[:, i, :].rearrange("p (h r) -> p h r", h=H) for i in range(2))
                w, z = (rtmp2[:, i, :].rearrange("p (h r) -> p h r", h=H) for i in range(2, 4))
                step(dve.tensor_tensor(u, a, c, ALU.mult))
                step(dve.tensor_tensor(v, b, s, ALU.mult))
                step(dve.tensor_tensor(w, b, c, ALU.mult))
                step(dve.tensor_tensor(z, a, s, ALU.mult))
                step.wait()
                step(dve.tensor_tensor(a, u, v, ALU.subtract))
                step.wait()
                step(dve.tensor_tensor(b, w, z, ALU.add))
                step.wait()
                dve.sem_inc(rot_ready, 1)
                dve.wait_ge(qm_psum, 2 * t + 2)
                dve.tensor_copy(qmT[:, 4:8, cols], PS[0:QK, 5, :].rearrange("p (h n) -> p h n", h=4)).then_inc(qm_ready[1], 1)
            for i in range(1, NITEM, 2):
                dve.wait_ge(item_psum[1], i // 2 + 1)
                dve.tensor_copy(*item_target(i)).then_inc(item_ready[1], 1)


def phase_prompt_attention(nc, A, env):
    sb, sem, PS, C, ident = (env[k] for k in ("sb", "sem", "PS", "C", "ident"))
    stat, qz, kT, vt, qmT, kmT, vm = (env[k] for k in ("stat", "qz", "kT", "vt", "qmT", "kmT", "vm"))
    osT = sb("osT", 135, [P, SBW // P, N])
    omT = sb("omT", 145, [P, SBW // P, N])
    env["env"].update(osT=osT, omT=omT)
    t1 = sb("t1", 189, [P, 2, SEQ])
    t2 = sb("t2", 193, [P, 2, SEQ])
    pr = sb("pr", 197, [P, 2, SEQ])
    aT = sb("aT", 10, [P, 2, PT, P])
    pT = sb("pT", 14, [P, 2, PT, P])
    peak, total, inverse = stat[:, 3, 0:2], stat[:, 4, 0:2], stat[:, 5, 0:2]
    wada = [sb(f"wada_b{i}", (66, 123.5)[i], [P, KD, 2 * P]) for i in range(2)]
    wada_in = [sem(f"pa_wada_in{i}") for i in range(2)]
    NREST = NM - 2 * KD
    rest = PS[:, 6, P:P + NREST * NC_]
    adaT, coef, vecT, cT = (env[k] for k in ("adaT", "coef", "vecT", "cT"))
    names = ("ada_psum ada_ready coef_step z_psum s_psum z_abs s_peak s_bias soft1 soft2 soft soft_kept tail logit logit_kept a_ready p_exp p_inv p_ready "
             "mT_psum aT_psum mT0 mT1 aT0 aT1 om_psum os_psum om_out os_out").split()
    S = {n: sem("pa_" + n) for n in names}
    ROUNDS = [(i, hp) for i in range(PT) for hp in range(H // 2)]
    R = len(ROUNDS)

    assert 2 * R == NREST

    def W(r):
        return (ROUNDS[r][0] + 1) * P

    with nc.Block() as block:
        @block.sync
        def _(sp):
            for r in range(R):
                if r >= 2:
                    sp.wait_ge(S["ada_psum"], r - 1)
                c0 = (2 * KD + 2 * r) * P
                sp.dma_start(wada[r % 2][:], A["w_ada"][0].rearrange("(k p) m -> p k m", p=P)[:, :, c0:c0 + 2 * P]).then_inc(wada_in[r % 2], 16)

        @block.gpsimd
        def _(pool):
            for r, (i, hp) in enumerate(ROUNDS):
                d = slice(i * P, i * P + P)
                for buf, mask, op, need, done in ((t1, "keep", ALU.mult, "soft", "soft_kept"), (t2, "drop", ALU.add, "logit", "logit_kept")):
                    pool.wait_ge(S[need], r + 1)
                    pool.tensor_tensor(buf[:, :, d], buf[:, :, d], C[mask].unsqueeze(1).broadcast_to((P, 2, P)), op).then_inc(S[done], 1)

        @block.scalar
        def _(act):
            def softplus(r):
                w = W(r)
                act.wait_ge(S["z_psum"], r + 1)
                if r:
                    act.wait_ge(S["tail"], 2 * r)
                act.activation(t1[:, :, 0:w], PS[:, 0:2, 0:w], ACT.Abs).then_inc(S["z_abs"], 1)
                act.wait_ge(S["z_abs"], r + 1)
                act.activation(t1[:, :, 0:w], t1[:, :, 0:w], ACT.Exp, scale=-1.0).then_inc(S["soft1"], 1)
                act.wait_ge(S["soft1"], r + 1)
                act.activation(t1[:, :, 0:w], t1[:, :, 0:w], ACT.Ln, bias=1.0).then_inc(S["soft2"], 1)

            def softmax(r):
                w = W(r)
                act.wait_ge(S["s_bias"], r + 1)
                if r:
                    act.wait_ge(S["mT_psum"], r)
                for j in range(2):
                    act.activation(pr[:, j, 0:w], PS[:, 2 + j, 0:w], ACT.Exp, bias=peak[:, j:j + 1], scale=MLA_SCALE,
                                   accum_out=total[:, j:j + 1]).then_inc(S["p_exp"], 1)

            def transposed(r, dst, psum, done, used):
                i = ROUNDS[r][0]
                act.wait_ge(S[psum], r + 1)
                if r:
                    act.wait_ge(S[used], r)
                act.activation(dst[:, 0, 0:i + 1, :], PS[:, 4, 0:W(r)].rearrange("p (k n) -> p k n", n=P), ACT.Copy).then_inc(S[done], 1)

            act.preload_act_table_set("natural_log_exp_and_others")
            softmax(0)
            softplus(0)
            transposed(0, pT, "mT_psum", "mT0", "om_psum")
            for r, (i, hp) in enumerate(ROUNDS):
                act.wait_ge(S["logit_kept"], r + 1)
                act.activation(t2[:, :, 0:W(r)], t2[:, :, 0:W(r)], ACT.Exp).then_inc(S["a_ready"], 1)
                if r + 1 < R:
                    softmax(r + 1)
                    softplus(r + 1)
                act.wait_ge(S["om_psum"], r + 1)
                act.activation(omT[:, hp, i * P:(i + 1) * P], PS[:, 7, 0:P], ACT.Copy).then_inc(S["om_out"], 1)
                transposed(r, aT, "aT_psum", "aT0", "os_psum")
                if r + 1 < R:
                    transposed(r + 1, pT, "mT_psum", "mT0", "om_psum")

        @block.tensor
        def _(pe):
            def sb_scores(r):
                i, hp = ROUNDS[r]
                if r:
                    pe.wait_ge(S["logit"], r)
                for j in range(2):
                    mm = pe.matmul(PS[:, j, 0:W(r)], qz[j][:, hp, i * P:(i + 1) * P], kT[:, hp, 0:W(r)], start=True, stop=True)
                mm.then_inc(S["z_psum"], 1)

            def mla_scores(r):
                i, hp = ROUNDS[r]
                if r:
                    pe.wait_ge(S["p_exp"], 2 * r)
                for j in range(2):
                    h = 2 * hp + j
                    pe.matmul(PS[:, 2 + j, 0:W(r)], qmT[:, h, i * P:(i + 1) * P], kmT[:, h, 0:W(r)], start=True, stop=False)
                    mm = pe.matmul(PS[:, 2 + j, i * P:(i + 1) * P], C["chunk_row"][0:QK, :], C["chunk_col"][0:QK, :], start=False, stop=True)
                mm.then_inc(S["s_psum"], 1)

            def transposes(r, src, need, count, free, done):
                for j in range(2):
                    pe.wait_ge(S[need], count)
                    for f, n in free:
                        if n:
                            pe.wait_ge(S[f], n)
                    for k in range(ROUNDS[r][0] + 1):
                        mm = pe.transpose(PS[:, 4 + j, k * P:(k + 1) * P], src[:, j, k * P:(k + 1) * P], ident)
                mm.then_inc(S[done], 1)

            def values(r, v, wT, need, free, bank, done):
                i, hp = ROUNDS[r]
                for n in need:
                    pe.wait_ge(S[n], r + 1)
                if r:
                    pe.wait_ge(S[free], r)
                for j in range(2):
                    h = 2 * hp + j
                    for k in range(i + 1):
                        mm = pe.matmul(PS[j * HD:(j + 1) * HD, bank, 0:P], v[:, k, h * HD:(h + 1) * HD], wT[:, j, k, :],
                                       start=k == 0, stop=k == i)
                mm.then_inc(S[done], 1)

            def conditioning(r):
                pe.wait_ge(wada_in[r % 2], 16 * (r // 2 + 1))
                for j in range(2):
                    m = 2 * r + j
                    for k in range(KD):
                        mm = pe.matmul(PS[:, 6, P + m * NC_:P + (m + COPIES) * NC_], wada[r % 2][:, k, j * P:(j + 1) * P],
                                       cT[:, :, k].unsqueeze(1).broadcast_to((P, COPIES, NC_)), start=k == 0, stop=k == KD - 1)
                mm.then_inc(S["ada_psum"], 1)

            sb_scores(0)
            mla_scores(0)
            for r in range(R):
                transposes(r, pr, "p_ready", 2 * (r + 1), (("aT0", r), ("aT1", r)), "mT_psum")
                if r + 1 < R:
                    mla_scores(r + 1)
                values(r, vm, pT, ("mT0", "mT1"), "om_out", 7, "om_psum")
                if r + 1 < R:
                    sb_scores(r + 1)
                conditioning(r)
                transposes(r, t2, "a_ready", r + 1, (("mT0", r + 1), ("mT1", r + 1)), "aT_psum")
                values(r, vt, aT, ("aT0", "aT1"), "os_out", 6, "os_psum")

        @block.vector
        def _(dve):
            def start(r):
                w = W(r)
                dve.wait_ge(S["s_psum"], r + 1)
                if r:
                    dve.wait_ge(S["p_ready"], 2 * r)
                dve.tensor_reduce(peak, PS[:, 2:4, 0:w], AX_X, ALU.max).then_inc(S["s_peak"], 1)
                dve.wait_ge(S["s_peak"], r + 1)
                dve.tensor_scalar(peak, peak, -MLA_SCALE, None, ALU.mult).then_inc(S["s_bias"], 1)

            def transposed(r, dst, psum, done, used):
                i = ROUNDS[r][0]
                dve.wait_ge(S[psum], r + 1)
                if r:
                    dve.wait_ge(S[used], r)
                dve.tensor_copy(dst[:, 1, 0:i + 1, :], PS[:, 5, 0:W(r)].rearrange("p (k n) -> p k n", n=P)).then_inc(S[done], 1)

            def weights(r):
                w = W(r)
                start(r)
                dve.wait_ge(S["p_exp"], 2 * (r + 1))
                dve.reciprocal(inverse, total).then_inc(S["p_inv"], 1)
                dve.wait_ge(S["p_inv"], r + 1)
                for j in range(2):
                    dve.tensor_scalar(pr[:, j, 0:w], pr[:, j, 0:w], inverse[:, j:j + 1], None, ALU.mult).then_inc(S["p_ready"], 1)
                dve.wait_ge(S["soft2"], r + 1)
                dve.scalar_tensor_tensor(out=t1[:, :, 0:w], in0=PS[:, 0:2, 0:w], scalar=0.0, in1=t1[:, :, 0:w],
                                         op0=ALU.max, op1=ALU.add).then_inc(S["soft"], 1)

            weights(0)
            for r, (i, hp) in enumerate(ROUNDS):
                w = W(r)
                dve.wait_ge(S["soft_kept"], r + 1)
                if r:
                    dve.wait_ge(S["aT_psum"], r)
                last = w - 1
                for j in range(2):
                    rev = (lambda b: b[:, j, last::-1])
                    dve.tensor_tensor_scan(rev(t2), C["ones"][:, 0:1].broadcast_to((P, w)), rev(t1), 0.0, ALU.mult, ALU.add).then_inc(S["tail"], 1)
                dve.wait_ge(S["tail"], 2 * (r + 1))
                dve.tensor_tensor(t2[:, :, 0:w], PS[:, 0:2, 0:w], t2[:, :, 0:w], ALU.subtract).then_inc(S["logit"], 1)
                transposed(r, pT, "mT_psum", "mT1", "om_psum")
                if r + 1 < R:
                    weights(r + 1)
                transposed(r, aT, "aT_psum", "aT1", "os_psum")
                dve.wait_ge(S["os_psum"], r + 1)
                dve.tensor_copy(osT[:, hp, i * P:(i + 1) * P], PS[:, 6, 0:P]).then_inc(S["os_out"], 1)
            dve.wait_ge(S["ada_psum"], R)
            dve.tensor_tensor(adaT[:, 2 * KD:NM, :], rest.rearrange("p (m c) -> p m c", c=NC_),
                              vecT[:, 2 * KD:NM].unsqueeze(2).broadcast_to((P, NREST, NC_)), ALU.add).then_inc(S["ada_ready"], 1)
            dve.wait_ge(S["ada_ready"], 1)
            dve.tensor_scalar(coef[:, 1], adaT[:, SC2:SC2 + KD, :], 1.0, None, ALU.add).then_inc(S["coef_step"], 1)
            dve.wait_ge(S["coef_step"], 1)
            g = VROW["g_ffn_pre"]
            dve.tensor_tensor(coef[:, 1], coef[:, 1], vecT[:, g:g + KD].unsqueeze(2).broadcast_to((P, KD, NC_)), ALU.mult
                              ).then_inc(S["coef_step"], 1)


def phase_sample_attention(nc, A, env):
    sb, sem, PS, C, ident = (env[k] for k in ("sb", "sem", "PS", "C", "ident"))
    stat, qT, kT, qmT, ckvT, krT, qabsT, osT, omT = (env[k] for k in ("stat", "qT", "kT", "qmT", "ckvT", "krT", "qabsT", "osT", "omT"))
    KBLK, CQ, CK = PAST // P, SBW // P, KVR // P
    flat = PS[:].rearrange("p b n -> p (b n)")
    z, s = flat[:, 0:KEYS], flat[:, 1024:1024 + KEYS]
    s_new = flat[:, 1024 + PAST:1024 + PAST + WIDE]
    kc = [sb("kc0", 46, [P, KBLK, SBW]), sb("kc1", 99, [P, KBLK, SBW])]
    vc = [sb("vc0", 54, [P, KBLK, SBW]), sb("vc1", 107, [P, KBLK, SBW])]
    cc = [sb("cc0", 62, [P, KBLK, KVR]), sb("cc1", 115, [P, KBLK, KVR])]
    kr = [sb("kr0", 201, [P, KBLK, QK]), sb("kr1", 119, [P, KBLK, QK])]
    vnew = [sb("vnew0", 155, [P, SBW]), sb("vnew1", 131.5, [P, SBW])]
    cnew = [sb("cnew0", 157, [P, KVR]), sb("cnew1", 133.5, [P, KVR])]
    keyT = sb("keyT", 10, [P, CQ, PAST])
    latT = sb("latT", 66, [P, CK, PAST])
    rotT = sb("rotT", 70, [QK, PAST])
    qblk = sb("qblk", 72, [P, CQ, P])
    qabs = sb("qabs", 120.5, [P, CK, P])
    qrot = sb("qrot", 121.5, [QK, P])
    olatT = sb("olatT", 123.5, [P, CK, H, P])
    t1, t2, pr = sb("st1", 189, [P, KEYS]), sb("st2", 191.25, [P, KEYS]), sb("spr", 193.5, [P, KEYS])
    aT, pT = sb("saT", 196, [P, KBLK + 1, P]), sb("spT", 198.5, [P, KBLK + 1, P])
    wuv = sb("wuv_again", 203, [P, CK, SBW])
    peak, total, inverse = stat[:, 3, 0:1], stat[:, 4, 0:1], stat[:, 5, 0:1]
    names = ("zeroed qblk_ready q_ready z_psum s_psum z_abs soft1 soft2 soft soft_kept tail logit logit_kept a_ready s_peak s_bias "
             "p_exp p_inv p_ready turned turn0 turn1 ol_psum ol_out os_psum os_out om_psum om_out wuv_in").split()
    S = {n: sem("sa_" + n) for n in names}
    IN = {n: [sem(f"sa_{n}{i}") for i in range(2)] for n in ("kc_in", "vc_in", "cc_in", "kr_in", "new_in")}
    turn = [S["turn0"], S["turn1"]]
    KV, PER = CQ + CK + 1, CQ + CK + 1 + 4

    def new_cols(b, step=STEP):
        return bass.ds(SEQ + b * step, step)

    def wide(cols):
        return cols.unsqueeze(1).broadcast_to((cols.shape[0], WIDE // STEP, STEP))

    def loop(eng, body):
        with eng.Fori(0, NSEQ // 2 - 1) as pair:
            body(pair, 0, True)
            body(pair, 1, True)
        body(NSEQ // 2 - 1, 0, True)
        body(NSEQ // 2 - 1, 1, False)

    def place(e, n, more):
        return KV + PER * e + (n if more else n - KV)

    def piece(pair, e, n, more):
        return pair * (2 * PER) + place(e, n, more)

    def parity(e, n, more):
        return place(e, n, more) % 2

    def before(pair, e, n, more):
        return pair * PER + (place(e, n, more) // 2 + 1)

    def piece_target(n, e):
        bank = 4 + e
        if n < CQ:
            return keyT[:, n, :], PS[:, bank, :]
        if n < CQ + CK:
            return latT[:, n - CQ, :], PS[:, bank, :]
        if n < KV:
            return rotT[:], PS[0:QK, bank, :]
        dst = (pT, aT)[(n - KV) // 2]
        if (n - KV) % 2 == 0:
            return dst[:, 0:KBLK, :], PS[:, bank, :].rearrange("p (k n) -> p k n", n=P)
        return dst[0:STEP, KBLK, :], PS[0:STEP, bank, 0:P]

    def evacuate_first(eng, copy, mine):
        for n in range(mine, KV, 2):
            eng.wait_ge(S["turned"], n + 1)
            copy(*piece_target(n, mine)).then_inc(turn[mine], 1)

    def evacuate(eng, copy, mine, pair, e, ns, more):
        for n in ns:
            if parity(e, n, more) == mine:
                eng.wait_ge(S["turned"], piece(pair, e, n, more) + 1)
                copy(*piece_target(n, mine)).then_inc(turn[mine], 1)

    with nc.Block() as block:
        @block.sync
        def _(sp):
            def load_keys(b, e):
                sp.dma_start(kc[e][:], A["cache_sb_k"][0, b].rearrange("(k p) h d -> p k (h d)", p=P)).then_inc(IN["kc_in"][e], 16)
                sp.dma_start(kr[e][:, :, HD:QK], A["cache_mla_krope"][0, b].rearrange("(k p) c -> p k c", p=P)).then_inc(IN["kr_in"][e], 16)

            def load_latents(b, e):
                sp.dma_start(cc[e][:], A["cache_mla_ckv"][0, b].rearrange("(k p) c -> p k c", p=P)).then_inc(IN["cc_in"][e], 16)
                sp.dma_start(cnew[e][0:STEP, :], A["ckv_s"][0, b]).then_inc(IN["new_in"][e], 16)

            def load_values(b, e):
                sp.dma_start(vc[e][:], A["cache_sb_v"][0, b].rearrange("(k p) h d -> p k (h d)", p=P)).then_inc(IN["vc_in"][e], 16)
                sp.dma_start(vnew[e][0:STEP, :], A["sbv_s"][0, b].rearrange("q h d -> q (h d)")).then_inc(IN["new_in"][e], 16)

            sp.wait_ge(S["zeroed"], 6)
            for e in range(2):
                load_keys(e, e)
                load_latents(e, e)
                load_values(e, e)
            sp.dma_start(wuv[:], A["w_uv"][0].rearrange("(c p) h m -> p c (h m)", p=P)).then_inc(S["wuv_in"], 16)
            with sp.Fori(1, NSEQ // 2) as it:
                for e in range(2):
                    sp.wait_ge(S["turned"], it * (2 * PER) + ((e - 2) * PER + KV))
                    load_keys(it * 2 + e, e)
                    sp.wait_ge(S["ol_psum"], it * 2 + (e - 1))
                    load_latents(it * 2 + e, e)
                    sp.wait_ge(S["os_psum"], it * 2 + (e - 1))
                    load_values(it * 2 + e, e)

        @block.gpsimd
        def _(pool):
            for i in range(2):
                pool.memset(vnew[i][:], 0.0).then_inc(S["zeroed"], 1)
                pool.memset(cnew[i][:], 0.0).then_inc(S["zeroed"], 1)
                pool.memset(kr[i][:, :, 0:HD], 0.0).then_inc(S["zeroed"], 1)
            pool.memset(qblk[:], 0.0).then_inc(S["zeroed"], 1)
            pool.memset(aT[:, KBLK, :], 0.0).then_inc(S["zeroed"], 1)
            pool.memset(pT[:, KBLK, :], 0.0).then_inc(S["zeroed"], 1)

            def body(pair, e, more):
                b = pair * 2 + e
                new = slice(PAST, KEYS)
                pool.wait_ge(S["soft"], b + 1)
                pool.tensor_tensor(t1[:, new], t1[:, new], C["new_keep"], ALU.mult).then_inc(S["soft_kept"], 1)
                pool.wait_ge(S["logit"], b + 1)
                pool.tensor_tensor(t2[:, new], t2[:, new], C["new_drop"], ALU.add).then_inc(S["logit_kept"], 1)

            loop(pool, body)

        @block.scalar
        def _(act):
            def copy(dst, src):
                return act.activation(dst, src, ACT.Copy)

            act.preload_act_table_set("natural_log_exp_and_others")
            act.sem_inc(turn[0], 1)
            act.sem_inc(S["ol_out"], 1)
            act.wait_ge(S["zeroed"], 9)
            evacuate_first(act, copy, 0)

            def softplus(b):
                act.wait_ge(S["z_psum"], b + 1)
                act.activation(t1[:], z, ACT.Abs).then_inc(S["z_abs"], 1)
                act.wait_ge(S["z_abs"], b + 1)
                act.activation(t1[:], t1[:], ACT.Exp, scale=-1.0).then_inc(S["soft1"], 1)
                act.wait_ge(S["soft1"], b + 1)
                act.activation(t1[:], t1[:], ACT.Ln, bias=1.0).then_inc(S["soft2"], 1)

            def body(pair, e, more):
                b = pair * 2 + e
                act.wait_ge(S["s_bias"], b + 1)
                act.activation(pr[:], s, ACT.Exp, bias=peak, scale=MLA_SCALE, accum_out=total).then_inc(S["p_exp"], 1)
                act.wait_ge(S["logit_kept"], b + 1)
                act.activation(t2[:], t2[:], ACT.Exp).then_inc(S["a_ready"], 1)
                if more:
                    evacuate(act, copy, 0, pair, e, range(KV), more)
                evacuate(act, copy, 0, pair, e, (KV, KV + 1), more)
                act.wait_ge(S["ol_psum"], b + 1)
                act.activation(olatT[:, :, :, bass.ds(b * STEP, STEP)],
                               PS[:, 7, 0:CK * P].rearrange("p (c h q) -> p c h q", c=CK, h=H), ACT.Copy).then_inc(S["ol_out"], 1)
                if more:
                    softplus(b + 1)
                evacuate(act, copy, 0, pair, e, (KV + 2, KV + 3), more)

            softplus(0)
            loop(act, body)

        @block.tensor
        def _(pe):
            def turn_piece(out, ins, bank, before):
                pe.wait_ge(turn[bank], before)
                for k, (o, i, idn) in enumerate(zip(out, ins, [ident] * len(ins))):
                    mm = pe.transpose(o, i, idn)
                mm.then_inc(S["turned"], 1)

            def caches(e, count, bank_of, before):
                for n in range(KV):
                    bank = bank_of(n)
                    if n < CQ:
                        src, arrived, rows, width = kc[e], "kc_in", P, slice(n * P, (n + 1) * P)
                    elif n < CQ + CK:
                        src, arrived, rows, width = cc[e], "cc_in", P, slice((n - CQ) * P, (n - CQ + 1) * P)
                    else:
                        src, arrived, rows, width = kr[e], "kr_in", QK, slice(0, QK)
                    pe.wait_ge(IN[arrived][e], count)
                    turn_piece([PS[0:rows, 4 + bank, k * P:(k + 1) * P] for k in range(KBLK)],
                               [src[:, k, width] for k in range(KBLK)], bank, before(n))

            caches(0, 16, lambda n: n % 2, lambda n: n // 2 + 1)
            pe.wait_ge(turn[0], (KV + 1) // 2 + 1)
            pe.wait_ge(turn[1], KV // 2 + 1)

            def scores(b):
                pe.wait_ge(S["qblk_ready"], b + 1)
                for c in range(CQ):
                    pe.matmul(flat[:, 0:PAST], qblk[:, c, :], keyT[:, c, :], start=c == 0, stop=c == CQ - 1)
                for c in range(CQ):
                    mm = pe.matmul(flat[:, PAST:PAST + WIDE], qblk[:, c, :], wide(kT[:, c, new_cols(b)]), start=c == 0, stop=c == CQ - 1)
                mm.then_inc(S["z_psum"], 1)
                pe.wait_ge(S["q_ready"], (b + 1) * 2)
                for c in range(CK):
                    pe.matmul(s[:, 0:PAST], qabs[:, c, :], latT[:, c, :], start=c == 0, stop=False)
                pe.matmul(s[:, 0:PAST], qrot[:], rotT[:], start=False, stop=True)
                for c in range(CK):
                    pe.matmul(s_new, qabs[:, c, :], wide(ckvT[:, c, new_cols(b)]), start=c == 0, stop=False)
                pe.matmul(s_new, qrot[:], wide(krT[:, bass.ds(b * STEP, STEP)]), start=False, stop=True).then_inc(S["s_psum"], 1)

            scores(0)

            def body(pair, e, more):
                b = pair * 2 + e
                if more:
                    caches(1 - e, pair * 16 + 16 * (e + 1), lambda n: parity(e, n, more), lambda n: before(pair, e, n, more))
                for w, (src, need) in enumerate(((pr, "p_ready"), (t2, "a_ready"))):
                    if w and more:
                        pe.wait_ge(S["logit"], b + 1)
                        scores(b + 1)
                    pe.wait_ge(S[need], b + 1)
                    n = KV + 2 * w
                    bank = parity(e, n, more)
                    turn_piece([PS[:, 4 + bank, k * P:(k + 1) * P] for k in range(KBLK)],
                               [src[:, k * P:(k + 1) * P] for k in range(KBLK)], bank, before(pair, e, n, more))
                    turn_piece([PS[0:STEP, 5 - bank, 0:P]], [src[:, PAST:KEYS]], 1 - bank, before(pair, e, n + 1, more))
                    pe.wait_ge(turn[bank], before(pair, e, n, more) + 1)
                    pe.wait_ge(turn[1 - bank], before(pair, e, n + 1, more) + 1)
                    if w == 0:
                        pe.wait_ge(IN["new_in"][e], pair * 32 + 32)
                        pe.wait_ge(S["ol_out"], b + 1)
                        for c in range(CK):
                            for k in range(KBLK + 1):
                                v = cc[e][:, k, c * P:(c + 1) * P] if k < KBLK else cnew[e][:, c * P:(c + 1) * P]
                                mm = pe.matmul(PS[:, 7, c * P:(c + 1) * P], v, pT[:, k, :], start=k == 0, stop=k == KBLK)
                        mm.then_inc(S["ol_psum"], 1)
                    else:
                        pe.wait_ge(IN["vc_in"][e], pair * 16 + 16)
                        pe.wait_ge(S["os_out"], b + 1)
                        for c in range(CQ):
                            for k in range(KBLK + 1):
                                v = vc[e][:, k, c * P:(c + 1) * P] if k < KBLK else vnew[e][:, c * P:(c + 1) * P]
                                mm = pe.matmul(PS[:, 6, c * P:(c + 1) * P], v, aT[:, k, :], start=k == 0, stop=k == KBLK)
                        mm.then_inc(S["os_psum"], 1)

            loop(pe, body)
            pe.wait_ge(S["ol_out"], NSEQ + 1)
            pe.wait_ge(S["wuv_in"], 16)
            for h in range(H):
                rows = slice((h % 2) * HD, (h % 2 + 1) * HD)
                for c in range(CK):
                    mm = pe.matmul(PS[rows, 4, h // 2 * P:(h // 2 + 1) * P], wuv[:, c, h * HD:(h + 1) * HD], olatT[:, c, h, :],
                                   start=c == 0, stop=c == CK - 1)
            mm.then_inc(S["om_psum"], 1)

        @block.vector
        def _(dve):
            def copy(dst, src):
                return dve.tensor_copy(dst, src)

            def queries(b):
                for j in range(2):
                    rows = slice(j * HD, (j + 1) * HD)
                    diag = qblk[rows].rearrange("p c (h q) -> p (c h) q", q=STEP)[:, j::H + 2, :]
                    ins = dve.tensor_copy(diag, qT[rows, :, new_cols(b)])
                    if j:
                        ins.then_inc(S["qblk_ready"], 1)
                dve.tensor_copy(qabs[:].rearrange("p c (h q) -> p c h q", q=STEP), qabsT[:, :, :, bass.ds(b * STEP, STEP)]).then_inc(S["q_ready"], 1)
                dve.tensor_copy(qrot[:].rearrange("p (h q) -> p h q", q=STEP), qmT[:, :, new_cols(b)]).then_inc(S["q_ready"], 1)

            dve.sem_inc(turn[1], 1)
            dve.sem_inc(S["os_out"], 1)
            dve.wait_ge(S["zeroed"], 9)
            queries(0)
            evacuate_first(dve, copy, 1)

            def weights(b, weights_turned):
                dve.wait_ge(S["s_psum"], b + 1)
                dve.tensor_reduce(peak, s, AX_X, ALU.max).then_inc(S["s_peak"], 1)
                dve.wait_ge(S["s_peak"], b + 1)
                dve.tensor_scalar(peak, peak, -MLA_SCALE, None, ALU.mult).then_inc(S["s_bias"], 1)
                dve.wait_ge(S["soft2"], b + 1)
                dve.scalar_tensor_tensor(out=t1[:], in0=z, scalar=0.0, in1=t1[:], op0=ALU.max, op1=ALU.add).then_inc(S["soft"], 1)
                dve.wait_ge(S["p_exp"], b + 1)
                dve.reciprocal(inverse, total).then_inc(S["p_inv"], 1)
                dve.wait_ge(S["p_inv"], b + 1)
                dve.tensor_scalar(pr[:], pr[:], inverse, None, ALU.mult).then_inc(S["p_ready"], 1)
                dve.wait_ge(S["soft_kept"], b + 1)
                if weights_turned is not None:
                    dve.wait_ge(S["turned"], weights_turned)
                dve.tensor_tensor_scan(t2[:, ::-1], C["ones"][:, 0:1].broadcast_to((P, KEYS)), t1[:, ::-1], 0.0, ALU.mult, ALU.add).then_inc(S["tail"], 1)
                dve.wait_ge(S["tail"], b + 1)
                dve.tensor_tensor(t2[:], z, t2[:], ALU.subtract).then_inc(S["logit"], 1)

            weights(0, None)

            def body(pair, e, more):
                b = pair * 2 + e
                if more:
                    evacuate(dve, copy, 1, pair, e, range(KV), more)
                    queries(b + 1)
                evacuate(dve, copy, 1, pair, e, range(KV, PER), more)
                if more:
                    weights(b + 1, pair * (2 * PER) + (KV + PER * (e + 1)))
                dve.wait_ge(S["os_psum"], b + 1)
                for j in range(2):
                    rows = slice(j * HD, (j + 1) * HD)
                    own = PS[rows, 6, :].rearrange("p (c q) -> p c q", q=STEP)[:, j::H + 2, :]
                    ins = dve.tensor_copy(osT[rows, :, new_cols(b)], own)
                ins.then_inc(S["os_out"], 1)

            loop(dve, body)
            dve.wait_ge(S["om_psum"], 1)
            dve.tensor_copy(omT[:, :, SEQ:N], PS[:, 4, :].rearrange("p (c n) -> p c n", c=CQ)).then_inc(S["om_out"], 1)


def phase_merge(nc, A, env):
    sb, sem, PS, C, ident = (env[k] for k in ("sb", "sem", "PS", "C", "ident"))
    vecT, adaT, coef, stat, x, hT, osT, omT = (env[k] for k in ("vecT", "adaT", "coef", "stat", "x", "hT", "osT", "omT"))
    CW = SBW // P
    wout = sb("wout", 66, [P, KD, D])
    wq = [sb(f"wq{k}", 66 + 8 * k, [P, NQ * P]) for k in range(KD)]
    y = sb("y", 159, [P, NT, D])
    gated = sb("gated", 159, [P, 2, KD, NC_])
    per_query = sb("per_query", 179, [P, 2, KD, P])
    xn = [sb(f"xm{i}", 179 + 4 * i, [P, D]) for i in range(2)]
    sq = sb("sq", 187, [P, 2 * CW, N])
    junk = sq[:].rearrange("p c n -> p (c n)")[:, 0:D]
    gmix, gffn = sb("gmix", 10, [P, 2, D]), sb("gffn", 18, [P, 2, D])
    env["env"].update(gffn=gffn, wq=wq)
    names = ("squared scaled ss_psum g_var g_sqrt g_rstd oa_psum ob_psum ya_ready y_ready y_sq y_var y_sqrt y_rstd "
             "gated row_psum row_ready mixed x1_ready x_sq x_var x_sqrt x_rstd xn_ready xT_psum h_ready step").split()
    S = {n: sem("mg_" + n) for n in names}
    wout_in = [sem(f"mg_wout_in{k}") for k in range(2)]
    wq_in = sem("mg_wq_in")
    groups = ((osT, "g_sb_out"), (omT, "g_mla_out"))

    with nc.Block() as block:
        @block.sync
        def _(sp):
            for k in range(2):
                sp.dma_start(wout[:, 4 * k:4 * k + 4, :], A["w_out"][0, 4 * k * P:4 * (k + 1) * P].rearrange("(k p) m -> p k m", p=P)
                             ).then_inc(wout_in[k], 16)
            for k in range(KD // 2, KD):
                sp.dma_start(wq[k][:], A["w_peer_q"][0, k * P:(k + 1) * P, :]).then_inc(wq_in, 16)
            sp.wait_ge(S["ob_psum"], NT)
            for k in range(KD // 2):
                sp.dma_start(wq[k][:], A["w_peer_q"][0, k * P:(k + 1) * P, :]).then_inc(wq_in, 16)
            sp.wait_ge(wq_in, 16 * KD)

        @block.gpsimd
        def _(pool):
            pass

        @block.scalar
        def _(act):
            for g, (o, _) in enumerate(groups):
                act.activation(sq[:, g * CW:(g + 1) * CW, :], o[:], ACT.Square).then_inc(S["squared"], 1)
            for i in range(4):
                act.wait_ge(S["row_psum"], i + 1)
                act.activation((gmix, gffn)[i // 2][:, i % 2, :].rearrange("p (b n) -> p b n", b=2),
                               PS[:, 4:6, :] if i % 2 else PS[:, 6:8, :], ACT.Copy).then_inc(S["row_ready"], 1)
            act.wait_ge(S["g_var"], 1)
            act.activation(stat[:, 0, 0:2 * NT], stat[:, 0, 0:2 * NT], ACT.Sqrt).then_inc(S["g_sqrt"], 1)
            act.wait_ge(S["g_rstd"], 1)

            def attention_half(t):
                act.wait_ge(S["oa_psum"], t + 1)
                act.activation(y[:, t, :].rearrange("p (b n) -> p b n", b=2), PS[:, 0:2, :], ACT.Copy,
                               scale=stat[:, 1, 2 * t:2 * t + 1]).then_inc(S["ya_ready"], 1)

            def mean_square(src, row, t, ready, count, squared, var, sqrt):
                act.wait_ge(S[ready], t + 1)
                if count:
                    act.wait_ge(S[count[0]], count[1])
                act.activation(junk, src, ACT.Square, accum_out=stat[:, row, t:t + 1]).then_inc(S[squared], 1)
                act.wait_ge(S[var], t + 1)
                act.activation(stat[:, row, t:t + 1], stat[:, row, t:t + 1], ACT.Sqrt).then_inc(S[sqrt], 1)

            attention_half(0)
            for t in range(NT):
                mean_square(y[:, t, :], 2, t, "y_ready", ("x_sq", t) if t else ("ss_psum", 1), "y_sq", "y_var", "y_sqrt")
                mean_square(x[:, t, :], 4, t, "x1_ready", ("y_sq", t + 1), "x_sq", "x_var", "x_sqrt")
                act.wait_ge(S["x_rstd"], t + 1)
                if t >= 2:
                    act.wait_ge(S["xT_psum"], 2 * (t - 1))
                act.activation(xn[t % 2][:], x[:, t, :], ACT.Copy, scale=stat[:, 5, t:t + 1]).then_inc(S["xn_ready"], 1)
                if t + 1 < NT:
                    attention_half(t + 1)

        @block.tensor
        def _(pe):
            pe.wait_ge(S["gated"], 4)
            for i in range(4):
                if i >= 2:
                    pe.wait_ge(S["row_ready"], i - 1)
                for k in range(KD):
                    per_token = gated[:, i // 2, k, 0:1].broadcast_to((P, P)) if i % 2 == 0 else per_query[:, i // 2, k, :]
                    bank = (6 if i % 2 == 0 else 4) + k // 4
                    mm = pe.matmul(PS[:, bank, (k % 4) * P:(k % 4 + 1) * P], per_token, ident, start=True, stop=True)
                mm.then_inc(S["row_psum"], 1)
            pe.wait_ge(S["squared"], 2)
            for t in range(NT):
                for g in range(2):
                    for c in range(CW):
                        mm = pe.matmul(PS[:, 0, 2 * t + g:2 * t + g + WIDE], sq[:, g * CW + c, t * P:(t + 1) * P],
                                       C["ones"][:, 0:1].broadcast_to((P, WIDE)),
                                       start=c == 0, stop=c == CW - 1)
            mm.then_inc(S["ss_psum"], 1)

            def project(t):
                for g, (o, _) in enumerate(groups):
                    if t == 0:
                        pe.wait_ge(wout_in[g], 16)
                        pe.wait_ge(S["scaled"], CW * (g + 1))
                        if g == 0:
                            pe.wait_ge(S["g_var"], 1)
                    else:
                        pe.wait_ge(S[("ya_ready", "y_ready")[g]], t)
                    for b in range(2):
                        for c in range(CW):
                            mm = pe.matmul(PS[:, 2 * g + b, :], o[:, c, t * P:(t + 1) * P], wout[:, g * CW + c, b * 512:(b + 1) * 512],
                                           start=c == 0, stop=c == CW - 1)
                    mm.then_inc(S[("oa_psum", "ob_psum")[g]], 1)

            def turn(t):
                pe.wait_ge(S["xn_ready"], t + 1)
                if t == 0:
                    pe.wait_ge(S["row_ready"], 4)
                for b in range(2):
                    if t >= 2:
                        pe.wait_ge(S["h_ready"], 2 * (t - 2) + b + 1)
                    for j in range(4):
                        k = 4 * b + j
                        mm = pe.transpose(PS[:, 4 + 2 * (t % 2) + b, j * P:(j + 1) * P], xn[t % 2][:, k * P:(k + 1) * P], ident)
                    mm.then_inc(S["xT_psum"], 1)

            for t in range(NT):
                project(t)
                if t:
                    turn(t - 1)
            turn(NT - 1)

        @block.vector
        def _(dve):
            step = Step(dve, S["step"])
            for i, (row, name) in enumerate(((GT1, "g_mix_post"), (GT2, "g_ffn_post"))):
                gain = vecT[:, VROW[name]:VROW[name] + KD].unsqueeze(2).broadcast_to((P, KD, NC_))
                dve.tensor_tensor(gated[:, i], adaT[:, row:row + KD, :], gain, ALU.mult).then_inc(S["gated"], 1)
            dve.wait_ge(S["gated"], 2)
            for i in range(2):
                dve.tensor_copy(per_query[:, i].rearrange("p k (s q) -> p k s q", q=STEP),
                                gated[:, i, :, 1:NC_].unsqueeze(3).broadcast_to((P, KD, NSEQ, STEP))).then_inc(S["gated"], 1)
            dve.wait_ge(S["squared"], 2)
            for o, name in groups:
                for c in range(CW):
                    g = vecT[:, VROW[name] + c:VROW[name] + c + 1]
                    dve.tensor_scalar(o[:, c, :], o[:, c, :], g, None, ALU.mult).then_inc(S["scaled"], 1)
            dve.wait_ge(S["ss_psum"], 1)
            dve.tensor_scalar(stat[:, 0, 0:2 * NT], PS[:, 0, 0:2 * NT], 1.0 / SBW, EPS, ALU.mult, ALU.add).then_inc(S["g_var"], 1)
            dve.wait_ge(S["g_sqrt"], 1)
            dve.reciprocal(stat[:, 1, 0:2 * NT], stat[:, 0, 0:2 * NT]).then_inc(S["g_rstd"], 1)
            dve.wait_ge(S["g_rstd"], 1)

            def factor(row, t, squared, var, sqrt, done):
                dve.wait_ge(S[squared], t + 1)
                dve.tensor_scalar(stat[:, row, t:t + 1], stat[:, row, t:t + 1], 1.0 / D, EPS, ALU.mult, ALU.add).then_inc(S[var], 1)
                dve.wait_ge(S[sqrt], t + 1)
                dve.reciprocal(stat[:, row + 1, t:t + 1], stat[:, row, t:t + 1]).then_inc(S[done], 1)

            def shifted(t):
                for b in range(2):
                    dve.wait_ge(S["xT_psum"], 2 * t + b + 1)
                    modulate(dve, step, hT, PS[:, 4 + 2 * (t % 2) + b, :], coef[:, 1], adaT[:, SH2:SH2 + KD, :], t, b, S["h_ready"])

            for t in range(NT):
                dve.wait_ge(S["ob_psum"], t + 1)
                dve.wait_ge(S["ya_ready"], t + 1)
                v = y[:, t, :].rearrange("p (b n) -> p b n", b=2)
                dve.scalar_tensor_tensor(out=v, in0=PS[:, 2:4, :], scalar=stat[:, 1, 2 * t + 1:2 * t + 2], in1=v,
                                         op0=ALU.mult, op1=ALU.add).then_inc(S["y_ready"], 1)
                factor(2, t, "y_sq", "y_var", "y_sqrt", "y_rstd")
                dve.wait_ge(S["y_rstd"], t + 1)
                dve.wait_ge(S["row_ready"], 2)
                dve.scalar_tensor_tensor(out=y[:, t, :], in0=y[:, t, :], scalar=stat[:, 3, t:t + 1], in1=gmix[:, int(t >= PT), :],
                                         op0=ALU.mult, op1=ALU.mult).then_inc(S["mixed"], 1)
                dve.wait_ge(S["mixed"], t + 1)
                dve.tensor_tensor(x[:, t, :], x[:, t, :], y[:, t, :], ALU.add).then_inc(S["x1_ready"], 1)
                factor(4, t, "x_sq", "x_var", "x_sqrt", "x_rstd")
                if t:
                    shifted(t - 1)
            shifted(NT - 1)


def phase_keys(nc, A, env):
    sb, sem, PS, C, ident = (env[k] for k in ("sb", "sem", "PS", "C", "ident"))
    hT = env["hT"]
    wq = env["wq"]
    qp = [sb(f"qp{i}", 130 + 8 * i, [P, NQ, P]) for i in range(2)]
    sc = [sb(f"sc{i}", 162 + 8 * i, [P, NQ, NKEYS]) for i in range(2)]
    SHORT = TOPK // 2
    NCAND = TOPK + (SHORT - 1) * SHORT + SHORT
    cand = sb("cand", 178, [P, H, NCAND])
    skey = sb("skey", 186, [P, 2, P])
    rest = sb("rest", 187, [P, NQ * NKEYS])
    hot = sb("hot", 187, [P, H, TOPK, TOPK])
    pick = sb("pick", 195, [P, NT, 3, H * TOPK])
    top = sb("top", 203, [P, NQ, TOPK])
    topi = sb("topi", 204, [P, NQ, TOPK], U32)
    topf = sb("topf", 205, [P, NQ, TOPK])
    best = sb("best", 206, [P, H, TOPK])
    besti = sb("besti", 206.5, [P, 2, H, TOPK], U32)
    sel = sb("sel", 10, [P, 3, N])
    rank = sb("rank", 146, [P, 2, H * TOPK])
    place, work = sb("place", 147, [P, H * TOPK]), sb("work", 147.5, [P, 2, H * TOPK])
    flat_stat = env["stat"][:].rearrange("p a b -> p (a b)")
    total, peak = flat_stat[:, 0:NT * H], flat_stat[:, 64:64 + H]
    env["env"].update(sel=sel)
    names = "sk_psum sk_ready q_psum q_ready s_psum s_ready topped ranked gate_exp gates sel_psum sel_ready0 sel_ready1 step".split()
    S = {n: sem("pk_" + n) for n in names}
    sk_in = sem("pk_sk_in")

    with nc.Block() as block:
        @block.sync
        def _(sp):
            sp.dma_start(skey[:, 0, :], A["sub_keys_1"][0]).then_inc(sk_in, 16)
            sp.dma_start(skey[:, 1, :], A["sub_keys_2"][0]).then_inc(sk_in, 16)

        @block.scalar
        def _(act):
            act.wait_ge(S["sk_psum"], 1)
            act.activation(skey[:].rearrange("p i n -> p (i n)"), PS[:, 7, 0:2 * P], ACT.Copy).then_inc(S["sk_ready"], 1)
            for t in range(NT):
                for m in range(NQ // 4):
                    act.wait_ge(S["q_psum"], t * (NQ // 4) + m + 1)
                    if t >= 2:
                        act.wait_ge(S["s_psum"], 4 * (t - 1))
                    act.activation(qp[t % 2][:, 4 * m:4 * m + 4, :], PS[:, m % 2, :].rearrange("p (m n) -> p m n", m=4), ACT.Copy
                                   ).then_inc(S["q_ready"], 1)
                if t >= 2:
                    act.wait_ge(S["topped"], t - 1)
                for g in range(4):
                    act.wait_ge(S["s_psum"], 4 * t + g + 1)
                    act.activation(sc[t % 2][:, 4 * g:4 * g + 4, :], PS[:, 2 + g, :].rearrange("p (m e) -> p m e", e=NKEYS),
                                   ACT.Copy).then_inc(S["s_ready"], 1)
            act.wait_ge(S["ranked"], NT)
            act.activation(pick[:, :, 2, :], pick[:, :, 2, :], ACT.Exp).then_inc(S["gate_exp"], 1)
            for t in range(1, NT, 2):
                act.wait_ge(S["sel_psum"], t + 1)
                act.activation(sel[:, :, t * P:(t + 1) * P], PS[:, 7, 0:3 * P].rearrange("p (i n) -> p i n", i=3), ACT.Copy
                               ).then_inc(S["sel_ready1"], 1)

        @block.tensor
        def _(pe):
            pe.wait_ge(sk_in, 32)
            for i in range(2):
                mm = pe.transpose(PS[:, 7, i * P:(i + 1) * P], skey[:, i, :], ident)
            mm.then_inc(S["sk_psum"], 1)
            for t in range(NT):
                cols = slice(t * P, (t + 1) * P)
                for m in range(NQ):
                    i = (t * NQ + m) // 4
                    if i >= 2 and m % 4 == 0:
                        pe.wait_ge(S["q_ready"], i - 1)
                    for k in range(KD):
                        mm = pe.matmul(PS[:, (m // 4) % 2, (m % 4) * P:(m % 4 + 1) * P], wq[k][:, m * P:(m + 1) * P], hT[:, k, cols],
                                       start=k == 0, stop=k == KD - 1)
                    if m % 4 == 3:
                        mm.then_inc(S["q_psum"], 1)
                pe.wait_ge(S["q_ready"], (t + 1) * (NQ // 4))
                for g in range(4):
                    if t:
                        pe.wait_ge(S["s_ready"], 4 * (t - 1) + g + 1)
                    elif g == 0:
                        pe.wait_ge(S["sk_ready"], 1)
                    for j in range(4):
                        m = 4 * g + j
                        mm = pe.matmul(PS[:, 2 + g, j * P:(j + 1) * P], qp[t % 2][:, m, :], skey[:, m % 2, :], start=True, stop=True)
                    mm.then_inc(S["s_psum"], 1)
            pe.wait_ge(S["gates"], 1)
            for t in range(NT):
                if t >= 2:
                    pe.wait_ge(S[f"sel_ready{t % 2}"], t // 2)
                for i in range(3):
                    mm = pe.transpose(PS[:, 6 + t % 2, i * P:(i + 1) * P], pick[:, t, i, :], ident)
                mm.then_inc(S["sel_psum"], 1)

        @block.vector
        def _(dve):
            step = Step(dve, S["step"])

            def sync(ins):
                step(ins)
                step.wait()

            def top16(values, width, out, index, count):
                spare = rest[:, 0:count * width].rearrange("p (m e) -> p m e", m=count)
                for m in range(count):
                    step(dve.max(out[:, m, 0:8], values[:, m, :]))
                step.wait()
                for m in range(count):
                    step(dve.max_index(index[:, m, 0:8], out[:, m, 0:8], values[:, m, :]))
                    step(dve.match_replace(spare[:, m, :], out[:, m, 0:8], values[:, m, :], NEG))
                step.wait()
                for m in range(count):
                    step(dve.max(out[:, m, 8:16], spare[:, m, :]))
                step.wait()
                for m in range(count):
                    ins = dve.max_index(index[:, m, 8:16], out[:, m, 8:16], spare[:, m, :])
                return ins

            for t in range(NT):
                dve.wait_ge(S["s_ready"], 4 * (t + 1))
                top16(sc[t % 2], NKEYS, top, topi, NQ).then_inc(S["topped"], 1)
                dve.wait_ge(S["topped"], t + 1)
                step(dve.tensor_copy(topf[:], topi[:]))
                pairs = top[:].rearrange("p (h i) k -> p h i k", i=2)
                one, two = pairs[:, :, 0, :], pairs[:, :, 1, :]
                step(dve.tensor_tensor(cand[:, :, 0:TOPK], one[:, :, 0:1].broadcast_to((P, H, TOPK)), two, ALU.add))
                rows = cand[:, :, TOPK:TOPK + (SHORT - 1) * SHORT].rearrange("p h (a b) -> p h a b", b=SHORT)
                step(dve.tensor_tensor(rows, one[:, :, 1:SHORT].unsqueeze(3).broadcast_to((P, H, SHORT - 1, SHORT)),
                                       two[:, :, 0:SHORT].unsqueeze(2).broadcast_to((P, H, SHORT - 1, SHORT)), ALU.add))
                sync(dve.tensor_tensor(cand[:, :, NCAND - SHORT:], one[:, :, SHORT:], two[:, :, 0:1].broadcast_to((P, H, SHORT)), ALU.add))
                sync(top16(cand, NCAND, best, besti[:, 0], H))
                step(dve.tensor_copy(peak, best[:, :, 0]))
                flat = besti[:, 0].rearrange("p h k -> p (h k)")
                eighth = besti[:, 1].rearrange("p h k -> p (h k)")
                step(dve.tensor_copy(place[:], flat))
                sync(dve.tensor_scalar(eighth, flat, 3, None, ALU.logical_shift_right))
                sync(dve.tensor_copy(work[:, 0, :], eighth))
                dve.tensor_tensor(pick[:, t, 2, :].rearrange("p (h k) -> p h k", h=H), best[:], peak.unsqueeze(2).broadcast_to((P, H, TOPK)),
                                  ALU.subtract).then_inc(S["ranked"], 1)
                sync(dve.tensor_scalar(work[:, 0, :], work[:, 0, :], -1.0, 0.0, ALU.add, ALU.max))
                sync(dve.scalar_tensor_tensor(out=rank[:, 0, :], in0=place[:], scalar=float(SHORT - (NCAND - SHORT)), in1=work[:, 0, :],
                                              op0=ALU.add, op1=ALU.max))
                sync(dve.tensor_scalar(work[:, 0, :], rank[:, 0, :], 1.0, float(SHORT), ALU.min, ALU.mult))
                sync(dve.scalar_tensor_tensor(out=work[:, 1, :], in0=rank[:, 0, :], scalar=float(SHORT), in1=work[:, 0, :],
                                              op0=ALU.mult, op1=ALU.add))
                sync(dve.tensor_tensor(work[:, 1, :], place[:], work[:, 1, :], ALU.subtract))
                sync(dve.tensor_scalar(rank[:, 1, :], work[:, 1, :], 0.0, None, ALU.max))
                keys = topf[:].rearrange("p (h i) k -> p h i k", i=2)
                for i in range(2):
                    sync(dve.tensor_tensor(hot[:].rearrange("p h k m -> p (h k) m"), rank[:, i, :].unsqueeze(2).broadcast_to((P, H * TOPK, TOPK)),
                                           C["slot"].unsqueeze(1).broadcast_to((P, H * TOPK, TOPK)), ALU.is_equal))
                    sync(dve.tensor_tensor(hot[:], hot[:], keys[:, :, i, :].unsqueeze(2).broadcast_to((P, H, TOPK, TOPK)), ALU.mult))
                    sync(dve.tensor_reduce(pick[:, t, i, :].rearrange("p (h k) -> p h k", h=H), hot[:], AX_X, ALU.add))
            dve.wait_ge(S["gate_exp"], 1)
            gate = pick[:, :, 2, :].rearrange("p t (h k) -> p t h k", h=H)
            totals = total.rearrange("p (t h) -> p t h", h=H)
            sync(dve.tensor_reduce(totals, gate, AX_X, ALU.add))
            sync(dve.reciprocal(total, total))
            dve.tensor_tensor(gate, gate, totals.unsqueeze(3).broadcast_to((P, NT, H, TOPK)), ALU.mult).then_inc(S["gates"], 1)
            for t in range(0, NT, 2):
                dve.wait_ge(S["sel_psum"], t + 1)
                dve.tensor_copy(sel[:, :, t * P:(t + 1) * P], PS[:, 6, 0:3 * P].rearrange("p (i n) -> p i n", i=3)).then_inc(S["sel_ready0"], 1)


TB = 64


def phase_gates(nc, A, env):
    sb, sem, PS, C, sel = (env[k] for k in ("sb", "sem", "PS", "C", "sel"))
    hT = env["hT"]
    stage = [sb(f"stage{i}", 138 + 32 * i, [P, NKEYS, TB]) for i in range(2)]
    G = 4
    first = [sb(f"first{i}", 66 + 2 * i, [P, G, NKEYS]) for i in range(G)]
    second = [sb(f"second{i}", 74 + 2 * i, [P, G, NKEYS]) for i in range(G)]
    h = [sb("h_hi", 86, [P, KD, N], F32R), sb("h_lo", 46, [P, KD, N], F32R)]
    u = [sb(f"u{i}", 106 + 4 * i, [P, D]) for i in range(4)]
    env["env"].update(h=h, u=u)
    h_split, u_in = sem("gt_h_split"), sem("gt_u_in")
    S = {n: sem("gt_" + n) for n in "marked hot_ready weighed hot_used table_ready".split()}
    stored = [nc.alloc_semaphore(f"gates_stored{i}") for i in range(2)]
    env["env"].update(gates_stored=stored)
    BLOCKS, INNER = N // TB, TB // (G * G)
    PB = INNER * G

    def loop(eng, body, edge=None):
        def groups(pair, e, i, last):
            for g in range(G):
                body(pair * (2 * PB) + i * G + (e * PB + g), g, e, i * (G * G) + g * G, pair * (2 * TB) + i * (G * G) + (e * TB + g * G),
                     last and g == G - 1)

        def block_of_tokens(pair, e, last):
            if edge:
                edge(pair, e)
            with eng.Fori(0, INNER - int(last)) as i:
                groups(pair, e, i, False)
            if last:
                groups(pair, e, INNER - 1, True)

        with eng.Fori(0, BLOCKS // 2 - 1) as pair:
            for e in range(2):
                block_of_tokens(pair, e, False)
        for e in range(2):
            block_of_tokens(BLOCKS // 2 - 1, e, e == 1)

    with nc.Block() as block:
        @block.sync
        def _(sp):
            for i in range(len(u)):
                sp.dma_start(u[i][:], A["u_experts"][0, i * P:(i + 1) * P, :]).then_inc(u_in, 16)
            with sp.Fori(0, BLOCKS // 2) as pair:
                for e in range(2):
                    sp.wait_ge(S["table_ready"], pair * (2 * PB) + (e + 1) * PB + G)
                    sp.dma_start(A["gates"][pair * 2 + e], stage[e][:]).then_inc(stored[e], 16)
            sp.wait_ge(u_in, 16 * len(u))

        @block.gpsimd
        def _(pool):
            pool.tensor_copy(h[0][:], hT[:]).then_inc(h_split, 1)
            pool.wait_ge(h_split, 1)
            pool.tensor_tensor(h[1][:], hT[:], h[0][:], ALU.subtract).then_inc(h_split, 1)

        @block.vector
        def _(dve):
            def body(n, g, e, at, token, last):
                dve.wait_ge(S["hot_used"], n + 1)
                dve.tensor_tensor(first[g][:, 0:G - 1, :], C["iota"].unsqueeze(1).broadcast_to((P, G - 1, NKEYS)),
                                  sel[:, 0, bass.ds(token, G - 1)].unsqueeze(2).broadcast_to((P, G - 1, NKEYS)), ALU.is_equal
                                  ).then_inc(S["marked"], 1)
                col = bass.ds(token + (G - 1), 1)
                dve.tensor_scalar(first[g][:, G - 1, :], C["iota"], sel[:, 0, col], sel[:, 2, col], ALU.is_equal, ALU.mult)
                dve.tensor_tensor(second[g][:], C["iota"].unsqueeze(1).broadcast_to((P, G, NKEYS)),
                                  sel[:, 1, bass.ds(token, G)].unsqueeze(2).broadcast_to((P, G, NKEYS)), ALU.is_equal
                                  ).then_inc(S["hot_ready"], 1)

            loop(dve, body)

        @block.tensor
        def _(pe):
            pe.sem_inc(S["hot_used"], G)

            def body(n, g, e, at, token, last):
                pe.wait_ge(S["hot_ready"], n + 1)
                pe.wait_ge(S["weighed"], n + 1)
                pe.wait_ge(S["table_ready"], n + 1)
                for j in range(G):
                    mm = pe.matmul(PS[:, g, j * NKEYS:(j + 1) * NKEYS], second[g][:, j, :], first[g][:, j, :], start=True, stop=True)
                mm.then_inc(S["hot_used"], 1)

            loop(pe, body)

        @block.scalar
        def _(act):
            act.sem_inc(S["table_ready"], G)
            for e in range(2):
                act.sem_inc(stored[e], 16)

            def edge(pair, e):
                act.wait_ge(stored[e], pair * 16 + 16)

            def weigh(n, g, token):
                act.wait_ge(S["marked"], n + 1)
                for j in range(G - 1):
                    ins = act.activation(first[g][:, j, :], first[g][:, j, :], ACT.Copy, scale=sel[:, 2, bass.ds(token + j, 1)])
                ins.then_inc(S["weighed"], 1)

            def body(n, g, e, at, token, last):
                if not last:
                    weigh(n + 1, (g + 1) % G, token + G)
                act.wait_ge(S["hot_used"], n + G + 1)
                act.activation(stage[e][:, :, bass.ds(at, G)].rearrange("p i n -> p n i"), PS[:, g, :].rearrange("p (n i) -> p n i", n=G),
                               ACT.Copy).then_inc(S["table_ready"], 1)

            weigh(0, 0, 0)
            loop(act, body, edge)


def phase_experts(nc, A, env):
    sb, sem, PS, C, ident = (env[k] for k in ("sb", "sem", "PS", "C", "ident"))
    x, h, u, gffn, stat = (env[k] for k in ("x", "h", "u", "gffn", "stat"))
    GC = 2
    NCH = NEXP // P
    NG = NCH // GC
    PAIR = 2 * GC
    NPAIR = NCH // PAIR
    BLK = N // TB
    UR = len(u)
    assert UR == PAIR
    HI, LO = 0, 1
    uT = [[sb(f"uT_{'hl'[s]}{i}", (10, 122)[s] + 4 * i, [P, KD, P], F32R) for s in (HI, LO)] for i in range(2)]
    acc = sb("acc", 66, [P, NT, D])
    v = [[sb(f"v_{'hl'[s]}{i}", 130 + 16 * s + 8 * i, [P, GC, D], F32R) for s in (HI, LO)] for i in range(2)]
    a = [[sb(f"a_{'hl'[s]}{i}", 162 + 10 * s + 5 * i, [P, GC, N], F32R) for s in (HI, LO)] for i in range(2)]
    gt = [sb(f"gt{i}", 182 + 5 * i, [P, BLK, GC, TB]) for i in range(2)]
    gl = [sb(f"gl{i}", 192 + 2.5 * i, [P, 2, HALF]) for i in range(2)]
    vraw = [sb(f"vraw{i}", 197 + 4 * i, [P, D]) for i in range(2)]
    y = [sb(f"yo{i}", 106 + 4 * i, [P, D]) for i in range(2)]
    junk = sb("ej", 114, [P, D])
    names = ("uT_psum uT_hi uT_lo s_psum gelu weighed a_hi a_lo v_hi v_lo f_psum added f_sq f_var f_sqrt f_rstd scaled "
             "y_ready").split()
    S = {n: sem("ex_" + n) for n in names}
    u_in = [sem(f"ex_u_in{i}") for i in range(UR)]
    v_in, g_in = ([sem(f"ex_{n}_in{i}") for i in range(2)] for n in "vg")
    y_out = [sem(f"ex_y_out{i}") for i in range(2)]
    ADDS = 2 * NT
    y_dram = [A["y_p"][0, t * P:(t + 1) * P, :] for t in range(PT)] + [A["y_s"].rearrange("b q d -> (b q) d")]

    def pairs(eng, body):
        body(0, True, False)
        with eng.Fori(1, NPAIR - 1) as i:
            body(i, False, False)
        body(NPAIR - 1, False, True)

    with nc.Block() as block:
        @block.sync
        def _(sp):
            def body(i, first, last):
                for q in range(PAIR):
                    e, c = divmod(q, GC)
                    if not first:
                        sp.wait_ge(S["uT_psum"], i * (2 * PAIR) + 2 * (q + 1 - UR))
                        sp.dma_start(u[q][:], A["u_experts"][0, bass.ds(i * (PAIR * P) + q * P, P), :]).then_inc(u_in[q], 16)
                    if c == 0:
                        if first and e == 0:
                            for stored in env["gates_stored"]:
                                sp.wait_ge(stored, 16 * (BLK // 2 + 1))
                        if not first:
                            sp.wait_ge(S["weighed"], i * PAIR + (e - 1) * GC)
                        sp.dma_start(gt[e][:], A["gates"][:, :, bass.ds(i * PAIR + e * GC, GC), :].rearrange("b p c n -> p b c n")
                                     ).then_inc(g_in[e], 16)
                    if not (first and q < 2):
                        sp.wait_ge(S["v_lo"], i * PAIR + q - 1)
                    sp.dma_start(vraw[q % 2][:], A["v_experts"][0, bass.ds(i * (PAIR * P) + q * P, P), :]).then_inc(v_in[q % 2], 16)

            pairs(sp, body)
            for t in range(NT):
                sp.wait_ge(S["y_ready"], t + 1)
                sp.dma_start(y_dram[t], y[t % 2][:]).then_inc(y_out[t % 2], 16)
            sp.wait_ge(y_out[0], 16 * 3)
            sp.wait_ge(y_out[1], 16 * 2)

        @block.gpsimd
        def _(pool):
            def body(i, first, last):
                for q in range(PAIR):
                    e, c = divmod(q, GC)
                    pool.wait_ge(S["gelu"], i * PAIR + q + 1)
                    if c == 0:
                        pool.wait_ge(g_in[e], i * 16 + 16)
                    act_by_block = gl[q % 2][:].rearrange("p s n -> p (s n)").rearrange("p (b n) -> p b n", n=TB)
                    pool.tensor_tensor(act_by_block, act_by_block, gt[e][:, :, c, :], ALU.mult).then_inc(S["weighed"], 1)

            pairs(pool, body)

        @block.scalar
        def _(act):
            def turned(i, q):
                for b in range(2):
                    act.wait_ge(S["uT_psum"], i * (2 * PAIR) + 2 * q + b + 1)
                    act.activation(uT[q % 2][HI][:, 4 * b:4 * b + 4, :], PS[:, b, :].rearrange("p (k n) -> p k n", k=4), ACT.Copy
                                   ).then_inc(S["uT_hi"], 1)

            def body(i, first, last):
                if first:
                    turned(0, 0)
                for q in range(PAIR):
                    e, c = divmod(q, GC)
                    if not (last and q == PAIR - 1):
                        turned(i, q + 1)
                    act.wait_ge(v_in[q % 2], i * (16 * PAIR // 2) + 16 * (q // 2 + 1))
                    if c == 0 and not first:
                        act.wait_ge(S["f_psum"], i * (2 * ADDS) + (e - 1) * ADDS)
                    act.activation(v[e][HI][:, c, :], vraw[q % 2][:], ACT.Copy).then_inc(S["v_hi"], 1)
                    act.wait_ge(S["s_psum"], i * PAIR + q + 1)
                    if not (first and q < 2):
                        act.wait_ge(S["a_lo"], i * PAIR + q - 1)
                    act.activation(gl[q % 2][:], PS[:, 2 + 2 * (q % 2):4 + 2 * (q % 2), 0:HALF], ACT.Gelu).then_inc(S["gelu"], 1)
                    act.wait_ge(S["weighed"], i * PAIR + q + 1)
                    act.activation(a[e][HI][:, c, :], gl[q % 2][:].rearrange("p s n -> p (s n)"), ACT.Copy).then_inc(S["a_hi"], 1)

            pairs(act, body)
            for t in range(NT):
                act.wait_ge(S["added"], (NG - 1) * ADDS + 2 * (t + 1))
                if t:
                    act.wait_ge(S["f_sq"], t)
                act.activation(junk[:], acc[:, t, :], ACT.Square, accum_out=stat[:, 0, t:t + 1]).then_inc(S["f_sq"], 1)
            act.wait_ge(S["f_var"], 1)
            act.activation(stat[:, 0, 0:NT], stat[:, 0, 0:NT], ACT.Sqrt).then_inc(S["f_sqrt"], 1)

        @block.tensor
        def _(pe):
            PASSES = ((HI, HI), (HI, LO), (LO, HI))

            def turn(i, q, first, first_of_all=False):
                if not (first and q < UR):
                    pe.wait_ge(u_in[q % UR], i * 16 + 16 * (q // UR))
                for b in range(2):
                    if not first_of_all:
                        pe.wait_ge(S["uT_lo"], i * (2 * PAIR) + 2 * q - 1 + b)
                    for j in range(4):
                        k = 4 * b + j
                        mm = pe.transpose(PS[:, b, j * P:(j + 1) * P], u[q % UR][:, k * P:(k + 1) * P], ident)
                    mm.then_inc(S["uT_psum"], 1)

            def hidden(i, q, fresh):
                if not fresh:
                    pe.wait_ge(S["gelu"], i * PAIR + q - 1)
                for b in range(2):
                    for k in range(KD):
                        if b == 0 and k % (KD // 2) == 0:
                            pe.wait_ge(S["uT_lo"], i * (2 * PAIR) + 2 * q + 1 + k // (KD // 2))
                        for w, m in PASSES:
                            mm = pe.matmul(PS[:, 2 + 2 * (q % 2) + b, 0:HALF], uT[q % 2][w][:, k, :], h[m][:, k, b * HALF:(b + 1) * HALF],
                                           start=k == 0 and (w, m) == PASSES[0], stop=k == KD - 1 and (w, m) == PASSES[-1])
                mm.then_inc(S["s_psum"], 1)

            def outputs(i, e, before, fresh):
                pe.wait_ge(S["v_lo"], i * PAIR + (e + 1) * GC)
                pe.wait_ge(S["a_lo"], i * PAIR + (e + 1) * GC)
                for n in range(ADDS):
                    t, b = divmod(n, 2)
                    if not (fresh and n < 2):
                        pe.wait_ge(S["added"], before + (n - 1))
                    for c in range(GC):
                        for w, m in PASSES:
                            mm = pe.matmul(PS[:, 6 + b, :], a[e][w][:, c, t * P:(t + 1) * P], v[e][m][:, c, b * 512:(b + 1) * 512],
                                           start=c == 0 and (w, m) == PASSES[0], stop=c == GC - 1 and (w, m) == PASSES[-1])
                    mm.then_inc(S["f_psum"], 1)

            def body(i, first, last):
                if first:
                    turn(0, 0, True, True)
                for q in range(PAIR):
                    if not (last and q == PAIR - 1):
                        turn(i, q + 1, first)
                    hidden(i, q, first and q < 2)
                    if q == GC - 1 and not first:
                        outputs(i - 1, 1, i * (2 * ADDS) - ADDS, False)
                    if q == PAIR - 1:
                        outputs(i, 0, i * (2 * ADDS), first)
                if last:
                    outputs(i, 1, i * (2 * ADDS) + ADDS, False)

            pairs(pe, body)

        @block.vector
        def _(dve):
            def turned(i, q):
                for b in range(2):
                    dve.wait_ge(S["uT_hi"], i * (2 * PAIR) + 2 * q + b + 1)
                    dve.tensor_tensor(uT[q % 2][LO][:, 4 * b:4 * b + 4, :], PS[:, b, :].rearrange("p (k n) -> p k n", k=4),
                                      uT[q % 2][HI][:, 4 * b:4 * b + 4, :], ALU.subtract).then_inc(S["uT_lo"], 1)

            def add(before, fresh=False):
                for n in range(ADDS):
                    t, b = divmod(n, 2)
                    dve.wait_ge(S["f_psum"], before + (n + 1))
                    dst = acc[:, t, b * 512:(b + 1) * 512]
                    if fresh:
                        dve.tensor_copy(dst, PS[:, 6 + b, :]).then_inc(S["added"], 1)
                    else:
                        dve.tensor_tensor(dst, PS[:, 6 + b, :], dst, ALU.add).then_inc(S["added"], 1)

            def body(i, first, last):
                if first:
                    turned(0, 0)
                for q in range(PAIR):
                    e, c = divmod(q, GC)
                    if not (last and q == PAIR - 1):
                        turned(i, q + 1)
                    dve.wait_ge(S["v_hi"], i * PAIR + q + 1)
                    dve.tensor_tensor(v[e][LO][:, c, :], vraw[q % 2][:], v[e][HI][:, c, :], ALU.subtract).then_inc(S["v_lo"], 1)
                    if q == GC - 1 and not first:
                        add(i * (2 * ADDS) - ADDS)
                    if q == PAIR - 1:
                        add(i * (2 * ADDS), first)
                    dve.wait_ge(S["a_hi"], i * PAIR + q + 1)
                    dve.tensor_tensor(a[e][LO][:, c, :], gl[q % 2][:].rearrange("p s n -> p (s n)"), a[e][HI][:, c, :], ALU.subtract
                                      ).then_inc(S["a_lo"], 1)
                if last:
                    add(i * (2 * ADDS) + ADDS)

            pairs(dve, body)
            dve.wait_ge(S["f_sq"], NT)
            dve.tensor_scalar(stat[:, 0, 0:NT], stat[:, 0, 0:NT], 1.0 / D, EPS, ALU.mult, ALU.add).then_inc(S["f_var"], 1)
            dve.wait_ge(S["f_sqrt"], 1)
            dve.reciprocal(stat[:, 1, 0:NT], stat[:, 0, 0:NT]).then_inc(S["f_rstd"], 1)
            dve.wait_ge(S["f_rstd"], 1)
            for t in range(NT):
                if t >= 2:
                    dve.wait_ge(y_out[t % 2], 16 * (t // 2))
                dve.scalar_tensor_tensor(out=y[t % 2][:], in0=acc[:, t, :], scalar=stat[:, 1, t:t + 1], in1=gffn[:, int(t >= PT), :],
                                         op0=ALU.mult, op1=ALU.mult).then_inc(S["scaled"], 1)
                dve.wait_ge(S["scaled"], t + 1)
                dve.tensor_tensor(y[t % 2][:], y[t % 2][:], x[:, t, :], ALU.add).then_inc(S["y_ready"], 1)


_INS = ["x_prompt", "x_sample", "c_prompt", "c_sample", "cache_sb_k", "cache_sb_v", "cache_mla_ckv", "cache_mla_krope",
        "w_ada", "b_ada", "g_mix_pre", "g_mix_post", "g_ffn_pre", "g_ffn_post", "w_in", "g_q_lat", "g_kv_lat", "w_uq",
        "w_uk", "w_uv", "g_sb_out", "g_mla_out", "w_out", "w_peer_q", "sub_keys_1", "sub_keys_2", "u_experts", "v_experts"]
_OUTS = [("y_p", (1, SEQ, D)), ("y_s", (NSEQ, STEP, D)),
         ("sbk_p", (1, 1, SEQ, H, HD)), ("sbv_p", (1, 1, SEQ, H, HD)), ("ckv_p", (1, 1, SEQ, KVR)), ("kr_p", (1, 1, SEQ, ROPE)),
         ("sbk_s", (1, NSEQ, STEP, H, HD)), ("sbv_s", (1, NSEQ, STEP, H, HD)), ("ckv_s", (1, NSEQ, STEP, KVR)),
         ("kr_s", (1, NSEQ, STEP, ROPE))]


def declare(nc, arrays):
    dram = {}
    for name in _INS + ["table"]:
        a = arrays[name]
        dram[name] = nc.dram_tensor(f"in_{name}", a.shape, mybir.dt.from_np(a.dtype), kind="ExternalInput").ap()
    for name, shape in _OUTS:
        dram[name] = nc.dram_tensor(f"out_{name}", shape, F32, kind="ExternalOutput").ap()
    dram["gates"] = nc.dram_tensor("gates", (N // 64, NKEYS, NKEYS, 64), F32).ap()
    return dram


def kernel(**inputs):
    import numpy as _np
    import concourse.bacc as _bacc
    from concourse.bass_utils import run_bass_kernel_spmd as _run

    nc = _bacc.Bacc("TRN2", target_bir_lowering=False, num_devices=1)
    arrays = {name: _np.ascontiguousarray(inputs[name]) for name in _INS}
    arrays["table"] = constant_table()
    build(nc, declare(nc, arrays))
    r = _run(nc, [{f"in_{k}": v for k, v in arrays.items()}], core_ids=[0])
    return tuple(r.results[0][f"out_{name}"] for name, _ in _OUTS)
```

```python
import math
from contextlib import ExitStack

import numpy as np

import concourse.bass as bass
from concourse import mybir

F32 = mybir.dt.float32
U32 = mybir.dt.uint32
BF16 = mybir.dt.bfloat16
F32R = mybir.dt.float32r
ALU = mybir.AluOpType
ACT = mybir.ActivationFunctionType
AX_X = mybir.AxisListType.X

P = 128
D = 1024
KD = D // P
SEQ = 512
NSEQ = 8
STEP = 16
PAST = 512
KEYS = PAST + STEP
N = SEQ + NSEQ * STEP
NT = N // P
PT = SEQ // P
HALF = N // 2
CHUNK = 64
H = 8
HD = 64
SBW = H * HD
QR = 384
KVR = 256
ROPE = 32
RH = ROPE // 2
QK = HD + ROPE
LAT = QR + KVR + ROPE
INW = 3 * SBW + LAT
NKEYS = 128
TOPK = 16
NEXP = NKEYS * NKEYS
NQ = 2 * H
EPS = 1e-6
NEG = -1e30
MLA_SCALE = float(QK) ** -0.5
SB_SCALE = float(HD) ** -0.5
NC_ = 1 + NSEQ
WIDE = 96
COPIES = WIDE // NC_ + 1
HI, LO = 0, 1
PASSES = ((HI, HI), (HI, LO), (LO, HI))
NM = 6 * KD
SH1, SC1, GT1, SH2, SC2, GT2 = (KD * i for i in range(6))

VECTORS = [("b_ada", NM), ("g_mix_pre", KD), ("g_mix_post", KD), ("g_ffn_pre", KD), ("g_ffn_post", KD),
           ("g_q_lat", QR // P), ("g_kv_lat", KVR // P), ("g_sb_out", SBW // P), ("g_mla_out", SBW // P)]
VROW, _at = {}, 0
for _name, _n in VECTORS:
    VROW[_name] = _at
    _at += _n
NV = _at

CONSTS = [("ident", P), ("iota", P), ("keep", P), ("drop", P), ("ones", 8), ("cos", NT * RH), ("sin", NT * RH),
          ("new_keep", STEP), ("new_drop", STEP), ("slot", TOPK), ("chunk_row", P), ("chunk_col", P)]
CCOL, _at = {}, 0
for _name, _n in CONSTS:
    CCOL[_name] = (_at, _n)
    _at += _n
NCONST = _at


def constant_table():
    t = np.zeros((P, NCONST), np.float32)

    def put(name, a):
        at, n = CCOL[name]
        t[:, at:at + n] = np.asarray(a, np.float32).reshape(-1, n)

    row, col = np.arange(P)[:, None], np.arange(P)[None, :]
    put("ident", row == col)
    put("iota", np.broadcast_to(col, (P, P)))
    put("keep", col < row)
    put("drop", np.where(col < row, 0.0, NEG))
    put("ones", np.ones((P, 8)))
    pos = np.concatenate([np.arange(SEQ), PAST + np.tile(np.arange(STEP), NSEQ)]).astype(np.float32)
    inv = (np.float32(10000.0) ** (-np.arange(RH, dtype=np.float32) / np.float32(RH))).astype(np.float32)
    angle = (pos[:, None] * inv[None, :]).astype(np.float32).astype(np.float64).reshape(NT, P, RH).transpose(1, 0, 2)
    put("cos", np.cos(angle).reshape(P, NT * RH))
    put("sin", np.sin(angle).reshape(P, NT * RH))
    query, key = (np.arange(P) % STEP)[:, None], np.arange(STEP)[None, :]
    put("new_keep", key < query)
    put("new_drop", np.where(key < query, 0.0, NEG))
    put("slot", np.broadcast_to(np.arange(TOPK), (P, TOPK)))
    put("chunk_row", (row == 0) & (col < CHUNK))
    put("chunk_col", np.where((row == 0) & (col >= CHUNK), NEG, 0.0))
    return t


class Step:

    def __init__(self, eng, sem, at=0):
        self.eng, self.sem, self.n = eng, sem, at

    def __call__(self, ins):
        ins.then_inc(self.sem, 1)
        self.n += 1
        return self.n

    def wait(self, n=None):
        self.eng.wait_ge(self.sem, self.n if n is None else n)


def build(nc, A):
    ctx = ExitStack()
    KB = 1024
    BASE = 16512

    def sb(name, kb, shape, dt=F32):
        return nc.alloc_sbuf_tensor_at(name, shape, dt, offset=BASE + int(kb * KB))

    def run(phase):
        mine = {}

        def sem(name):
            if name not in mine:
                mine[name] = nc.alloc_semaphore(name)
            return mine[name]

        phase(nc, A, env | {"sem": sem, "env": env})
        nc.clear_and_free_semaphores(list(mine.values()))
        nc.all_engine_barrier()

    with ctx:
        PS = ctx.enter_context(nc.psum_tensor("PS", [P, 8, 512], F32))
        const = sb("const", 0, [P, NCONST])
        C = {k: const[:, a:a + n] for k, (a, n) in CCOL.items()}
        ident = C["ident"]
        KC = NCONST * 4 / KB
        assert KC <= 6
        vecT = sb("vecT", 6, [P, NV])
        adaT = sb("adaT", 6.375, [P, NM, NC_])
        coef = sb("coef", 8.0625, [P, 2, KD, NC_])
        stat = sb("stat", 8.65625, [P, 8, 16])
        cT = sb("cT", 9.1875, [P, NC_, KD])
        x = sb("x", 26, [P, NT, D])
        hT = sb("hT", 46, [P, KD, N])
        env = dict(locals())
        phases = (phase_condition_and_project, phase_latents, phase_prompt_attention, phase_sample_attention,
                  phase_merge, phase_keys, phase_gates, phase_experts)
        for phase in phases:
            run(phase)


def phase_condition_and_project(nc, A, env):
    sb, sem, PS, ident = (env[k] for k in ("sb", "sem", "PS", "ident"))
    const, vecT, adaT, coef, stat, cT, x, hT = (env[k] for k in ("const", "vecT", "adaT", "coef", "stat", "cT", "x", "hT"))
    GROUPS = [(SBW, SBW), (2 * SBW, SBW), (3 * SBW, LAT // 2), (3 * SBW + LAT // 2, LAT // 2), (0, SBW)]
    NG = len(GROUPS)
    hin = [sb("hin_hi", 66, [P, KD, N], F32R), sb("hin_lo", 46, [P, KD, N], F32R)]
    raw = sb("win_raw", 86, [P, KD * SBW])
    win = [[sb(f"win_{'hl'[s]}{i}", 102 + 32 * i + 16 * s, [P, KD * SBW], F32R) for s in (HI, LO)] for i in range(2)]
    WA = 2
    NWA = 2 * KD // WA
    wada = [sb(f"wada{i}", 102 + 8 * i, [P, KD, WA * P]) for i in range(NWA)]
    xn = [sb(f"xn{i}", 10 + 4 * i, [P, D]) for i in range(2)]
    ktok = [sb(f"ktok{i}", 18 + 2 * i, [P, SBW]) for i in range(2)]
    crow = sb("crow", 22, [NC_ * KD, P])
    cexp = sb("cexp", 22.5, [P, NC_ * KD])
    vrow = sb("vrow", 23, [NV, P])
    junk = sb("junk", 203, [P, D])
    qT = sb("qT", 26, [P, SBW // P, N])
    kT = sb("kT", 36, [P, SBW // P, N])
    vt = sb("vt", 179, [P, NT, SBW])
    lat = sb("lat", 189, [P, NT, LAT])
    env["env"].update(qT=qT, kT=kT, vt=vt, lat=lat, junk=junk)

    const_in, vec_in, c_in = sem("const_in"), sem("vec_in"), sem("c_in")
    x_in = [sem(f"x_in{t}") for t in range(NT)]
    wada_in = [sem(f"wada_in{i}") for i in range(NWA)]
    win_in = [sem(f"win_in{g}") for g in range(NG)]
    w_hi, w_lo, h_hi, h_lo = sem("w_hi"), sem("w_lo"), sem("h_hi"), sem("h_lo")
    small_T, small_ready = sem("small_T"), sem("small_ready")
    c_exp = sem("c_exp")
    ada_psum, ada_ready = sem("ada_psum"), sem("ada_ready")
    x_sq, x_rstd, x_sqrt, xn_ready = sem("x_sq"), sem("x_rstd"), sem("x_sqrt"), sem("xn_ready")
    xT_psum, hT_ready, v_step = sem("xT_psum"), sem("hT_ready"), sem("v_step")
    q_psum, q_ready = sem("q_psum"), sem("q_ready")
    tok_psum = [sem(f"tok_psum{g}") for g in range(4)]
    tok_ready = [sem(f"tok_ready{g}") for g in range(4)]
    kT_psum, kT_ready, sbv_out = sem("kT_psum"), sem("kT_ready"), sem("sbv_out")
    sbk_out = [sem("sbk_out0"), sem("sbk_out1")]
    x_dram = [A["x_prompt"][0, t * P:(t + 1) * P, :] for t in range(PT)] + [A["x_sample"].rearrange("b q d -> (b q) d")]
    sbk_dram = ([A["sbk_p"][0, 0, t * P:(t + 1) * P].rearrange("t h d -> t (h d)") for t in range(PT)]
                + [A["sbk_s"][0].rearrange("b q h d -> (b q) (h d)")])
    sbv_dram = ([A["sbv_p"][0, 0, t * P:(t + 1) * P].rearrange("t h d -> t (h d)") for t in range(PT)]
                + [A["sbv_s"][0].rearrange("b q h d -> (b q) (h d)")])

    def half(g, i):
        n = KD * GROUPS[g][1]
        return slice(i * n // 2, (i + 1) * n // 2) if g == 0 else slice(0, n)

    def columns(buf, g):
        return buf[:, 0:KD * GROUPS[g][1]].rearrange("p (k m) -> p k m", k=KD)

    with nc.Block() as block:
        @block.sync
        def _(sp):
            sp.dma_start(crow[0:KD, :], A["c_prompt"].rearrange("b (k p) -> (b k) p", p=P)).then_inc(c_in, 16)
            sp.dma_start(crow[KD:, :], A["c_sample"].rearrange("b (k p) -> (b k) p", p=P)).then_inc(c_in, 16)
            sp.wait_ge(const_in, 16)
            sp.wait_ge(vec_in, 16 * len(VECTORS))
            for i in range(NWA):
                sp.dma_start(wada[i][:], A["w_ada"][0].rearrange("(k p) m -> p k m", p=P)[:, :, i * WA * P:(i + 1) * WA * P]
                             ).then_inc(wada_in[i], 16)
                if i == NWA // 2:
                    for t in range(NT):
                        sp.dma_start(x[:, t, :], x_dram[t]).then_inc(x_in[t], 16)

            def load(g):
                if g:
                    sp.wait_ge(w_lo, g + 1)
                c0, w = GROUPS[g]
                sp.dma_start(columns(raw, g), A["w_in"][0].rearrange("(k p) m -> p k m", p=P)[:, :, c0:c0 + w]).then_inc(win_in[g], 16)

            load(0)
            load(1)
            for t in range(NT):
                sp.wait_ge(tok_ready[0], t + 1)
                sp.dma_start(sbk_dram[t], ktok[t % 2][:]).then_inc(sbk_out[t % 2], 16)
                if t == 3:
                    load(2)
            for t in range(NT):
                sp.wait_ge(tok_ready[1], t + 1)
                sp.dma_start(sbv_dram[t], vt[:, t, :]).then_inc(sbv_out, 16)
                if t == 0:
                    load(3)
            load(4)
            sp.wait_ge(sbk_out[0], 16 * 3)
            sp.wait_ge(sbk_out[1], 16 * 2)
            sp.wait_ge(sbv_out, 16 * NT)

        @block.gpsimd
        def _(pool):
            pass

        @block.scalar
        def _(act):
            act.dma_start(const[:], A["table"]).then_inc(const_in, 16)
            for name, n in VECTORS:
                act.dma_start(vrow[VROW[name]:VROW[name] + n, :], A[name].rearrange("a (k p) -> (a k) p", p=P)).then_inc(vec_in, 16)
            act.wait_ge(small_T, 2)
            act.activation(cexp[:], PS[:, 0, 0:NC_ * KD], ACT.Exp, scale=-1.0).then_inc(c_exp, 1)
            for t in range(NT):
                act.wait_ge(x_in[t], 16)
                if t >= 1:
                    act.wait_ge(x_sq, t)
                act.activation(junk[:], x[:, t, :], ACT.Square, accum_out=stat[:, 0, t:t + 1]).then_inc(x_sq, 1)
            act.wait_ge(x_rstd, 1)
            act.activation(stat[:, 1, 0:NT], stat[:, 1, 0:NT], ACT.Sqrt).then_inc(x_sqrt, 1)
            act.wait_ge(x_rstd, 2)

            def normed(t):
                if t >= 2:
                    act.wait_ge(xT_psum, 2 * (t - 1))
                act.activation(xn[t % 2][:], x[:, t, :], ACT.Copy, scale=stat[:, 2, t:t + 1]).then_inc(xn_ready, 1)

            def upper(t):
                cols = slice(t * P, (t + 1) * P)
                act.wait_ge(hT_ready, 2 * (t + 1))
                act.activation(hin[HI][:, :, cols], hT[:, :, cols], ACT.Copy).then_inc(h_hi, 1)

            def keys(t):
                act.wait_ge(tok_psum[0], t + 1)
                if t >= 2:
                    act.wait_ge(sbk_out[t % 2], 16 * (t // 2))
                    act.wait_ge(kT_psum, t - 1)
                act.activation(ktok[t % 2][:], PS[:, t % 2, :], ACT.Copy).then_inc(tok_ready[0], 1)

            def keys_turned(t):
                act.wait_ge(kT_psum, t + 1)
                if t == 0:
                    act.wait_ge(xn_ready, NT)
                act.activation(kT[:, :, t * P:(t + 1) * P], PS[:, 2 + t % 2, :].rearrange("p (c n) -> p c n", c=4), ACT.Copy
                               ).then_inc(kT_ready, 1)

            def upper_columns(g, i=0):
                act.wait_ge(win_in[g], 16)
                if g >= 2:
                    act.wait_ge(tok_psum[g - 2], NT)
                elif i == 0:
                    act.wait_ge(ada_psum, 1)
                act.activation(win[g % 2][HI][:, half(g, i)], raw[:, half(g, i)], ACT.Copy).then_inc(w_hi, 1)

            normed(0)
            normed(1)
            upper_columns(0, 0)
            upper(0)
            upper_columns(0, 1)
            normed(2)
            upper(1)
            keys(0)
            normed(3)
            upper(2)
            keys(1)
            normed(4)
            keys_turned(0)
            upper(3)
            keys(2)
            keys_turned(1)
            upper(4)
            upper_columns(1)
            keys(3)
            keys_turned(2)
            keys(4)
            keys_turned(3)
            keys_turned(4)
            upper_columns(2)
            upper_columns(3)
            for t in range(NT):
                act.wait_ge(tok_psum[2], t + 1)
                act.activation(lat[:, t, 0:LAT // 2], PS[:, t % 2, 0:LAT // 2], ACT.Copy).then_inc(tok_ready[2], 1)
            upper_columns(4)

        @block.tensor
        def _(pe):
            pe.wait_ge(const_in, 16)
            pe.wait_ge(vec_in, 16 * len(VECTORS))
            pe.transpose(PS[:, 1, 0:NV], vrow[:], ident[0:NV, 0:NV]).then_inc(small_T, 1)
            pe.wait_ge(c_in, 32)
            pe.transpose(PS[:, 0, 0:NC_ * KD], crow[:], ident[0:NC_ * KD, 0:NC_ * KD]).then_inc(small_T, 1)
            pe.wait_ge(small_ready, 2)
            for i in range(NWA):
                pe.wait_ge(wada_in[i], 16)
                for j in range(WA):
                    m = i * WA + j
                    for k in range(KD):
                        mm = pe.matmul(PS[:, 2, m * NC_:(m + COPIES) * NC_], wada[i][:, k, j * P:(j + 1) * P],
                                       cT[:, :, k].unsqueeze(1).broadcast_to((P, COPIES, NC_)), start=k == 0, stop=k == KD - 1)
            mm.then_inc(ada_psum, 1)

            def turn(t):
                pe.wait_ge(xn_ready, t + 1)
                for b in range(2):
                    if t >= 2:
                        pe.wait_ge(hT_ready, 2 * (t - 2) + b + 1)
                    for j in range(4):
                        k = 4 * b + j
                        mm = pe.transpose(PS[:, 4 + 2 * (t % 2) + b, j * P:(j + 1) * P], xn[t % 2][:, k * P:(k + 1) * P], ident)
                    mm.then_inc(xT_psum, 1)

            def project(g, t):
                w = GROUPS[g][1]
                if t == 0 and g:
                    pe.wait_ge(w_lo, g + 2)
                if g == 0:
                    pe.wait_ge(h_lo, t + 1)
                if t >= 2:
                    pe.wait_ge(tok_ready[g], t - 1)
                elif g >= 2:
                    pe.wait_ge(tok_ready[g - 2], NT)
                elif g == 1:
                    pe.wait_ge(kT_ready, NT)
                for k in range(KD):
                    if g == 0 and t == 0 and k % (KD // 2) == 0:
                        pe.wait_ge(w_lo, k // (KD // 2) + 1)
                    for a, b in PASSES:
                        mm = pe.matmul(PS[:, 2 * (g % 2) + t % 2, 0:w], hin[a][:, k, t * P:(t + 1) * P], columns(win[g % 2][b], g)[:, k, :],
                                       start=k == 0 and (a, b) == PASSES[0], stop=k == KD - 1 and (a, b) == PASSES[-1])
                mm.then_inc(tok_psum[g], 1)

            def turn_keys(t):
                pe.wait_ge(tok_ready[0], t + 1)
                if t >= 2:
                    pe.wait_ge(kT_ready, t - 1)
                for c in range(4):
                    mm = pe.transpose(PS[:, 2 + t % 2, c * P:(c + 1) * P], ktok[t % 2][:, c * P:(c + 1) * P], ident)
                mm.then_inc(kT_psum, 1)

            turn(0)
            turn(1)
            for t in range(NT):
                project(0, t)
                if t + 2 < NT:
                    turn(t + 2)
                if t:
                    turn_keys(t - 1)
            turn_keys(NT - 1)
            for g in range(1, NG - 1):
                for t in range(NT):
                    project(g, t)
            pe.wait_ge(w_lo, NG + 1)
            last = win[(NG - 1) % 2]
            for c in range(SBW // P):
                for b in range(2):
                    i = 2 * c + b
                    if i >= 2:
                        pe.wait_ge(q_ready, i - 1)
                    for k in range(KD):
                        for w, m in PASSES:
                            mm = pe.matmul(PS[:, 6 + b, 0:HALF], columns(last[w], NG - 1)[:, k, c * P:(c + 1) * P],
                                           hin[m][:, k, b * HALF:(b + 1) * HALF],
                                           start=k == 0 and (w, m) == PASSES[0], stop=k == KD - 1 and (w, m) == PASSES[-1])
                    mm.then_inc(q_psum, 1)

        @block.vector
        def _(dve):
            step = Step(dve, v_step)
            dve.wait_ge(small_T, 1)
            dve.tensor_copy(vecT[:], PS[:, 1, 0:NV]).then_inc(small_ready, 1)
            dve.wait_ge(c_exp, 1)
            step(dve.tensor_scalar(cexp[:], cexp[:], 1.0, None, ALU.add))
            step.wait()
            step(dve.reciprocal(cexp[:], cexp[:]))
            step.wait()
            dve.tensor_tensor(cT[:].rearrange("p a k -> p (a k)"), PS[:, 0, 0:NC_ * KD], cexp[:], ALU.mult).then_inc(small_ready, 1)
            dve.wait_ge(x_sq, NT)
            dve.tensor_scalar(stat[:, 1, 0:NT], stat[:, 0, 0:NT], 1.0 / D, EPS, ALU.mult, ALU.add).then_inc(x_rstd, 1)
            dve.wait_ge(x_sqrt, 1)
            dve.reciprocal(stat[:, 2, 0:NT], stat[:, 1, 0:NT]).then_inc(x_rstd, 1)
            dve.wait_ge(ada_psum, 1)
            dve.wait_ge(small_ready, 1)
            m = 2 * KD
            dve.tensor_tensor(adaT[:, 0:m, :], PS[:, 2, 0:m * NC_].rearrange("p (m c) -> p m c", c=NC_),
                              vecT[:, VROW["b_ada"]:VROW["b_ada"] + m].unsqueeze(2).broadcast_to((P, m, NC_)), ALU.add).then_inc(ada_ready, 1)
            dve.wait_ge(ada_ready, 1)
            dve.tensor_scalar(coef[:, 0], adaT[:, SC1:SC1 + KD, :], 1.0, None, ALU.add).then_inc(ada_ready, 1)
            dve.wait_ge(ada_ready, 2)
            g = VROW["g_mix_pre"]
            dve.tensor_tensor(coef[:, 0], coef[:, 0], vecT[:, g:g + KD].unsqueeze(2).broadcast_to((P, KD, NC_)), ALU.mult).then_inc(ada_ready, 1)
            dve.wait_ge(ada_ready, 3)

            def shifted(t):
                for b in range(2):
                    dve.wait_ge(xT_psum, 2 * t + b + 1)
                    modulate(dve, step, hT, PS[:, 4 + 2 * (t % 2) + b, :], coef[:, 0], adaT[:, SH1:SH1 + KD, :], t, b, hT_ready)

            def lower(t):
                cols = slice(t * P, (t + 1) * P)
                dve.wait_ge(h_hi, t + 1)
                dve.tensor_tensor(hin[LO][:, :, cols], hT[:, :, cols], hin[HI][:, :, cols], ALU.subtract).then_inc(h_lo, 1)

            def lower_columns(g, i=0):
                dve.wait_ge(w_hi, g + 1 + (i if g == 0 else 1))
                dve.tensor_tensor(win[g % 2][LO][:, half(g, i)], raw[:, half(g, i)], win[g % 2][HI][:, half(g, i)], ALU.subtract
                                  ).then_inc(w_lo, 1)

            shifted(0)
            lower(0)
            lower_columns(0, 0)
            lower_columns(0, 1)
            shifted(1)
            for t in range(2, NT):
                lower(t - 1)
                shifted(t)
            lower(NT - 1)
            lower_columns(1)
            lower_columns(2)
            for t in range(NT):
                dve.wait_ge(tok_psum[1], t + 1)
                dve.tensor_copy(vt[:, t, :], PS[:, 2 + t % 2, :]).then_inc(tok_ready[1], 1)
            lower_columns(3)
            lower_columns(4)
            for t in range(NT):
                dve.wait_ge(tok_psum[3], t + 1)
                dve.tensor_copy(lat[:, t, LAT // 2:LAT], PS[:, 2 + t % 2, 0:LAT // 2]).then_inc(tok_ready[3], 1)
            for c in range(SBW // P):
                for b in range(2):
                    dve.wait_ge(q_psum, 2 * c + b + 1)
                    dve.tensor_scalar(qT[:, c, b * HALF:(b + 1) * HALF], PS[:, 6 + b, 0:HALF], SB_SCALE, None, ALU.mult).then_inc(q_ready, 1)


def modulate(dve, step, out, psum, scale, shift, t, b, done):
    cols = slice(4 * b, 4 * b + 4)
    if t < PT:
        dst = out[:, cols, t * P:(t + 1) * P]
        src = psum.rearrange("p (k n) -> p k n", k=4)
        s, h = (v[:, cols, 0:1].broadcast_to((P, 4, P)) for v in (scale, shift))
    else:
        dst = out[:, cols, t * P:(t + 1) * P].rearrange("p k (s q) -> p k s q", q=STEP)
        src = psum.rearrange("p (k s q) -> p k s q", k=4, q=STEP)
        s, h = (v[:, cols, 1:NC_].unsqueeze(3).broadcast_to((P, 4, NSEQ, STEP)) for v in (scale, shift))
    step(dve.tensor_tensor(dst, src, s, ALU.mult))
    step.wait()
    dve.tensor_tensor(dst, dst, h, ALU.add).then_inc(done, 1)


def phase_latents(nc, A, env):
    sb, sem, PS, C, ident = (env[k] for k in ("sb", "sem", "PS", "C", "ident"))
    vecT, stat, lat, junk, qT = (env[k] for k in ("vecT", "stat", "lat", "junk", "qT"))
    CQ, CK = QR // P, KVR // P
    wuq = sb("wuq", 135, [P, CQ, H * QK])
    wuk = sb("wuk", 144, [P, CK, H * HD])
    wuv = sb("wuv", 148, [P, CK, H * HD])
    qtok = [sb(f"qtok{i}", 152 + 3 * i, [P, H * QK]) for i in range(2)]
    gkv = sb("gkv", 158, [P, KVR])
    qlatT = sb("qlatT", 66, [P, CQ, N])
    ckvT = sb("ckvT", 74, [P, CK, N])
    qmT = sb("qmT", 79, [QK, H, N])
    kmT = sb("kmT", 99, [QK, H, SEQ])
    vm = sb("vm", 115, [P, PT, SBW])
    krT = sb("krT", 123, [QK, P])
    wukT = sb("wukT", 123.5, [HD, H, CK, P])
    qz = [sb(f"qz{j}", 46 + 8 * j, [P, SBW // P, SEQ]) for j in range(2)]
    krpad = sb("krpad", 10, [P, NT, QK])
    rtmp = sb("rtmp", 12, [P, 2, H * RH])
    rtmp2 = sb("rtmp2", 13, [P, 4, H * RH])
    qabsT = sb("qabsT", 18, [P, CK, H, P])
    env["env"].update(ckvT=ckvT, qmT=qmT, kmT=kmT, vm=vm, krT=krT, qabsT=qabsT, qz=qz)
    cos = C["cos"].rearrange("p (t r) -> p t r", r=RH)
    sin = C["sin"].rearrange("p (t r) -> p t r", r=RH)
    nq, nkv, nrope = 0, QR, QR + KVR

    qz_ready = sem("qz_ready")
    wuq_in, wuk_in, wuv_in, gkv_in = sem("wuq_in"), sem("wuk_in"), sem("wuv_in"), sem("gkv_in")
    l_sq, l_var, l_sqrt, l_rstd, l_step = sem("l_sq"), sem("l_var"), sem("l_sqrt"), sem("l_rstd"), sem("l_step")
    pad_zero, kr_ready, ckv_ready, qn_ready = sem("pad_zero"), sem("kr_ready"), sem("ckv_ready"), sem("qn_ready")
    lat_out = sem("lat_out")
    ql_psum, ql_ready, cl_psum, cl_ready, kr_evac = sem("ql_psum"), sem("ql_ready"), sem("cl_psum"), sem("cl_ready"), sem("kr_evac")
    up_psum, up_ready, rot_ready = sem("up_psum"), sem("up_ready"), sem("rot_ready")
    qm_psum, qm_ready = sem("qm_psum"), [sem("qm_ready0"), sem("qm_ready1")]
    item_psum, item_ready = [sem("item_psum0"), sem("item_psum1")], [sem("item_ready0"), sem("item_ready1")]
    ckv_dram = ([A["ckv_p"][0, 0, t * P:(t + 1) * P, :] for t in range(PT)] + [A["ckv_s"][0].rearrange("b q c -> (b q) c")])
    kr_dram = ([A["kr_p"][0, 0, t * P:(t + 1) * P, :] for t in range(PT)] + [A["kr_s"][0].rearrange("b q c -> (b q) c")])
    NITEM = H + PT + 2 * H * CK // 4

    def item_target(i):
        if i < H:
            return kmT[0:HD, i, :], PS[0:HD, 6 + i % 2, :]
        if i < H + PT:
            return vm[:, i - H, :], PS[:, 6 + i % 2, :]
        j = i - H - PT
        if j < 4:
            return wukT[:].rearrange("p h c n -> p (h c n)")[:, 512 * j:512 * (j + 1)], PS[0:HD, 6 + i % 2, :]
        j -= 4
        return qabsT[:].rearrange("p c h n -> p (c h n)")[:, 512 * j:512 * (j + 1)], PS[:, 6 + i % 2, :]

    with nc.Block() as block:
        @block.sync
        def _(sp):
            sp.dma_start(wuq[:], A["w_uq"][0].rearrange("(c p) m -> p c m", p=P)).then_inc(wuq_in, 16)
            sp.dma_start(gkv[:], A["g_kv_lat"].broadcast_to((P, KVR))).then_inc(gkv_in, 16)
            sp.dma_start(wuk[:], A["w_uk"][0].rearrange("(c p) h m -> p c (h m)", p=P)).then_inc(wuk_in, 16)
            sp.dma_start(wuv[:], A["w_uv"][0].rearrange("(c p) h m -> p c (h m)", p=P)).then_inc(wuv_in, 16)
            sp.wait_ge(kr_ready, 1)
            for t in range(NT):
                sp.dma_start(kr_dram[t], krpad[:, t, HD:QK]).then_inc(lat_out, 16)
            for t in range(NT):
                sp.wait_ge(ckv_ready, t + 1)
                sp.dma_start(ckv_dram[t], lat[:, t, nkv:nrope]).then_inc(lat_out, 16)
            sp.wait_ge(lat_out, 16 * 2 * NT)

        @block.gpsimd
        def _(pool):
            pool.memset(krpad[:, :, 0:HD], 0.0).then_inc(pad_zero, 1)
            for j in range(2):
                pool.memset(qz[j][:], 0.0).then_inc(qz_ready, 1)
            pool.wait_ge(qz_ready, 2)
            for j in range(2):
                own = slice(j * HD, (j + 1) * HD)
                if j:
                    pool.wait_ge(qz_ready, 3)
                pool.tensor_copy(qz[j][own], qT[own, :, 0:SEQ]).then_inc(qz_ready, 1)

        @block.scalar
        def _(act):
            for t in range(NT):
                for j, (a, b) in enumerate(((nq, nkv), (nkv, nrope))):
                    if t + j:
                        act.wait_ge(l_sq, 2 * t + j)
                    act.activation(junk[:, 0:b - a], lat[:, t, a:b], ACT.Square, accum_out=stat[:, 3 + j, t:t + 1]).then_inc(l_sq, 1)
            act.wait_ge(l_var, 2)
            act.activation(stat[:, 3:5, 0:NT], stat[:, 3:5, 0:NT], ACT.Sqrt).then_inc(l_sqrt, 1)
            act.wait_ge(l_rstd, 1)
            for t in range(NT):
                act.activation(lat[:, t, nq:nkv], lat[:, t, nq:nkv], ACT.Copy, scale=stat[:, 5, t:t + 1]).then_inc(qn_ready, 1)

            def latent_columns(t):
                act.wait_ge(cl_psum, t + 1)
                act.activation(ckvT[:, :, t * P:(t + 1) * P], PS[:, 1, 0:KVR].rearrange("p (c n) -> p c n", c=CK), ACT.Copy
                               ).then_inc(cl_ready, 1)
                src = PS[HD:QK, 1, KVR:KVR + P]
                if t < PT:
                    act.activation(kmT[HD:QK, :, t * P:(t + 1) * P], src.unsqueeze(1).broadcast_to((ROPE, H, P)), ACT.Copy).then_inc(kr_evac, 1)
                else:
                    act.activation(krT[:], PS[0:QK, 1, KVR:KVR + P], ACT.Copy).then_inc(kr_evac, 1)

            latent_columns(0)
            for t in range(NT):
                act.wait_ge(up_psum, t + 1)
                if t >= 2:
                    act.wait_ge(qm_psum, 2 * (t - 1))
                act.activation(qtok[t % 2][:].rearrange("p (a b) -> p a b", a=2), PS[:, 2:4, 0:H * QK // 2], ACT.Copy).then_inc(up_ready, 1)
                if t + 1 < NT:
                    latent_columns(t + 1)
                act.wait_ge(qm_psum, 2 * t + 1)
                act.activation(qmT[:, 0:4, t * P:(t + 1) * P], PS[0:QK, 4, :].rearrange("p (h n) -> p h n", h=4), ACT.Copy).then_inc(qm_ready[0], 1)
            for i in range(0, NITEM, 2):
                act.wait_ge(item_psum[0], i // 2 + 1)
                act.activation(*item_target(i), ACT.Copy).then_inc(item_ready[0], 1)

        @block.tensor
        def _(pe):
            def latents(t):
                cols = slice(t * P, (t + 1) * P)
                pe.wait_ge(qn_ready, t + 1)
                if t:
                    pe.wait_ge(ql_ready, t)
                for c in range(CQ):
                    mm = pe.transpose(PS[:, 0, c * P:(c + 1) * P], lat[:, t, c * P:(c + 1) * P], ident)
                mm.then_inc(ql_psum, 1)
                pe.wait_ge(ckv_ready, t + 1)
                pe.wait_ge(kr_ready, 1)
                if t:
                    pe.wait_ge(kr_evac, t)
                for c in range(CK):
                    pe.transpose(PS[:, 1, c * P:(c + 1) * P], lat[:, t, nkv + c * P:nkv + (c + 1) * P], ident)
                pe.transpose(PS[0:QK, 1, KVR:KVR + P], krpad[:, t, :], ident).then_inc(cl_psum, 1)
                pe.wait_ge(ql_ready, t + 1)
                if t:
                    pe.wait_ge(up_ready, t)
                else:
                    pe.wait_ge(wuq_in, 16)
                for b in range(2):
                    for c in range(CQ):
                        mm = pe.matmul(PS[:, 2 + b, 0:H * QK // 2], qlatT[:, c, cols], wuq[:, c, b * H * QK // 2:(b + 1) * H * QK // 2],
                                       start=c == 0, stop=c == CQ - 1)
                mm.then_inc(up_psum, 1)

            def queries(t):
                pe.wait_ge(rot_ready, t + 1)
                for b in range(2):
                    if t:
                        pe.wait_ge(qm_ready[b], t)
                    for j in range(4):
                        h = 4 * b + j
                        mm = pe.transpose(PS[0:QK, 4 + b, j * P:(j + 1) * P], qtok[t % 2][:, h * QK:(h + 1) * QK], ident)
                    mm.then_inc(qm_psum, 1)

            latents(0)
            for t in range(NT):
                if t + 1 < NT:
                    latents(t + 1)
                queries(t)
            pe.wait_ge(cl_ready, NT)
            pe.wait_ge(wuk_in, 16)
            pe.wait_ge(wuv_in, 16)
            for i in range(NITEM):
                out = item_target(i)[1]
                if i >= 2:
                    pe.wait_ge(item_ready[i % 2], i // 2)
                if i < H:
                    for c in range(CK):
                        mm = pe.matmul(out, wuk[:, c, i * HD:(i + 1) * HD], ckvT[:, c, 0:SEQ], start=c == 0, stop=c == CK - 1)
                elif i < H + PT:
                    t = i - H
                    for c in range(CK):
                        mm = pe.matmul(out, ckvT[:, c, t * P:(t + 1) * P], wuv[:, c, :], start=c == 0, stop=c == CK - 1)
                elif i < H + PT + 4:
                    for n in range(4):
                        h, c = divmod(4 * (i - H - PT) + n, CK)
                        mm = pe.transpose(out[:, n * P:(n + 1) * P], wuk[:, c, h * HD:(h + 1) * HD], ident)
                else:
                    if i == H + PT + 4:
                        pe.wait_ge(item_ready[0], (i + 1) // 2)
                        pe.wait_ge(item_ready[1], i // 2)
                        pe.wait_ge(qm_ready[0], NT)
                        pe.wait_ge(qm_ready[1], NT)
                    for n in range(4):
                        c, h = divmod(4 * (i - H - PT - 4) + n, H)
                        mm = pe.matmul(out[:, n * P:(n + 1) * P], wukT[:, h, c, :], qmT[0:HD, h, SEQ:N], start=True, stop=True)
                mm.then_inc(item_psum[i % 2], 1)

        @block.vector
        def _(dve):
            step = Step(dve, l_step)
            dve.wait_ge(l_sq, 2 * NT)
            dve.tensor_scalar(stat[:, 3, 0:NT], stat[:, 3, 0:NT], 1.0 / QR, EPS, ALU.mult, ALU.add).then_inc(l_var, 1)
            dve.tensor_scalar(stat[:, 4, 0:NT], stat[:, 4, 0:NT], 1.0 / KVR, EPS, ALU.mult, ALU.add).then_inc(l_var, 1)
            a, b = lat[:, :, nrope:nrope + RH], lat[:, :, nrope + RH:LAT]
            u, v = (rtmp[:, i, 0:NT * RH].rearrange("p (t r) -> p t r", r=RH) for i in range(2))
            for x1, x2, op, dst in ((a, b, ALU.subtract, krpad[:, :, HD:HD + RH]), (b, a, ALU.add, krpad[:, :, HD + RH:QK])):
                step(dve.tensor_tensor(u, x1, cos, ALU.mult))
                step(dve.tensor_tensor(v, x2, sin, ALU.mult))
                step.wait()
                step(dve.tensor_tensor(dst, u, v, op))
                step.wait()
            dve.wait_ge(l_sqrt, 1)
            dve.reciprocal(stat[:, 5:7, 0:NT], stat[:, 3:5, 0:NT]).then_inc(l_rstd, 1)
            dve.wait_ge(l_rstd, 1)
            dve.wait_ge(pad_zero, 1)
            dve.sem_inc(kr_ready, 1)
            dve.wait_ge(gkv_in, 16)
            for t in range(NT):
                dve.scalar_tensor_tensor(out=lat[:, t, nkv:nrope], in0=lat[:, t, nkv:nrope], scalar=stat[:, 6, t:t + 1], in1=gkv[:],
                                         op0=ALU.mult, op1=ALU.mult).then_inc(ckv_ready, 1)
            g = VROW["g_q_lat"]

            def latent_columns(t):
                dve.wait_ge(ql_psum, t + 1)
                dve.tensor_tensor(qlatT[:, :, t * P:(t + 1) * P], PS[:, 0, 0:QR].rearrange("p (c n) -> p c n", c=CQ),
                                  vecT[:, g:g + CQ].unsqueeze(2).broadcast_to((P, CQ, P)), ALU.mult).then_inc(ql_ready, 1)

            latent_columns(0)
            for t in range(NT):
                cols = slice(t * P, (t + 1) * P)
                if t + 1 < NT:
                    latent_columns(t + 1)
                dve.wait_ge(up_ready, t + 1)
                q = qtok[t % 2][:].rearrange("p (h m) -> p h m", h=H)
                a, b = q[:, :, HD:HD + RH], q[:, :, HD + RH:QK]
                c, s = (w[:, t, :].unsqueeze(1).broadcast_to((P, H, RH)) for w in (cos, sin))
                u, v = (rtmp2[:, i, :].rearrange("p (h r) -> p h r", h=H) for i in range(2))
                w, z = (rtmp2[:, i, :].rearrange("p (h r) -> p h r", h=H) for i in range(2, 4))
                step(dve.tensor_tensor(u, a, c, ALU.mult))
                step(dve.tensor_tensor(v, b, s, ALU.mult))
                step(dve.tensor_tensor(w, b, c, ALU.mult))
                step(dve.tensor_tensor(z, a, s, ALU.mult))
                step.wait()
                step(dve.tensor_tensor(a, u, v, ALU.subtract))
                step.wait()
                step(dve.tensor_tensor(b, w, z, ALU.add))
                step.wait()
                dve.sem_inc(rot_ready, 1)
                dve.wait_ge(qm_psum, 2 * t + 2)
                dve.tensor_copy(qmT[:, 4:8, cols], PS[0:QK, 5, :].rearrange("p (h n) -> p h n", h=4)).then_inc(qm_ready[1], 1)
            for i in range(1, NITEM, 2):
                dve.wait_ge(item_psum[1], i // 2 + 1)
                dve.tensor_copy(*item_target(i)).then_inc(item_ready[1], 1)


def phase_prompt_attention(nc, A, env):
    sb, sem, PS, C, ident = (env[k] for k in ("sb", "sem", "PS", "C", "ident"))
    stat, qz, kT, vt, qmT, kmT, vm = (env[k] for k in ("stat", "qz", "kT", "vt", "qmT", "kmT", "vm"))
    osT = sb("osT", 135, [P, SBW // P, N])
    omT = sb("omT", 145, [P, SBW // P, N])
    env["env"].update(osT=osT, omT=omT)
    t1 = sb("t1", 189, [P, 2, SEQ])
    t2 = sb("t2", 193, [P, 2, SEQ])
    pr = sb("pr", 197, [P, 2, SEQ])
    aT = sb("aT", 10, [P, 2, PT, P])
    pT = sb("pT", 14, [P, 2, PT, P])
    peak, total, inverse = stat[:, 3, 0:2], stat[:, 4, 0:2], stat[:, 5, 0:2]
    wada = [sb(f"wada_b{i}", (66, 123.5)[i], [P, KD, 2 * P]) for i in range(2)]
    wada_in = [sem(f"pa_wada_in{i}") for i in range(2)]
    NREST = NM - 2 * KD
    rest = PS[:, 6, P:P + NREST * NC_]
    adaT, coef, vecT, cT = (env[k] for k in ("adaT", "coef", "vecT", "cT"))
    names = ("ada_psum ada_ready coef_step z_psum s_psum z_abs s_peak s_bias soft1 soft2 soft soft_kept tail logit logit_kept a_ready p_exp p_inv p_ready "
             "mT_psum aT_psum mT0 mT1 aT0 aT1 om_psum os_psum om_out os_out").split()
    S = {n: sem("pa_" + n) for n in names}
    ROUNDS = [(i, hp) for i in range(PT) for hp in range(H // 2)]
    R = len(ROUNDS)

    assert 2 * R == NREST

    def W(r):
        return (ROUNDS[r][0] + 1) * P

    with nc.Block() as block:
        @block.sync
        def _(sp):
            for r in range(R):
                if r >= 2:
                    sp.wait_ge(S["ada_psum"], r - 1)
                c0 = (2 * KD + 2 * r) * P
                sp.dma_start(wada[r % 2][:], A["w_ada"][0].rearrange("(k p) m -> p k m", p=P)[:, :, c0:c0 + 2 * P]).then_inc(wada_in[r % 2], 16)

        @block.gpsimd
        def _(pool):
            for r, (i, hp) in enumerate(ROUNDS):
                d = slice(i * P, i * P + P)
                for buf, mask, op, need, done in ((t1, "keep", ALU.mult, "soft", "soft_kept"), (t2, "drop", ALU.add, "logit", "logit_kept")):
                    pool.wait_ge(S[need], r + 1)
                    pool.tensor_tensor(buf[:, :, d], buf[:, :, d], C[mask].unsqueeze(1).broadcast_to((P, 2, P)), op).then_inc(S[done], 1)

        @block.scalar
        def _(act):
            def softplus(r):
                w = W(r)
                act.wait_ge(S["z_psum"], r + 1)
                if r:
                    act.wait_ge(S["tail"], 2 * r)
                act.activation(t1[:, :, 0:w], PS[:, 0:2, 0:w], ACT.Abs).then_inc(S["z_abs"], 1)
                act.wait_ge(S["z_abs"], r + 1)
                act.activation(t1[:, :, 0:w], t1[:, :, 0:w], ACT.Exp, scale=-1.0).then_inc(S["soft1"], 1)
                act.wait_ge(S["soft1"], r + 1)
                act.activation(t1[:, :, 0:w], t1[:, :, 0:w], ACT.Ln, bias=1.0).then_inc(S["soft2"], 1)

            def softmax(r):
                w = W(r)
                act.wait_ge(S["s_bias"], r + 1)
                if r:
                    act.wait_ge(S["mT_psum"], r)
                for j in range(2):
                    act.activation(pr[:, j, 0:w], PS[:, 2 + j, 0:w], ACT.Exp, bias=peak[:, j:j + 1], scale=MLA_SCALE,
                                   accum_out=total[:, j:j + 1]).then_inc(S["p_exp"], 1)

            def transposed(r, dst, psum, done, used):
                i = ROUNDS[r][0]
                act.wait_ge(S[psum], r + 1)
                if r:
                    act.wait_ge(S[used], r)
                act.activation(dst[:, 0, 0:i + 1, :], PS[:, 4, 0:W(r)].rearrange("p (k n) -> p k n", n=P), ACT.Copy).then_inc(S[done], 1)

            act.preload_act_table_set("natural_log_exp_and_others")
            softmax(0)
            softplus(0)
            transposed(0, pT, "mT_psum", "mT0", "om_psum")
            for r, (i, hp) in enumerate(ROUNDS):
                act.wait_ge(S["logit_kept"], r + 1)
                act.activation(t2[:, :, 0:W(r)], t2[:, :, 0:W(r)], ACT.Exp).then_inc(S["a_ready"], 1)
                if r + 1 < R:
                    softmax(r + 1)
                    softplus(r + 1)
                act.wait_ge(S["om_psum"], r + 1)
                act.activation(omT[:, hp, i * P:(i + 1) * P], PS[:, 7, 0:P], ACT.Copy).then_inc(S["om_out"], 1)
                transposed(r, aT, "aT_psum", "aT0", "os_psum")
                if r + 1 < R:
                    transposed(r + 1, pT, "mT_psum", "mT0", "om_psum")

        @block.tensor
        def _(pe):
            def sb_scores(r):
                i, hp = ROUNDS[r]
                if r:
                    pe.wait_ge(S["logit"], r)
                for j in range(2):
                    mm = pe.matmul(PS[:, j, 0:W(r)], qz[j][:, hp, i * P:(i + 1) * P], kT[:, hp, 0:W(r)], start=True, stop=True)
                mm.then_inc(S["z_psum"], 1)

            def mla_scores(r):
                i, hp = ROUNDS[r]
                if r:
                    pe.wait_ge(S["p_exp"], 2 * r)
                for j in range(2):
                    h = 2 * hp + j
                    pe.matmul(PS[:, 2 + j, 0:W(r)], qmT[:, h, i * P:(i + 1) * P], kmT[:, h, 0:W(r)], start=True, stop=False)
                    mm = pe.matmul(PS[:, 2 + j, i * P:(i + 1) * P], C["chunk_row"][0:QK, :], C["chunk_col"][0:QK, :], start=False, stop=True)
                mm.then_inc(S["s_psum"], 1)

            def transposes(r, src, need, count, free, done):
                for j in range(2):
                    pe.wait_ge(S[need], count)
                    for f, n in free:
                        if n:
                            pe.wait_ge(S[f], n)
                    for k in range(ROUNDS[r][0] + 1):
                        mm = pe.transpose(PS[:, 4 + j, k * P:(k + 1) * P], src[:, j, k * P:(k + 1) * P], ident)
                mm.then_inc(S[done], 1)

            def values(r, v, wT, need, free, bank, done):
                i, hp = ROUNDS[r]
                for n in need:
                    pe.wait_ge(S[n], r + 1)
                if r:
                    pe.wait_ge(S[free], r)
                for j in range(2):
                    h = 2 * hp + j
                    for k in range(i + 1):
                        mm = pe.matmul(PS[j * HD:(j + 1) * HD, bank, 0:P], v[:, k, h * HD:(h + 1) * HD], wT[:, j, k, :],
                                       start=k == 0, stop=k == i)
                mm.then_inc(S[done], 1)

            def conditioning(r):
                pe.wait_ge(wada_in[r % 2], 16 * (r // 2 + 1))
                for j in range(2):
                    m = 2 * r + j
                    for k in range(KD):
                        mm = pe.matmul(PS[:, 6, P + m * NC_:P + (m + COPIES) * NC_], wada[r % 2][:, k, j * P:(j + 1) * P],
                                       cT[:, :, k].unsqueeze(1).broadcast_to((P, COPIES, NC_)), start=k == 0, stop=k == KD - 1)
                mm.then_inc(S["ada_psum"], 1)

            sb_scores(0)
            mla_scores(0)
            for r in range(R):
                transposes(r, pr, "p_ready", 2 * (r + 1), (("aT0", r), ("aT1", r)), "mT_psum")
                if r + 1 < R:
                    mla_scores(r + 1)
                values(r, vm, pT, ("mT0", "mT1"), "om_out", 7, "om_psum")
                if r + 1 < R:
                    sb_scores(r + 1)
                conditioning(r)
                transposes(r, t2, "a_ready", r + 1, (("mT0", r + 1), ("mT1", r + 1)), "aT_psum")
                values(r, vt, aT, ("aT0", "aT1"), "os_out", 6, "os_psum")

        @block.vector
        def _(dve):
            def start(r):
                w = W(r)
                dve.wait_ge(S["s_psum"], r + 1)
                if r:
                    dve.wait_ge(S["p_ready"], 2 * r)
                dve.tensor_reduce(peak, PS[:, 2:4, 0:w], AX_X, ALU.max).then_inc(S["s_peak"], 1)
                dve.wait_ge(S["s_peak"], r + 1)
                dve.tensor_scalar(peak, peak, -MLA_SCALE, None, ALU.mult).then_inc(S["s_bias"], 1)

            def transposed(r, dst, psum, done, used):
                i = ROUNDS[r][0]
                dve.wait_ge(S[psum], r + 1)
                if r:
                    dve.wait_ge(S[used], r)
                dve.tensor_copy(dst[:, 1, 0:i + 1, :], PS[:, 5, 0:W(r)].rearrange("p (k n) -> p k n", n=P)).then_inc(S[done], 1)

            def weights(r):
                w = W(r)
                start(r)
                dve.wait_ge(S["p_exp"], 2 * (r + 1))
                dve.reciprocal(inverse, total).then_inc(S["p_inv"], 1)
                dve.wait_ge(S["p_inv"], r + 1)
                for j in range(2):
                    dve.tensor_scalar(pr[:, j, 0:w], pr[:, j, 0:w], inverse[:, j:j + 1], None, ALU.mult).then_inc(S["p_ready"], 1)
                dve.wait_ge(S["soft2"], r + 1)
                dve.scalar_tensor_tensor(out=t1[:, :, 0:w], in0=PS[:, 0:2, 0:w], scalar=0.0, in1=t1[:, :, 0:w],
                                         op0=ALU.max, op1=ALU.add).then_inc(S["soft"], 1)

            weights(0)
            for r, (i, hp) in enumerate(ROUNDS):
                w = W(r)
                dve.wait_ge(S["soft_kept"], r + 1)
                if r:
                    dve.wait_ge(S["aT_psum"], r)
                last = w - 1
                for j in range(2):
                    rev = (lambda b: b[:, j, last::-1])
                    dve.tensor_tensor_scan(rev(t2), C["ones"][:, 0:1].broadcast_to((P, w)), rev(t1), 0.0, ALU.mult, ALU.add).then_inc(S["tail"], 1)
                dve.wait_ge(S["tail"], 2 * (r + 1))
                dve.tensor_tensor(t2[:, :, 0:w], PS[:, 0:2, 0:w], t2[:, :, 0:w], ALU.subtract).then_inc(S["logit"], 1)
                transposed(r, pT, "mT_psum", "mT1", "om_psum")
                if r + 1 < R:
                    weights(r + 1)
                transposed(r, aT, "aT_psum", "aT1", "os_psum")
                dve.wait_ge(S["os_psum"], r + 1)
                dve.tensor_copy(osT[:, hp, i * P:(i + 1) * P], PS[:, 6, 0:P]).then_inc(S["os_out"], 1)
            dve.wait_ge(S["ada_psum"], R)
            dve.tensor_tensor(adaT[:, 2 * KD:NM, :], rest.rearrange("p (m c) -> p m c", c=NC_),
                              vecT[:, 2 * KD:NM].unsqueeze(2).broadcast_to((P, NREST, NC_)), ALU.add).then_inc(S["ada_ready"], 1)
            dve.wait_ge(S["ada_ready"], 1)
            dve.tensor_scalar(coef[:, 1], adaT[:, SC2:SC2 + KD, :], 1.0, None, ALU.add).then_inc(S["coef_step"], 1)
            dve.wait_ge(S["coef_step"], 1)
            g = VROW["g_ffn_pre"]
            dve.tensor_tensor(coef[:, 1], coef[:, 1], vecT[:, g:g + KD].unsqueeze(2).broadcast_to((P, KD, NC_)), ALU.mult
                              ).then_inc(S["coef_step"], 1)


def phase_sample_attention(nc, A, env):
    sb, sem, PS, C, ident = (env[k] for k in ("sb", "sem", "PS", "C", "ident"))
    stat, qT, kT, qmT, ckvT, krT, qabsT, osT, omT = (env[k] for k in ("stat", "qT", "kT", "qmT", "ckvT", "krT", "qabsT", "osT", "omT"))
    KBLK, CQ, CK = PAST // P, SBW // P, KVR // P
    flat = PS[:].rearrange("p b n -> p (b n)")
    z, s = flat[:, 0:KEYS], flat[:, 1024:1024 + KEYS]
    s_new = flat[:, 1024 + PAST:1024 + PAST + WIDE]
    kc = [sb("kc0", 46, [P, KBLK, SBW]), sb("kc1", 99, [P, KBLK, SBW])]
    vc = [sb("vc0", 54, [P, KBLK, SBW]), sb("vc1", 107, [P, KBLK, SBW])]
    cc = [sb("cc0", 62, [P, KBLK, KVR]), sb("cc1", 115, [P, KBLK, KVR])]
    kr = [sb("kr0", 201, [P, KBLK, QK]), sb("kr1", 119, [P, KBLK, QK])]
    vnew = [sb("vnew0", 155, [P, SBW]), sb("vnew1", 131.5, [P, SBW])]
    cnew = [sb("cnew0", 157, [P, KVR]), sb("cnew1", 133.5, [P, KVR])]
    keyT = sb("keyT", 10, [P, CQ, PAST])
    latT = sb("latT", 66, [P, CK, PAST])
    rotT = sb("rotT", 70, [QK, PAST])
    qblk = sb("qblk", 72, [P, CQ, P])
    qabs = sb("qabs", 120.5, [P, CK, P])
    qrot = sb("qrot", 121.5, [QK, P])
    olatT = sb("olatT", 123.5, [P, CK, H, P])
    t1, t2, pr = sb("st1", 189, [P, KEYS]), sb("st2", 191.25, [P, KEYS]), sb("spr", 193.5, [P, KEYS])
    aT, pT = sb("saT", 196, [P, KBLK + 1, P]), sb("spT", 198.5, [P, KBLK + 1, P])
    wuv = sb("wuv_again", 203, [P, CK, SBW])
    peak, total, inverse = stat[:, 3, 0:1], stat[:, 4, 0:1], stat[:, 5, 0:1]
    names = ("zeroed qblk_ready q_ready z_psum s_psum z_abs soft1 soft2 soft soft_kept tail logit logit_kept a_ready s_peak s_bias "
             "p_exp p_inv p_ready turned turn0 turn1 ol_psum ol_out os_psum os_out om_psum om_out wuv_in").split()
    S = {n: sem("sa_" + n) for n in names}
    IN = {n: [sem(f"sa_{n}{i}") for i in range(2)] for n in ("kc_in", "vc_in", "cc_in", "kr_in", "new_in")}
    turn = [S["turn0"], S["turn1"]]
    KV, OWN = CQ + CK + 1, 4
    PER = OWN + KV

    def new_cols(b, step=STEP):
        return bass.ds(SEQ + b * step, step)

    def wide(cols):
        return cols.unsqueeze(1).broadcast_to((cols.shape[0], WIDE // STEP, STEP))

    def loop(eng, body):
        with eng.Fori(0, NSEQ // 2 - 1) as pair:
            body(pair, 0, True, True)
            body(pair, 1, True, True)
        body(NSEQ // 2 - 1, 0, True, False)
        body(NSEQ // 2 - 1, 1, False, False)

    def place(e, n, caches):
        return 2 * KV + (PER if caches else OWN) * e + n

    def piece(pair, e, n, caches):
        return pair * (2 * PER) + place(e, n, caches)

    def parity(e, n, caches):
        return place(e, n, caches) % 2

    def before(pair, e, n, caches):
        return pair * PER + (place(e, n, caches) // 2 + 1)

    def weight_target(n, e):
        bank, dst = 4 + e, (pT, aT)[n // 2]
        if n % 2 == 0:
            return dst[:, 0:KBLK, :], PS[:, bank, :].rearrange("p (k n) -> p k n", n=P)
        return dst[0:STEP, KBLK, :], PS[0:STEP, bank, 0:P]

    def cache_target(n, e):
        bank = 4 + e
        if n < CQ:
            return keyT[:, n, :], PS[:, bank, :]
        if n < CQ + CK:
            return latT[:, n - CQ, :], PS[:, bank, :]
        return rotT[:], PS[0:QK, bank, :]

    def evacuate_first(eng, copy, mine, i):
        for n in range(KV):
            if (i * KV + n) % 2 == mine:
                eng.wait_ge(S["turned"], i * KV + n + 1)
                copy(*cache_target(n, mine)).then_inc(turn[mine], 1)

    def evacuate(eng, copy, mine, pair, e, ns, caches):
        for n in ns:
            if parity(e, n, caches) == mine:
                eng.wait_ge(S["turned"], piece(pair, e, n, caches) + 1)
                copy(*(weight_target(n, mine) if n < OWN else cache_target(n - OWN, mine))).then_inc(turn[mine], 1)

    with nc.Block() as block:
        @block.sync
        def _(sp):
            def load_keys(b, e):
                sp.dma_start(kc[e][:], A["cache_sb_k"][0, b].rearrange("(k p) h d -> p k (h d)", p=P)).then_inc(IN["kc_in"][e], 16)
                sp.dma_start(kr[e][:, :, HD:QK], A["cache_mla_krope"][0, b].rearrange("(k p) c -> p k c", p=P)).then_inc(IN["kr_in"][e], 16)

            def load_latents(b, e):
                sp.dma_start(cc[e][:], A["cache_mla_ckv"][0, b].rearrange("(k p) c -> p k c", p=P)).then_inc(IN["cc_in"][e], 16)
                sp.dma_start(cnew[e][0:STEP, :], A["ckv_s"][0, b]).then_inc(IN["new_in"][e], 16)

            def load_values(b, e):
                sp.dma_start(vc[e][:], A["cache_sb_v"][0, b].rearrange("(k p) h d -> p k (h d)", p=P)).then_inc(IN["vc_in"][e], 16)
                sp.dma_start(vnew[e][0:STEP, :], A["sbv_s"][0, b].rearrange("q h d -> q (h d)")).then_inc(IN["new_in"][e], 16)

            sp.wait_ge(S["zeroed"], 6)
            for e in range(2):
                load_keys(e, e)
                load_latents(e, e)
                load_values(e, e)
            sp.dma_start(wuv[:], A["w_uv"][0].rearrange("(c p) h m -> p c (h m)", p=P)).then_inc(S["wuv_in"], 16)
            with sp.Fori(1, NSEQ // 2) as it:
                for e in range(2):
                    sp.wait_ge(S["turned"], it * (2 * PER) + ((e - 2) * PER + KV))
                    load_keys(it * 2 + e, e)
                    sp.wait_ge(S["ol_psum"], it * 2 + (e - 1))
                    load_latents(it * 2 + e, e)
                    sp.wait_ge(S["os_psum"], it * 2 + (e - 1))
                    load_values(it * 2 + e, e)

        @block.gpsimd
        def _(pool):
            for i in range(2):
                pool.memset(vnew[i][:], 0.0).then_inc(S["zeroed"], 1)
                pool.memset(cnew[i][:], 0.0).then_inc(S["zeroed"], 1)
                pool.memset(kr[i][:, :, 0:HD], 0.0).then_inc(S["zeroed"], 1)
            pool.memset(qblk[:], 0.0).then_inc(S["zeroed"], 1)
            pool.memset(aT[:, KBLK, :], 0.0).then_inc(S["zeroed"], 1)
            pool.memset(pT[:, KBLK, :], 0.0).then_inc(S["zeroed"], 1)

            def body(pair, e, more, caches):
                b = pair * 2 + e
                new = slice(PAST, KEYS)
                pool.wait_ge(S["soft"], b + 1)
                pool.tensor_tensor(t1[:, new], t1[:, new], C["new_keep"], ALU.mult).then_inc(S["soft_kept"], 1)
                pool.wait_ge(S["logit"], b + 1)
                pool.tensor_tensor(t2[:, new], t2[:, new], C["new_drop"], ALU.add).then_inc(S["logit_kept"], 1)

            loop(pool, body)

        @block.scalar
        def _(act):
            def copy(dst, src):
                return act.activation(dst, src, ACT.Copy)

            act.preload_act_table_set("natural_log_exp_and_others")
            act.sem_inc(turn[0], 1)
            act.sem_inc(S["ol_out"], 1)
            act.wait_ge(S["zeroed"], 9)
            evacuate_first(act, copy, 0, 0)

            def softplus(b):
                act.wait_ge(S["z_psum"], b + 1)
                act.activation(t1[:], z, ACT.Abs).then_inc(S["z_abs"], 1)
                act.wait_ge(S["z_abs"], b + 1)
                act.activation(t1[:], t1[:], ACT.Exp, scale=-1.0).then_inc(S["soft1"], 1)
                act.wait_ge(S["soft1"], b + 1)
                act.activation(t1[:], t1[:], ACT.Ln, bias=1.0).then_inc(S["soft2"], 1)

            def softmax(b):
                act.wait_ge(S["s_bias"], b + 1)
                act.activation(pr[:], s, ACT.Exp, bias=peak, scale=MLA_SCALE, accum_out=total).then_inc(S["p_exp"], 1)

            def stick(b):
                act.wait_ge(S["logit_kept"], b + 1)
                act.activation(t2[:], t2[:], ACT.Exp).then_inc(S["a_ready"], 1)

            def body(pair, e, more, caches):
                b = pair * 2 + e
                evacuate(act, copy, 0, pair, e, (0, 1), caches)
                act.wait_ge(S["ol_psum"], b + 1)
                act.activation(olatT[:, :, :, bass.ds(b * STEP, STEP)],
                               PS[:, 7, 0:CK * P].rearrange("p (c h q) -> p c h q", c=CK, h=H), ACT.Copy).then_inc(S["ol_out"], 1)
                if more:
                    softplus(b + 1)
                evacuate(act, copy, 0, pair, e, (2, 3), caches)
                if more:
                    softmax(b + 1)
                if caches:
                    evacuate(act, copy, 0, pair, e, range(OWN, OWN + KV - 3), caches)
                if more:
                    stick(b + 1)
                if caches:
                    evacuate(act, copy, 0, pair, e, range(OWN + KV - 3, PER), caches)

            softplus(0)
            softmax(0)
            stick(0)
            evacuate_first(act, copy, 0, 1)
            loop(act, body)

        @block.tensor
        def _(pe):
            def turn_piece(out, ins, bank, before):
                pe.wait_ge(turn[bank], before)
                for k, (o, i, idn) in enumerate(zip(out, ins, [ident] * len(ins))):
                    mm = pe.transpose(o, i, idn)
                mm.then_inc(S["turned"], 1)

            def cache_pieces(e, count, ns, bank_of, before):
                for n in ns:
                    bank = bank_of(n)
                    if n < CQ:
                        src, arrived, rows, width = kc[e], "kc_in", P, slice(n * P, (n + 1) * P)
                    elif n < CQ + CK:
                        src, arrived, rows, width = cc[e], "cc_in", P, slice((n - CQ) * P, (n - CQ + 1) * P)
                    else:
                        src, arrived, rows, width = kr[e], "kr_in", QK, slice(0, QK)
                    pe.wait_ge(IN[arrived][e], count)
                    turn_piece([PS[0:rows, 4 + bank, k * P:(k + 1) * P] for k in range(KBLK)],
                               [src[:, k, width] for k in range(KBLK)], bank, before(n))

            cache_pieces(0, 16, range(KV), lambda n: n % 2, lambda n: n // 2 + 1)
            pe.wait_ge(turn[0], (KV + 1) // 2 + 1)
            pe.wait_ge(turn[1], KV // 2 + 1)

            def scores(b):
                pe.wait_ge(S["qblk_ready"], b + 1)
                for c in range(CQ):
                    pe.matmul(flat[:, 0:PAST], qblk[:, c, :], keyT[:, c, :], start=c == 0, stop=c == CQ - 1)
                for c in range(CQ):
                    mm = pe.matmul(flat[:, PAST:PAST + WIDE], qblk[:, c, :], wide(kT[:, c, new_cols(b)]), start=c == 0, stop=c == CQ - 1)
                mm.then_inc(S["z_psum"], 1)
                pe.wait_ge(S["q_ready"], (b + 1) * 2)
                for c in range(CK):
                    pe.matmul(s[:, 0:PAST], qabs[:, c, :], latT[:, c, :], start=c == 0, stop=False)
                pe.matmul(s[:, 0:PAST], qrot[:], rotT[:], start=False, stop=True)
                for c in range(CK):
                    pe.matmul(s_new, qabs[:, c, :], wide(ckvT[:, c, new_cols(b)]), start=c == 0, stop=False)
                pe.matmul(s_new, qrot[:], wide(krT[:, bass.ds(b * STEP, STEP)]), start=False, stop=True).then_inc(S["s_psum"], 1)

            scores(0)
            cache_pieces(1, 16, range(KV), lambda n: (KV + n) % 2, lambda n: (KV + n) // 2 + 1)

            def body(pair, e, more, caches):
                b = pair * 2 + e
                for w, (src, need) in enumerate(((pr, "p_ready"), (t2, "a_ready"))):
                    if w and more:
                        pe.wait_ge(S["logit"], b + 1)
                        scores(b + 1)
                    pe.wait_ge(S[need], b + 1)
                    n = 2 * w
                    bank = parity(e, n, caches)
                    turn_piece([PS[:, 4 + bank, k * P:(k + 1) * P] for k in range(KBLK)],
                               [src[:, k * P:(k + 1) * P] for k in range(KBLK)], bank, before(pair, e, n, caches))
                    turn_piece([PS[0:STEP, 5 - bank, 0:P]], [src[:, PAST:KEYS]], 1 - bank, before(pair, e, n + 1, caches))
                    pe.wait_ge(turn[bank], before(pair, e, n, caches) + 1)
                    pe.wait_ge(turn[1 - bank], before(pair, e, n + 1, caches) + 1)
                    if w == 0:
                        pe.wait_ge(IN["new_in"][e], pair * 32 + 32)
                        pe.wait_ge(S["ol_out"], b + 1)
                        for c in range(CK):
                            for k in range(KBLK + 1):
                                v = cc[e][:, k, c * P:(c + 1) * P] if k < KBLK else cnew[e][:, c * P:(c + 1) * P]
                                mm = pe.matmul(PS[:, 7, c * P:(c + 1) * P], v, pT[:, k, :], start=k == 0, stop=k == KBLK)
                        mm.then_inc(S["ol_psum"], 1)
                    else:
                        pe.wait_ge(IN["vc_in"][e], pair * 16 + 16)
                        pe.wait_ge(S["os_out"], b + 1)
                        for c in range(CQ):
                            for k in range(KBLK + 1):
                                v = vc[e][:, k, c * P:(c + 1) * P] if k < KBLK else vnew[e][:, c * P:(c + 1) * P]
                                mm = pe.matmul(PS[:, 6, c * P:(c + 1) * P], v, aT[:, k, :], start=k == 0, stop=k == KBLK)
                            if c == CQ - 1:
                                mm.then_inc(S["os_psum"], 1)
                            if caches and c:
                                cache_pieces(e, pair * 16 + 32, ((), (0, 1), (2, 3), (4, 5, 6))[c],
                                             lambda n: parity(e, OWN + n, caches), lambda n: before(pair, e, OWN + n, caches))

            loop(pe, body)
            pe.wait_ge(S["ol_out"], NSEQ + 1)
            pe.wait_ge(S["wuv_in"], 16)
            for h in range(H):
                rows = slice((h % 2) * HD, (h % 2 + 1) * HD)
                for c in range(CK):
                    mm = pe.matmul(PS[rows, 4, h // 2 * P:(h // 2 + 1) * P], wuv[:, c, h * HD:(h + 1) * HD], olatT[:, c, h, :],
                                   start=c == 0, stop=c == CK - 1)
            mm.then_inc(S["om_psum"], 1)

        @block.vector
        def _(dve):
            def copy(dst, src):
                return dve.tensor_copy(dst, src)

            def queries(b):
                for j in range(2):
                    rows = slice(j * HD, (j + 1) * HD)
                    diag = qblk[rows].rearrange("p c (h q) -> p (c h) q", q=STEP)[:, j::H + 2, :]
                    ins = dve.tensor_copy(diag, qT[rows, :, new_cols(b)])
                    if j:
                        ins.then_inc(S["qblk_ready"], 1)
                dve.tensor_copy(qabs[:].rearrange("p c (h q) -> p c h q", q=STEP), qabsT[:, :, :, bass.ds(b * STEP, STEP)]).then_inc(S["q_ready"], 1)
                dve.tensor_copy(qrot[:].rearrange("p (h q) -> p h q", q=STEP), qmT[:, :, new_cols(b)]).then_inc(S["q_ready"], 1)

            dve.sem_inc(turn[1], 1)
            dve.sem_inc(S["os_out"], 1)
            dve.wait_ge(S["zeroed"], 9)
            queries(0)
            evacuate_first(dve, copy, 1, 0)

            def weights(b, weights_turned):
                dve.wait_ge(S["s_psum"], b + 1)
                dve.tensor_reduce(peak, s, AX_X, ALU.max).then_inc(S["s_peak"], 1)
                dve.wait_ge(S["s_peak"], b + 1)
                dve.tensor_scalar(peak, peak, -MLA_SCALE, None, ALU.mult).then_inc(S["s_bias"], 1)
                dve.wait_ge(S["soft2"], b + 1)
                dve.scalar_tensor_tensor(out=t1[:], in0=z, scalar=0.0, in1=t1[:], op0=ALU.max, op1=ALU.add).then_inc(S["soft"], 1)
                dve.wait_ge(S["p_exp"], b + 1)
                dve.reciprocal(inverse, total).then_inc(S["p_inv"], 1)
                dve.wait_ge(S["p_inv"], b + 1)
                dve.tensor_scalar(pr[:], pr[:], inverse, None, ALU.mult).then_inc(S["p_ready"], 1)
                dve.wait_ge(S["soft_kept"], b + 1)
                if weights_turned is not None:
                    dve.wait_ge(S["turned"], weights_turned)
                dve.tensor_tensor_scan(t2[:, ::-1], C["ones"][:, 0:1].broadcast_to((P, KEYS)), t1[:, ::-1], 0.0, ALU.mult, ALU.add).then_inc(S["tail"], 1)
                dve.wait_ge(S["tail"], b + 1)
                dve.tensor_tensor(t2[:], z, t2[:], ALU.subtract).then_inc(S["logit"], 1)

            weights(0, None)
            evacuate_first(dve, copy, 1, 1)
            queries(1)

            def body(pair, e, more, caches):
                b = pair * 2 + e
                evacuate(dve, copy, 1, pair, e, range(OWN), caches)
                if more:
                    weights(b + 1, pair * (2 * PER) + (2 * KV + (PER if caches else OWN) * e + OWN))
                if caches:
                    evacuate(dve, copy, 1, pair, e, range(OWN, PER), caches)
                    queries(b + 2)
                dve.wait_ge(S["os_psum"], b + 1)
                for j in range(2):
                    rows = slice(j * HD, (j + 1) * HD)
                    own = PS[rows, 6, :].rearrange("p (c q) -> p c q", q=STEP)[:, j::H + 2, :]
                    ins = dve.tensor_copy(osT[rows, :, new_cols(b)], own)
                ins.then_inc(S["os_out"], 1)

            loop(dve, body)
            dve.wait_ge(S["om_psum"], 1)
            dve.tensor_copy(omT[:, :, SEQ:N], PS[:, 4, :].rearrange("p (c n) -> p c n", c=CQ)).then_inc(S["om_out"], 1)


def phase_merge(nc, A, env):
    sb, sem, PS, C, ident = (env[k] for k in ("sb", "sem", "PS", "C", "ident"))
    vecT, adaT, coef, stat, x, hT, osT, omT = (env[k] for k in ("vecT", "adaT", "coef", "stat", "x", "hT", "osT", "omT"))
    CW = SBW // P
    wout = sb("wout", 66, [P, KD, D])
    wq = [sb(f"wq{k}", 66 + 8 * k, [P, NQ * P]) for k in range(KD)]
    y = sb("y", 159, [P, NT, D])
    gated = sb("gated", 159, [P, 2, KD, NC_])
    per_query = sb("per_query", 179, [P, 2, KD, P])
    xn = [sb(f"xm{i}", 179 + 4 * i, [P, D]) for i in range(2)]
    sq = sb("sq", 187, [P, 2 * CW, N])
    junk = sq[:].rearrange("p c n -> p (c n)")[:, 0:D]
    gmix, gffn = sb("gmix", 10, [P, 2, D]), sb("gffn", 18, [P, 2, D])
    env["env"].update(gffn=gffn, wq=wq)
    names = ("squared scaled ss_psum g_var g_sqrt g_rstd oa_psum ob_psum ya_ready y_ready y_sq y_var y_sqrt y_rstd "
             "gated row_psum row_ready mixed x1_ready x_sq x_var x_sqrt x_rstd xn_ready xT_psum h_ready step").split()
    S = {n: sem("mg_" + n) for n in names}
    wout_in = [sem(f"mg_wout_in{k}") for k in range(2)]
    wq_in = nc.alloc_semaphore("wq_in")
    env["env"].update(wq_in=wq_in)
    x_in = [sem(f"mg_x_in{t}") for t in range(NT)]
    x_dram = [A["x_prompt"][0, t * P:(t + 1) * P, :] for t in range(PT)] + [A["x_sample"].rearrange("b q d -> (b q) d")]
    groups = ((osT, "g_sb_out"), (omT, "g_mla_out"))

    with nc.Block() as block:
        @block.sync
        def _(sp):
            for k in range(2):
                sp.dma_start(wout[:, 4 * k:4 * k + 4, :], A["w_out"][0, 4 * k * P:4 * (k + 1) * P].rearrange("(k p) m -> p k m", p=P)
                             ).then_inc(wout_in[k], 16)
            for t in range(NT):
                sp.dma_start(x[:, t, :], x_dram[t]).then_inc(x_in[t], 16)
            for k in range(KD // 2, KD):
                sp.dma_start(wq[k][:], A["w_peer_q"][0, k * P:(k + 1) * P, :]).then_inc(wq_in, 16)
            sp.wait_ge(S["ob_psum"], NT)
            for k in range(KD // 2):
                sp.dma_start(wq[k][:], A["w_peer_q"][0, k * P:(k + 1) * P, :]).then_inc(wq_in, 16)

        @block.gpsimd
        def _(pool):
            pass

        @block.scalar
        def _(act):
            for g, (o, _) in enumerate(groups):
                act.activation(sq[:, g * CW:(g + 1) * CW, :], o[:], ACT.Square).then_inc(S["squared"], 1)
            for i in range(4):
                act.wait_ge(S["row_psum"], i + 1)
                act.activation((gmix, gffn)[i // 2][:, i % 2, :].rearrange("p (b n) -> p b n", b=2),
                               PS[:, 4:6, :] if i % 2 else PS[:, 6:8, :], ACT.Copy).then_inc(S["row_ready"], 1)
            act.wait_ge(S["g_var"], 1)
            act.activation(stat[:, 0, 0:2 * NT], stat[:, 0, 0:2 * NT], ACT.Sqrt).then_inc(S["g_sqrt"], 1)
            act.wait_ge(S["g_rstd"], 1)

            def attention_half(t):
                act.wait_ge(S["oa_psum"], t + 1)
                act.activation(y[:, t, :].rearrange("p (b n) -> p b n", b=2), PS[:, 0:2, :], ACT.Copy,
                               scale=stat[:, 1, 2 * t:2 * t + 1]).then_inc(S["ya_ready"], 1)

            def mean_square(src, row, t, ready, count, squared, var, sqrt):
                act.wait_ge(S[ready], t + 1)
                if count:
                    act.wait_ge(S[count[0]], count[1])
                act.activation(junk, src, ACT.Square, accum_out=stat[:, row, t:t + 1]).then_inc(S[squared], 1)
                act.wait_ge(S[var], t + 1)
                act.activation(stat[:, row, t:t + 1], stat[:, row, t:t + 1], ACT.Sqrt).then_inc(S[sqrt], 1)

            attention_half(0)
            for t in range(NT):
                mean_square(y[:, t, :], 2, t, "y_ready", ("x_sq", t) if t else ("ss_psum", 1), "y_sq", "y_var", "y_sqrt")
                mean_square(x[:, t, :], 4, t, "x1_ready", ("y_sq", t + 1), "x_sq", "x_var", "x_sqrt")
                act.wait_ge(S["x_rstd"], t + 1)
                if t >= 2:
                    act.wait_ge(S["xT_psum"], 2 * (t - 1))
                act.activation(xn[t % 2][:], x[:, t, :], ACT.Copy, scale=stat[:, 5, t:t + 1]).then_inc(S["xn_ready"], 1)
                if t + 1 < NT:
                    attention_half(t + 1)

        @block.tensor
        def _(pe):
            pe.wait_ge(S["gated"], 4)
            for i in range(4):
                if i >= 2:
                    pe.wait_ge(S["row_ready"], i - 1)
                for k in range(KD):
                    per_token = gated[:, i // 2, k, 0:1].broadcast_to((P, P)) if i % 2 == 0 else per_query[:, i // 2, k, :]
                    bank = (6 if i % 2 == 0 else 4) + k // 4
                    mm = pe.matmul(PS[:, bank, (k % 4) * P:(k % 4 + 1) * P], per_token, ident, start=True, stop=True)
                mm.then_inc(S["row_psum"], 1)
            pe.wait_ge(S["squared"], 2)
            for t in range(NT):
                for g in range(2):
                    for c in range(CW):
                        mm = pe.matmul(PS[:, 0, 2 * t + g:2 * t + g + WIDE], sq[:, g * CW + c, t * P:(t + 1) * P],
                                       C["ones"][:, 0:1].broadcast_to((P, WIDE)),
                                       start=c == 0, stop=c == CW - 1)
            mm.then_inc(S["ss_psum"], 1)

            def project(t):
                for g, (o, _) in enumerate(groups):
                    if t == 0:
                        pe.wait_ge(wout_in[g], 16)
                        pe.wait_ge(S["scaled"], CW * (g + 1))
                        if g == 0:
                            pe.wait_ge(S["g_var"], 1)
                    else:
                        pe.wait_ge(S[("ya_ready", "y_ready")[g]], t)
                    for b in range(2):
                        for c in range(CW):
                            mm = pe.matmul(PS[:, 2 * g + b, :], o[:, c, t * P:(t + 1) * P], wout[:, g * CW + c, b * 512:(b + 1) * 512],
                                           start=c == 0, stop=c == CW - 1)
                    mm.then_inc(S[("oa_psum", "ob_psum")[g]], 1)

            def turn(t):
                pe.wait_ge(S["xn_ready"], t + 1)
                if t == 0:
                    pe.wait_ge(S["row_ready"], 4)
                for b in range(2):
                    if t >= 2:
                        pe.wait_ge(S["h_ready"], 2 * (t - 2) + b + 1)
                    for j in range(4):
                        k = 4 * b + j
                        mm = pe.transpose(PS[:, 4 + 2 * (t % 2) + b, j * P:(j + 1) * P], xn[t % 2][:, k * P:(k + 1) * P], ident)
                    mm.then_inc(S["xT_psum"], 1)

            for t in range(NT):
                project(t)
                if t:
                    turn(t - 1)
            turn(NT - 1)

        @block.vector
        def _(dve):
            step = Step(dve, S["step"])
            for i, (row, name) in enumerate(((GT1, "g_mix_post"), (GT2, "g_ffn_post"))):
                gain = vecT[:, VROW[name]:VROW[name] + KD].unsqueeze(2).broadcast_to((P, KD, NC_))
                dve.tensor_tensor(gated[:, i], adaT[:, row:row + KD, :], gain, ALU.mult).then_inc(S["gated"], 1)
            dve.wait_ge(S["gated"], 2)
            for i in range(2):
                dve.tensor_copy(per_query[:, i].rearrange("p k (s q) -> p k s q", q=STEP),
                                gated[:, i, :, 1:NC_].unsqueeze(3).broadcast_to((P, KD, NSEQ, STEP))).then_inc(S["gated"], 1)
            dve.wait_ge(S["squared"], 2)
            for o, name in groups:
                for c in range(CW):
                    g = vecT[:, VROW[name] + c:VROW[name] + c + 1]
                    dve.tensor_scalar(o[:, c, :], o[:, c, :], g, None, ALU.mult).then_inc(S["scaled"], 1)
            dve.wait_ge(S["ss_psum"], 1)
            dve.tensor_scalar(stat[:, 0, 0:2 * NT], PS[:, 0, 0:2 * NT], 1.0 / SBW, EPS, ALU.mult, ALU.add).then_inc(S["g_var"], 1)
            dve.wait_ge(S["g_sqrt"], 1)
            dve.reciprocal(stat[:, 1, 0:2 * NT], stat[:, 0, 0:2 * NT]).then_inc(S["g_rstd"], 1)
            dve.wait_ge(S["g_rstd"], 1)

            def factor(row, t, squared, var, sqrt, done):
                dve.wait_ge(S[squared], t + 1)
                dve.tensor_scalar(stat[:, row, t:t + 1], stat[:, row, t:t + 1], 1.0 / D, EPS, ALU.mult, ALU.add).then_inc(S[var], 1)
                dve.wait_ge(S[sqrt], t + 1)
                dve.reciprocal(stat[:, row + 1, t:t + 1], stat[:, row, t:t + 1]).then_inc(S[done], 1)

            def shifted(t):
                for b in range(2):
                    dve.wait_ge(S["xT_psum"], 2 * t + b + 1)
                    modulate(dve, step, hT, PS[:, 4 + 2 * (t % 2) + b, :], coef[:, 1], adaT[:, SH2:SH2 + KD, :], t, b, S["h_ready"])

            for t in range(NT):
                dve.wait_ge(S["ob_psum"], t + 1)
                dve.wait_ge(S["ya_ready"], t + 1)
                v = y[:, t, :].rearrange("p (b n) -> p b n", b=2)
                dve.scalar_tensor_tensor(out=v, in0=PS[:, 2:4, :], scalar=stat[:, 1, 2 * t + 1:2 * t + 2], in1=v,
                                         op0=ALU.mult, op1=ALU.add).then_inc(S["y_ready"], 1)
                factor(2, t, "y_sq", "y_var", "y_sqrt", "y_rstd")
                dve.wait_ge(S["y_rstd"], t + 1)
                dve.wait_ge(S["row_ready"], 2)
                dve.scalar_tensor_tensor(out=y[:, t, :], in0=y[:, t, :], scalar=stat[:, 3, t:t + 1], in1=gmix[:, int(t >= PT), :],
                                         op0=ALU.mult, op1=ALU.mult).then_inc(S["mixed"], 1)
                dve.wait_ge(S["mixed"], t + 1)
                dve.wait_ge(x_in[t], 16)
                dve.tensor_tensor(x[:, t, :], x[:, t, :], y[:, t, :], ALU.add).then_inc(S["x1_ready"], 1)
                factor(4, t, "x_sq", "x_var", "x_sqrt", "x_rstd")
                if t:
                    shifted(t - 1)
            shifted(NT - 1)


def phase_keys(nc, A, env):
    sb, sem, PS, C, ident = (env[k] for k in ("sb", "sem", "PS", "C", "ident"))
    hT = env["hT"]
    wq = env["wq"]
    qp = [sb(f"qp{i}", 130 + 8 * i, [P, NQ, P]) for i in range(2)]
    sc = [sb(f"sc{i}", 162 + 8 * i, [P, NQ, NKEYS]) for i in range(2)]
    SHORT = TOPK // 2
    NCAND = TOPK + (SHORT - 1) * SHORT + SHORT
    cand = sb("cand", 178, [P, H, NCAND])
    skey = sb("skey", 186, [P, 2, P])
    rest = sb("rest", 187, [P, NQ * NKEYS])
    hot = sb("hot", 187, [P, NQ, TOPK, TOPK], BF16)
    halves = [sb(f"halves{w}", at, [P, NQ, TOPK, w], BF16) for w, at in ((8, 150), (4, 154), (2, 156))]
    pick = sb("pick", 195, [P, NT, 3, H * TOPK])
    top = sb("top", 203, [P, NQ, TOPK])
    topi = sb("topi", 204, [P, NQ, TOPK], U32)
    topf = sb("topf", 205, [P, NQ, TOPK], BF16)
    best = sb("best", 206, [P, H, TOPK])
    besti = sb("besti", 206.5, [P, 2, H, TOPK], U32)
    sel = sb("sel", 10, [P, 3, N])
    rank = sb("rank", 146, [P, H, 2, TOPK])
    place, work = sb("place", 147, [P, H * TOPK]), sb("work", 147.5, [P, 2, H * TOPK])
    flat_stat = env["stat"][:].rearrange("p a b -> p (a b)")
    total, peak = flat_stat[:, 0:NT * H], flat_stat[:, 64:64 + H]
    env["env"].update(sel=sel)
    names = "sk_psum sk_ready q_psum q_ready s_psum s_ready topped ranked gate_exp gates sel_psum sel_ready0 sel_ready1 step".split()
    S = {n: sem("pk_" + n) for n in names}
    sk_in = sem("pk_sk_in")

    with nc.Block() as block:
        @block.sync
        def _(sp):
            sp.dma_start(skey[:, 0, :], A["sub_keys_1"][0]).then_inc(sk_in, 16)
            sp.dma_start(skey[:, 1, :], A["sub_keys_2"][0]).then_inc(sk_in, 16)

        @block.scalar
        def _(act):
            act.wait_ge(S["sk_psum"], 1)
            act.activation(skey[:].rearrange("p i n -> p (i n)"), PS[:, 7, 0:2 * P], ACT.Copy).then_inc(S["sk_ready"], 1)
            def queries(t, g):
                act.wait_ge(S["q_psum"], t * (NQ // 4) + g + 1)
                if t >= 2:
                    act.wait_ge(S["s_psum"], 4 * (t - 1))
                act.activation(qp[t % 2][:, 4 * g:4 * g + 4, :], PS[:, g % 2, :].rearrange("p (m n) -> p m n", m=4), ACT.Copy
                               ).then_inc(S["q_ready"], 1)

            for t in range(NT):
                queries(t, 0)
                for g in range(4):
                    if g < 3:
                        queries(t, g + 1)
                    if t >= 2 and g == 0:
                        act.wait_ge(S["topped"], t - 1)
                    act.wait_ge(S["s_psum"], 4 * t + g + 1)
                    act.activation(sc[t % 2][:, 4 * g:4 * g + 4, :], PS[:, 2 + g, :].rearrange("p (m e) -> p m e", e=NKEYS),
                                   ACT.Copy).then_inc(S["s_ready"], 1)
            act.wait_ge(S["ranked"], NT)
            act.activation(pick[:, :, 2, :], pick[:, :, 2, :], ACT.Exp).then_inc(S["gate_exp"], 1)
            for t in range(1, NT, 2):
                act.wait_ge(S["sel_psum"], t + 1)
                act.activation(sel[:, :, t * P:(t + 1) * P], PS[:, 7, 0:3 * P].rearrange("p (i n) -> p i n", i=3), ACT.Copy
                               ).then_inc(S["sel_ready1"], 1)

        @block.tensor
        def _(pe):
            pe.wait_ge(sk_in, 32)
            for i in range(2):
                mm = pe.transpose(PS[:, 7, i * P:(i + 1) * P], skey[:, i, :], ident)
            mm.then_inc(S["sk_psum"], 1)
            pe.wait_ge(env["wq_in"], 16 * KD)

            def queries(t, g):
                i = t * (NQ // 4) + g
                if i >= 2:
                    pe.wait_ge(S["q_ready"], i - 1)
                for j in range(4):
                    m = 4 * g + j
                    for k in range(KD):
                        mm = pe.matmul(PS[:, g % 2, j * P:(j + 1) * P], wq[k][:, m * P:(m + 1) * P], hT[:, k, t * P:(t + 1) * P],
                                       start=k == 0, stop=k == KD - 1)
                mm.then_inc(S["q_psum"], 1)

            for t in range(NT):
                queries(t, 0)
                for g in range(4):
                    if g < 3:
                        queries(t, g + 1)
                    pe.wait_ge(S["q_ready"], t * (NQ // 4) + g + 1)
                    if t:
                        pe.wait_ge(S["s_ready"], 4 * (t - 1) + g + 1)
                    elif g == 0:
                        pe.wait_ge(S["sk_ready"], 1)
                    for j in range(4):
                        m = 4 * g + j
                        mm = pe.matmul(PS[:, 2 + g, j * P:(j + 1) * P], qp[t % 2][:, m, :], skey[:, m % 2, :], start=True, stop=True)
                    mm.then_inc(S["s_psum"], 1)
            pe.wait_ge(S["gates"], 1)
            for t in range(NT):
                if t >= 2:
                    pe.wait_ge(S[f"sel_ready{t % 2}"], t // 2)
                for i in range(3):
                    mm = pe.transpose(PS[:, 6 + t % 2, i * P:(i + 1) * P], pick[:, t, i, :], ident)
                mm.then_inc(S["sel_psum"], 1)

        @block.vector
        def _(dve):
            step = Step(dve, S["step"])

            def sync(ins):
                step(ins)
                step.wait()

            def top16(values, width, out, index, rows):
                spare = rest[:, 0:NQ * width].rearrange("p (m e) -> p m e", m=NQ)
                for m in rows:
                    step(dve.max(out[:, m, 0:8], values[:, m, :]))
                step.wait()
                for m in rows:
                    step(dve.max_index(index[:, m, 0:8], out[:, m, 0:8], values[:, m, :]))
                    step(dve.match_replace(spare[:, m, :], out[:, m, 0:8], values[:, m, :], NEG))
                step.wait()
                for m in rows:
                    step(dve.max(out[:, m, 8:16], spare[:, m, :]))
                step.wait()
                for m in rows:
                    ins = dve.max_index(index[:, m, 8:16], out[:, m, 8:16], spare[:, m, :])
                return ins

            for t in range(NT):
                for g in range(4):
                    dve.wait_ge(S["s_ready"], 4 * t + g + 1)
                    ins = top16(sc[t % 2], NKEYS, top, topi, range(4 * g, 4 * g + 4))
                ins.then_inc(S["topped"], 1)
                dve.wait_ge(S["topped"], t + 1)
                step(dve.tensor_copy(topf[:], topi[:]))
                pairs = top[:].rearrange("p (h i) k -> p h i k", i=2)
                one, two = pairs[:, :, 0, :], pairs[:, :, 1, :]
                step(dve.tensor_tensor(cand[:, :, 0:TOPK], one[:, :, 0:1].broadcast_to((P, H, TOPK)), two, ALU.add))
                rows = cand[:, :, TOPK:TOPK + (SHORT - 1) * SHORT].rearrange("p h (a b) -> p h a b", b=SHORT)
                step(dve.tensor_tensor(rows, one[:, :, 1:SHORT].unsqueeze(3).broadcast_to((P, H, SHORT - 1, SHORT)),
                                       two[:, :, 0:SHORT].unsqueeze(2).broadcast_to((P, H, SHORT - 1, SHORT)), ALU.add))
                sync(dve.tensor_tensor(cand[:, :, NCAND - SHORT:], one[:, :, SHORT:], two[:, :, 0:1].broadcast_to((P, H, SHORT)), ALU.add))
                sync(top16(cand, NCAND, best, besti[:, 0], range(H)))
                step(dve.tensor_copy(peak, best[:, :, 0]))
                flat = besti[:, 0].rearrange("p h k -> p (h k)")
                eighth = besti[:, 1].rearrange("p h k -> p (h k)")
                step(dve.tensor_copy(place[:], flat))
                sync(dve.tensor_scalar(eighth, flat, 3, None, ALU.logical_shift_right))
                sync(dve.tensor_copy(work[:, 0, :], eighth))
                dve.tensor_tensor(pick[:, t, 2, :].rearrange("p (h k) -> p h k", h=H), best[:], peak.unsqueeze(2).broadcast_to((P, H, TOPK)),
                                  ALU.subtract).then_inc(S["ranked"], 1)
                sync(dve.tensor_scalar(work[:, 0, :], work[:, 0, :], -1.0, 0.0, ALU.add, ALU.max))
                by_head = (lambda ap: ap.rearrange("p (h k) -> p h k", h=H))
                sync(dve.scalar_tensor_tensor(out=rank[:, :, 0, :], in0=by_head(place[:]), scalar=float(SHORT - (NCAND - SHORT)), in1=by_head(work[:, 0, :]),
                                              op0=ALU.add, op1=ALU.max))
                sync(dve.tensor_scalar(by_head(work[:, 0, :]), rank[:, :, 0, :], 1.0, float(SHORT), ALU.min, ALU.mult))
                sync(dve.scalar_tensor_tensor(out=by_head(work[:, 1, :]), in0=rank[:, :, 0, :], scalar=float(SHORT), in1=by_head(work[:, 0, :]),
                                              op0=ALU.mult, op1=ALU.add))
                sync(dve.tensor_tensor(work[:, 1, :], place[:], work[:, 1, :], ALU.subtract))
                sync(dve.tensor_scalar(rank[:, :, 1, :], by_head(work[:, 1, :]), 0.0, None, ALU.max))
                sync(dve.tensor_tensor(hot[:].rearrange("p n k m -> p (n k) m"),
                                       rank[:].rearrange("p h i k -> p (h i k)").unsqueeze(2).broadcast_to((P, NQ * TOPK, TOPK)),
                                       C["slot"].unsqueeze(1).broadcast_to((P, NQ * TOPK, TOPK)), ALU.is_equal))
                sync(dve.tensor_tensor(hot[:], hot[:], topf[:].unsqueeze(2).broadcast_to((P, NQ, TOPK, TOPK)), ALU.mult))
                src = hot
                for half in halves:
                    w = half.shape[3]
                    sync(dve.tensor_tensor(half[:], src[:, :, :, 0:w], src[:, :, :, w:2 * w], ALU.add))
                    src = half
                pairs = src[:].rearrange("p (h i) k m -> p h i k m", i=2)
                for i in range(2):
                    step(dve.tensor_tensor(by_head(pick[:, t, i, :]), pairs[:, :, i, :, 0], pairs[:, :, i, :, 1], ALU.add))
                step.wait()
            dve.wait_ge(S["gate_exp"], 1)
            gate = pick[:, :, 2, :].rearrange("p t (h k) -> p t h k", h=H)
            totals = total.rearrange("p (t h) -> p t h", h=H)
            sync(dve.tensor_reduce(totals, gate, AX_X, ALU.add))
            sync(dve.reciprocal(total, total))
            dve.tensor_tensor(gate, gate, totals.unsqueeze(3).broadcast_to((P, NT, H, TOPK)), ALU.mult).then_inc(S["gates"], 1)
            for t in range(0, NT, 2):
                dve.wait_ge(S["sel_psum"], t + 1)
                dve.tensor_copy(sel[:, :, t * P:(t + 1) * P], PS[:, 6, 0:3 * P].rearrange("p (i n) -> p i n", i=3)).then_inc(S["sel_ready0"], 1)


TB = 64


def phase_gates(nc, A, env):
    sb, sem, PS, C, sel = (env[k] for k in ("sb", "sem", "PS", "C", "sel"))
    hT = env["hT"]
    stage = [sb(f"stage{i}", 138 + 32 * i, [P, NKEYS, TB]) for i in range(2)]
    G = 4
    first = [sb(f"first{i}", 66 + 2 * i, [P, G, NKEYS]) for i in range(G)]
    second = [sb(f"second{i}", 74 + 2 * i, [P, G, NKEYS]) for i in range(G)]
    h = [sb("h_hi", 86, [P, KD, N], F32R), sb("h_lo", 46, [P, KD, N], F32R)]
    u = [sb(f"u{i}", 106 + 4 * i, [P, D]) for i in range(4)]
    env["env"].update(h=h, u=u)
    h_split, u_in = sem("gt_h_split"), sem("gt_u_in")
    S = {n: sem("gt_" + n) for n in "marked hot_ready weighed hot_used table_ready".split()}
    stored = [nc.alloc_semaphore(f"gates_stored{i}") for i in range(2)]
    env["env"].update(gates_stored=stored)
    BLOCKS, INNER = N // TB, TB // (G * G)
    PB = INNER * G

    def loop(eng, body, edge=None):
        def groups(pair, e, i, last):
            for g in range(G):
                body(pair * (2 * PB) + i * G + (e * PB + g), g, e, i * (G * G) + g * G, pair * (2 * TB) + i * (G * G) + (e * TB + g * G),
                     last and g == G - 1)

        def block_of_tokens(pair, e, last):
            if edge:
                edge(pair, e)
            with eng.Fori(0, INNER - int(last)) as i:
                groups(pair, e, i, False)
            if last:
                groups(pair, e, INNER - 1, True)

        with eng.Fori(0, BLOCKS // 2 - 1) as pair:
            for e in range(2):
                block_of_tokens(pair, e, False)
        for e in range(2):
            block_of_tokens(BLOCKS // 2 - 1, e, e == 1)

    with nc.Block() as block:
        @block.sync
        def _(sp):
            for i in range(len(u)):
                sp.dma_start(u[i][:], A["u_experts"][0, i * P:(i + 1) * P, :]).then_inc(u_in, 16)
            with sp.Fori(0, BLOCKS // 2) as pair:
                for e in range(2):
                    sp.wait_ge(S["table_ready"], pair * (2 * PB) + (e + 1) * PB + G)
                    sp.dma_start(A["gates"][pair * 2 + e], stage[e][:]).then_inc(stored[e], 16)
            sp.wait_ge(u_in, 16 * len(u))

        @block.gpsimd
        def _(pool):
            pool.tensor_copy(h[0][:], hT[:]).then_inc(h_split, 1)
            pool.wait_ge(h_split, 1)
            pool.tensor_tensor(h[1][:], hT[:], h[0][:], ALU.subtract).then_inc(h_split, 1)

        @block.vector
        def _(dve):
            def body(n, g, e, at, token, last):
                dve.wait_ge(S["hot_used"], n + 1)
                dve.tensor_tensor(first[g][:, 0:G - 1, :], C["iota"].unsqueeze(1).broadcast_to((P, G - 1, NKEYS)),
                                  sel[:, 0, bass.ds(token, G - 1)].unsqueeze(2).broadcast_to((P, G - 1, NKEYS)), ALU.is_equal
                                  ).then_inc(S["marked"], 1)
                col = bass.ds(token + (G - 1), 1)
                dve.tensor_scalar(first[g][:, G - 1, :], C["iota"], sel[:, 0, col], sel[:, 2, col], ALU.is_equal, ALU.mult)
                dve.tensor_tensor(second[g][:], C["iota"].unsqueeze(1).broadcast_to((P, G, NKEYS)),
                                  sel[:, 1, bass.ds(token, G)].unsqueeze(2).broadcast_to((P, G, NKEYS)), ALU.is_equal
                                  ).then_inc(S["hot_ready"], 1)

            loop(dve, body)

        @block.tensor
        def _(pe):
            pe.sem_inc(S["hot_used"], G)

            def body(n, g, e, at, token, last):
                pe.wait_ge(S["hot_ready"], n + 1)
                pe.wait_ge(S["weighed"], n + 1)
                pe.wait_ge(S["table_ready"], n + 1)
                for j in range(G):
                    mm = pe.matmul(PS[:, g, j * NKEYS:(j + 1) * NKEYS], second[g][:, j, :], first[g][:, j, :], start=True, stop=True)
                mm.then_inc(S["hot_used"], 1)

            loop(pe, body)

        @block.scalar
        def _(act):
            act.sem_inc(S["table_ready"], G)
            for e in range(2):
                act.sem_inc(stored[e], 16)

            def edge(pair, e):
                act.wait_ge(stored[e], pair * 16 + 16)

            def weigh(n, g, token):
                act.wait_ge(S["marked"], n + 1)
                for j in range(G - 1):
                    ins = act.activation(first[g][:, j, :], first[g][:, j, :], ACT.Copy, scale=sel[:, 2, bass.ds(token + j, 1)])
                ins.then_inc(S["weighed"], 1)

            def body(n, g, e, at, token, last):
                if not last:
                    weigh(n + 1, (g + 1) % G, token + G)
                act.wait_ge(S["hot_used"], n + G + 1)
                act.activation(stage[e][:, :, bass.ds(at, G)].rearrange("p i n -> p n i"), PS[:, g, :].rearrange("p (n i) -> p n i", n=G),
                               ACT.Copy).then_inc(S["table_ready"], 1)

            weigh(0, 0, 0)
            loop(act, body, edge)


def phase_experts(nc, A, env):
    sb, sem, PS, ident = (env[k] for k in ("sb", "sem", "PS", "ident"))
    x, h, u, gffn, stat = (env[k] for k in ("x", "h", "u", "gffn", "stat"))
    GC = 2
    NCH = NEXP // P
    NG = NCH // GC
    PAIR = 2 * GC
    NPAIR = NCH // PAIR
    BLK = N // TB
    UR = len(u)
    assert UR == PAIR
    uT = [[sb(f"uT_{'hl'[s]}{i}", (10, 122)[s] + 4 * i, [P, KD, P], F32R) for s in (HI, LO)] for i in range(2)]
    acc = sb("acc", 66, [P, NT, D])
    v = [[sb(f"v_{'hl'[s]}{i}", 130 + 16 * s + 8 * i, [P, GC, D], F32R) for s in (HI, LO)] for i in range(2)]
    a = [[sb(f"a_{'hl'[s]}{i}", 162 + 10 * s + 5 * i, [P, GC, N], F32R) for s in (HI, LO)] for i in range(2)]
    gt = [sb(f"gt{i}", 182 + 5 * i, [P, BLK, GC, TB]) for i in range(2)]
    gl = [sb(f"gl{i}", 192 + 2.5 * i, [P, 2, HALF]) for i in range(2)]
    vraw = [sb(f"vraw{i}", 197 + 4 * i, [P, D]) for i in range(2)]
    y = [sb(f"yo{i}", 106 + 4 * i, [P, D]) for i in range(2)]
    junk = sb("ej", 114, [P, D])
    names = ("uT_psum uT_hi uT_lo s_psum gelu weighed a_hi a_lo v_hi v_lo f_psum added f_sq f_var f_sqrt f_rstd scaled "
             "y_ready").split()
    S = {n: sem("ex_" + n) for n in names}
    u_in = [sem(f"ex_u_in{i}") for i in range(UR)]
    v_in, g_in = ([sem(f"ex_{n}_in{i}") for i in range(2)] for n in "vg")
    y_out = [sem(f"ex_y_out{i}") for i in range(2)]
    ADDS = 2 * NT
    y_dram = [A["y_p"][0, t * P:(t + 1) * P, :] for t in range(PT)] + [A["y_s"].rearrange("b q d -> (b q) d")]

    def pairs(eng, body):
        body(0, True, False)
        with eng.Fori(1, NPAIR - 1) as i:
            body(i, False, False)
        body(NPAIR - 1, False, True)

    with nc.Block() as block:
        @block.sync
        def _(sp):
            def body(i, first, last):
                for q in range(PAIR):
                    e, c = divmod(q, GC)
                    if not first:
                        sp.wait_ge(S["uT_psum"], i * (2 * PAIR) + 2 * (q + 1 - UR))
                        sp.dma_start(u[q][:], A["u_experts"][0, bass.ds(i * (PAIR * P) + q * P, P), :]).then_inc(u_in[q], 16)
                    if c == 0:
                        if first and e == 0:
                            for stored in env["gates_stored"]:
                                sp.wait_ge(stored, 16 * (BLK // 2 + 1))
                        if not first:
                            sp.wait_ge(S["weighed"], i * PAIR + (e - 1) * GC)
                        sp.dma_start(gt[e][:], A["gates"][:, :, bass.ds(i * PAIR + e * GC, GC), :].rearrange("b p c n -> p b c n")
                                     ).then_inc(g_in[e], 16)
                    if not (first and q < 2):
                        sp.wait_ge(S["v_lo"], i * PAIR + q - 1)
                    sp.dma_start(vraw[q % 2][:], A["v_experts"][0, bass.ds(i * (PAIR * P) + q * P, P), :]).then_inc(v_in[q % 2], 16)

            pairs(sp, body)
            for t in range(NT):
                sp.wait_ge(S["y_ready"], t + 1)
                sp.dma_start(y_dram[t], y[t % 2][:]).then_inc(y_out[t % 2], 16)
            sp.wait_ge(y_out[0], 16 * 3)
            sp.wait_ge(y_out[1], 16 * 2)

        @block.gpsimd
        def _(pool):
            def body(i, first, last):
                for q in range(PAIR):
                    e, c = divmod(q, GC)
                    pool.wait_ge(S["gelu"], i * PAIR + q + 1)
                    if c == 0:
                        pool.wait_ge(g_in[e], i * 16 + 16)
                    act_by_block = gl[q % 2][:].rearrange("p s n -> p (s n)").rearrange("p (b n) -> p b n", n=TB)
                    pool.tensor_tensor(act_by_block, act_by_block, gt[e][:, :, c, :], ALU.mult).then_inc(S["weighed"], 1)

            pairs(pool, body)

        @block.scalar
        def _(act):
            def turned(i, q):
                for b in range(2):
                    act.wait_ge(S["uT_psum"], i * (2 * PAIR) + 2 * q + b + 1)
                    act.activation(uT[q % 2][HI][:, 4 * b:4 * b + 4, :], PS[:, b, :].rearrange("p (k n) -> p k n", k=4), ACT.Copy
                                   ).then_inc(S["uT_hi"], 1)

            def body(i, first, last):
                if first:
                    turned(0, 0)
                for q in range(PAIR):
                    e, c = divmod(q, GC)
                    if not (last and q == PAIR - 1):
                        turned(i, q + 1)
                    act.wait_ge(v_in[q % 2], i * (16 * PAIR // 2) + 16 * (q // 2 + 1))
                    if c == 0 and not first:
                        act.wait_ge(S["f_psum"], i * (2 * ADDS) + (e - 1) * ADDS)
                    act.activation(v[e][HI][:, c, :], vraw[q % 2][:], ACT.Copy).then_inc(S["v_hi"], 1)
                    act.wait_ge(S["s_psum"], i * PAIR + q + 1)
                    if not (first and q < 2):
                        act.wait_ge(S["a_lo"], i * PAIR + q - 1)
                    act.activation(gl[q % 2][:], PS[:, 2 + 2 * (q % 2):4 + 2 * (q % 2), 0:HALF], ACT.Gelu).then_inc(S["gelu"], 1)
                    act.wait_ge(S["weighed"], i * PAIR + q + 1)
                    act.activation(a[e][HI][:, c, :], gl[q % 2][:].rearrange("p s n -> p (s n)"), ACT.Copy).then_inc(S["a_hi"], 1)

            pairs(act, body)
            for t in range(NT):
                act.wait_ge(S["added"], (NG - 1) * ADDS + 2 * (t + 1))
                if t:
                    act.wait_ge(S["f_sq"], t)
                act.activation(junk[:], acc[:, t, :], ACT.Square, accum_out=stat[:, 0, t:t + 1]).then_inc(S["f_sq"], 1)
                act.wait_ge(S["f_var"], t + 1)
                act.activation(stat[:, 0, t:t + 1], stat[:, 0, t:t + 1], ACT.Sqrt).then_inc(S["f_sqrt"], 1)

        @block.tensor
        def _(pe):
            def turn(i, q, first, first_of_all=False):
                if not (first and q < UR):
                    pe.wait_ge(u_in[q % UR], i * 16 + 16 * (q // UR))
                for b in range(2):
                    if not first_of_all:
                        pe.wait_ge(S["uT_lo"], i * (2 * PAIR) + 2 * q - 1 + b)
                    for j in range(4):
                        k = 4 * b + j
                        mm = pe.transpose(PS[:, b, j * P:(j + 1) * P], u[q % UR][:, k * P:(k + 1) * P], ident)
                    mm.then_inc(S["uT_psum"], 1)

            def hidden(i, q, fresh):
                if not fresh:
                    pe.wait_ge(S["gelu"], i * PAIR + q - 1)
                for b in range(2):
                    for k in range(KD):
                        if b == 0 and k % (KD // 2) == 0:
                            pe.wait_ge(S["uT_lo"], i * (2 * PAIR) + 2 * q + 1 + k // (KD // 2))
                        for w, m in PASSES:
                            mm = pe.matmul(PS[:, 2 + 2 * (q % 2) + b, 0:HALF], uT[q % 2][w][:, k, :], h[m][:, k, b * HALF:(b + 1) * HALF],
                                           start=k == 0 and (w, m) == PASSES[0], stop=k == KD - 1 and (w, m) == PASSES[-1])
                mm.then_inc(S["s_psum"], 1)

            def outputs(i, e, before, fresh):
                pe.wait_ge(S["v_lo"], i * PAIR + (e + 1) * GC)
                pe.wait_ge(S["a_lo"], i * PAIR + (e + 1) * GC)
                for n in range(ADDS):
                    t, b = divmod(n, 2)
                    if not (fresh and n < 2):
                        pe.wait_ge(S["added"], before + (n - 1))
                    for c in range(GC):
                        for w, m in PASSES:
                            mm = pe.matmul(PS[:, 6 + b, :], a[e][w][:, c, t * P:(t + 1) * P], v[e][m][:, c, b * 512:(b + 1) * 512],
                                           start=c == 0 and (w, m) == PASSES[0], stop=c == GC - 1 and (w, m) == PASSES[-1])
                    mm.then_inc(S["f_psum"], 1)

            def body(i, first, last):
                if first:
                    turn(0, 0, True, True)
                for q in range(PAIR):
                    if not (last and q == PAIR - 1):
                        turn(i, q + 1, first)
                    hidden(i, q, first and q < 2)
                    if q == GC - 1 and not first:
                        outputs(i - 1, 1, i * (2 * ADDS) - ADDS, False)
                    if q == PAIR - 1:
                        outputs(i, 0, i * (2 * ADDS), first)
                if last:
                    outputs(i, 1, i * (2 * ADDS) + ADDS, False)

            pairs(pe, body)

        @block.vector
        def _(dve):
            def turned(i, q):
                for b in range(2):
                    dve.wait_ge(S["uT_hi"], i * (2 * PAIR) + 2 * q + b + 1)
                    dve.tensor_tensor(uT[q % 2][LO][:, 4 * b:4 * b + 4, :], PS[:, b, :].rearrange("p (k n) -> p k n", k=4),
                                      uT[q % 2][HI][:, 4 * b:4 * b + 4, :], ALU.subtract).then_inc(S["uT_lo"], 1)

            def finish(t):
                dve.wait_ge(S["f_sq"], t + 1)
                dve.tensor_scalar(stat[:, 0, t:t + 1], stat[:, 0, t:t + 1], 1.0 / D, EPS, ALU.mult, ALU.add).then_inc(S["f_var"], 1)
                dve.wait_ge(S["f_sqrt"], t + 1)
                dve.reciprocal(stat[:, 1, t:t + 1], stat[:, 0, t:t + 1]).then_inc(S["f_rstd"], 1)
                dve.wait_ge(S["f_rstd"], t + 1)
                if t >= 2:
                    dve.wait_ge(y_out[t % 2], 16 * (t // 2))
                dve.scalar_tensor_tensor(out=y[t % 2][:], in0=acc[:, t, :], scalar=stat[:, 1, t:t + 1], in1=gffn[:, int(t >= PT), :],
                                         op0=ALU.mult, op1=ALU.mult).then_inc(S["scaled"], 1)
                dve.wait_ge(S["scaled"], t + 1)
                dve.tensor_tensor(y[t % 2][:], y[t % 2][:], x[:, t, :], ALU.add).then_inc(S["y_ready"], 1)

            def add(before, fresh=False, final=False):
                for n in range(ADDS):
                    t, b = divmod(n, 2)
                    dve.wait_ge(S["f_psum"], before + (n + 1))
                    dst = acc[:, t, b * 512:(b + 1) * 512]
                    if fresh:
                        dve.tensor_copy(dst, PS[:, 6 + b, :]).then_inc(S["added"], 1)
                    else:
                        dve.tensor_tensor(dst, PS[:, 6 + b, :], dst, ALU.add).then_inc(S["added"], 1)
                    if final and b and t:
                        finish(t - 1)
                if final:
                    finish(NT - 1)

            def body(i, first, last):
                if first:
                    turned(0, 0)
                for q in range(PAIR):
                    e, c = divmod(q, GC)
                    if not (last and q == PAIR - 1):
                        turned(i, q + 1)
                    dve.wait_ge(S["v_hi"], i * PAIR + q + 1)
                    dve.tensor_tensor(v[e][LO][:, c, :], vraw[q % 2][:], v[e][HI][:, c, :], ALU.subtract).then_inc(S["v_lo"], 1)
                    if q == GC - 1 and not first:
                        add(i * (2 * ADDS) - ADDS)
                    if q == PAIR - 1:
                        add(i * (2 * ADDS), first)
                    dve.wait_ge(S["a_hi"], i * PAIR + q + 1)
                    dve.tensor_tensor(a[e][LO][:, c, :], gl[q % 2][:].rearrange("p s n -> p (s n)"), a[e][HI][:, c, :], ALU.subtract
                                      ).then_inc(S["a_lo"], 1)
                if last:
                    add(i * (2 * ADDS) + ADDS, final=True)

            pairs(dve, body)


_INS = ["x_prompt", "x_sample", "c_prompt", "c_sample", "cache_sb_k", "cache_sb_v", "cache_mla_ckv", "cache_mla_krope",
        "w_ada", "b_ada", "g_mix_pre", "g_mix_post", "g_ffn_pre", "g_ffn_post", "w_in", "g_q_lat", "g_kv_lat", "w_uq",
        "w_uk", "w_uv", "g_sb_out", "g_mla_out", "w_out", "w_peer_q", "sub_keys_1", "sub_keys_2", "u_experts", "v_experts"]
_OUTS = [("y_p", (1, SEQ, D)), ("y_s", (NSEQ, STEP, D)),
         ("sbk_p", (1, 1, SEQ, H, HD)), ("sbv_p", (1, 1, SEQ, H, HD)), ("ckv_p", (1, 1, SEQ, KVR)), ("kr_p", (1, 1, SEQ, ROPE)),
         ("sbk_s", (1, NSEQ, STEP, H, HD)), ("sbv_s", (1, NSEQ, STEP, H, HD)), ("ckv_s", (1, NSEQ, STEP, KVR)),
         ("kr_s", (1, NSEQ, STEP, ROPE))]


def declare(nc, arrays):
    dram = {}
    for name in _INS + ["table"]:
        a = arrays[name]
        dram[name] = nc.dram_tensor(f"in_{name}", a.shape, mybir.dt.from_np(a.dtype), kind="ExternalInput").ap()
    for name, shape in _OUTS:
        dram[name] = nc.dram_tensor(f"out_{name}", shape, F32, kind="ExternalOutput").ap()
    dram["gates"] = nc.dram_tensor("gates", (N // TB, NKEYS, NKEYS, TB), F32).ap()
    return dram


def kernel(**inputs):
    import numpy as _np
    import concourse.bacc as _bacc
    from concourse.bass_utils import run_bass_kernel_spmd as _run

    nc = _bacc.Bacc("TRN2", target_bir_lowering=False, num_devices=1)
    arrays = {name: _np.ascontiguousarray(inputs[name]) for name in _INS}
    arrays["table"] = constant_table()
    build(nc, declare(nc, arrays))
    r = _run(nc, [{f"in_{k}": v for k, v in arrays.items()}], core_ids=[0])
    return tuple(r.results[0][f"out_{name}"] for name, _ in _OUTS)
```
